# Optimizing a Trainium2 kernel written in Bass

```python
import jax, jax.numpy as jnp
from jax import lax
import numpy as np

D_MODEL = 2048
BATCH = 1
SEQ = 256
DEPTH = 1
DEC_BATCH = 8
DEC_SEQ = 1
PAST_LEN = 2048
PAGE_SIZE = 128

A_HEADS = 12
A_HD = 64
A_W = A_HEADS * A_HD
BRANCHES = ((128, 1), (512, 4), (2048, 16))
MAX_WIN = max(w for w, _ in BRANCHES)
A_SCALE = A_HD ** -0.5
NUM_BUCKETS = 32
MAX_DISTANCE = MAX_WIN
POOL_WINDOWS = (2, 4, 8, 16)
POOL_G = len(POOL_WINDOWS)
POOL_W = D_MODEL - A_W
POOL_C = POOL_W // POOL_G
POOL_HIST = max(POOL_WINDOWS) - 1
IN_W = 3 * A_W + POOL_W
N_MEM = 256
X_HEADS = 4
X_HD = 128
X_W = X_HEADS * X_HD
X_SCALE = X_HD ** -0.5
N_GROUPS = 4
E_PER_GROUP = 8
N_EXPERTS = N_GROUPS * E_PER_GROUP
TOP_K = 2
D_EXPERT = 512
MOE_BLOCK = 128
EPS = 1e-6

kernel_name = "hymba_dilated_pool_hmoe_step"

def _rms(x, g):
    x32 = x.astype(jnp.float32)
    y = x32 * lax.rsqrt(jnp.mean(x32 * x32, axis=-1, keepdims=True) + EPS) * g.astype(jnp.float32)
    return y.astype(x.dtype)

def _t5_bucket(dist):
    n = np.asarray(dist, dtype=np.int64)
    exact = NUM_BUCKETS // 2
    ratio = np.log(np.maximum(n, 1) / exact) / np.log(MAX_DISTANCE / exact)
    large = np.minimum(exact + (ratio * (NUM_BUCKETS - exact)).astype(np.int64), NUM_BUCKETS - 1)
    return np.where(n < exact, n, large).astype(np.int32)

def _mix_in(x, norm_g, w_in, q_norm_g, k_norm_g):
    B, T, _ = x.shape
    z = _rms(x, norm_g) @ w_in
    q = _rms(z[..., :A_W].reshape(B, T, A_HEADS, A_HD), q_norm_g)
    k = _rms(z[..., A_W:2 * A_W].reshape(B, T, A_HEADS, A_HD), k_norm_g)
    v = z[..., 2 * A_W:3 * A_W].reshape(B, T, A_HEADS, A_HD)
    u = z[..., 3 * A_W:]
    return q, k, v, u

def _branch_prompt(q, k, v, w, d, rel_bias):
    B, Sp, H, E = q.shape
    nk = w // d
    n = Sp // d
    nb = n // nk

    def strided(t):
        return t.reshape(B, n, d, H, E).transpose(0, 2, 1, 3, 4).reshape(B, d, nb, nk, H, E)

    def band(t):
        prev = jnp.pad(t[:, :, :-1], ((0, 0), (0, 0), (1, 0), (0, 0), (0, 0), (0, 0)))
        return jnp.concatenate([prev, t], axis=3)

    qs, ks, vs = strided(q), strided(k), strided(v)
    rel = (np.arange(nk)[:, None] + nk) - np.arange(2 * nk)[None, :]
    ok = np.broadcast_to((rel >= 0) & (rel <= nk), (nb, nk, 2 * nk)).copy()
    ok[0] &= (np.arange(2 * nk)[None, :] >= nk)
    bias = rel_bias.astype(jnp.float32)[_t5_bucket(np.clip(rel, 0, None) * d)].transpose(2, 0, 1)
    s = jnp.einsum('brnqhe,brnkhe->brnhqk', qs, band(ks), preferred_element_type=jnp.float32)
    s = jnp.where(ok[None, None, :, None], s * A_SCALE + bias, -jnp.inf)
    m = jnp.max(s, axis=-1, keepdims=True)
    p = jnp.exp(s - m)
    l = jnp.sum(p, axis=-1, keepdims=True)
    o = jnp.einsum('brnhqk,brnkhe->brnqhe', p, band(vs).astype(jnp.float32)) / jnp.swapaxes(l, 3, 4)
    lse = jnp.swapaxes((m + jnp.log(l))[..., 0], 3, 4)
    o = o.reshape(B, d, n, H, E).transpose(0, 2, 1, 3, 4).reshape(B, Sp, H, E)
    lse = lse.reshape(B, d, n, H).transpose(0, 2, 1, 3).reshape(B, Sp, H)
    return o, lse

def _branch_step(q, kcat, vcat, w, d, wb, rel_bias):
    T = q.shape[1]
    steps = np.arange(w // d + 1)
    idx = wb + np.arange(T)[:, None] - steps[None, :] * d
    valid = idx >= 0
    idx = np.maximum(idx, 0)
    kg, vg = kcat[:, idx], vcat[:, idx]
    bias = rel_bias.astype(jnp.float32)[_t5_bucket(steps * d)].T
    s = jnp.einsum('bthe,btkhe->bthk', q, kg, preferred_element_type=jnp.float32)
    s = jnp.where(valid[None, :, None, :], s * A_SCALE + bias, -jnp.inf)
    m = jnp.max(s, axis=-1, keepdims=True)
    p = jnp.exp(s - m)
    l = jnp.sum(p, axis=-1, keepdims=True)
    o = jnp.einsum('bthk,btkhe->bthe', p, vg.astype(jnp.float32)) / l
    return o, (m + jnp.log(l))[..., 0]

def _merge_dilations(outs, lses):
    wts = jax.nn.softmax(jnp.stack(lses), axis=0)
    return jnp.sum(wts[..., None] * jnp.stack(outs), axis=0)

def _attn_prompt(q, k, v, rel_bias):
    S = q.shape[1]
    span = int(np.lcm.reduce([w for w, _ in BRANCHES]))
    Sp = -(-S // span) * span
    pad = ((0, 0), (0, Sp - S), (0, 0), (0, 0))
    qp, kp, vp = jnp.pad(q, pad), jnp.pad(k, pad), jnp.pad(v, pad)
    outs, lses = [], []
    for w, d in BRANCHES:
        o, l = _branch_prompt(qp, kp, vp, w, d, rel_bias)
        outs.append(o[:, :S])
        lses.append(l[:, :S])
    return _merge_dilations(outs, lses)

def _attn_step(q, k_new, v_new, cache_k, cache_v, rel_bias):
    wb = cache_k.shape[1]
    kcat = jnp.concatenate([cache_k, k_new], axis=1)
    vcat = jnp.concatenate([cache_v, v_new], axis=1)
    outs, lses = [], []
    for w, d in BRANCHES:
        o, l = _branch_step(q, kcat, vcat, w, d, wb, rel_bias)
        outs.append(o)
        lses.append(l)
    return _merge_dilations(outs, lses), kcat[:, -wb:], vcat[:, -wb:]

def _multi_pool(u_ext, n_prev, start_pos):
    B, L, _ = u_ext.shape
    T = L - n_prev
    u32 = u_ext.astype(jnp.float32)
    cs = jnp.concatenate([jnp.zeros((B, 1, POOL_W), jnp.float32), jnp.cumsum(u32, axis=1)], axis=1)
    i = np.arange(n_prev, L)
    means = []
    for g, w in enumerate(POOL_WINDOWS):
        csg = cs[..., g * POOL_C:(g + 1) * POOL_C]
        lo = np.maximum(i + 1 - w, 0)
        cnt = np.minimum(w, start_pos + np.arange(T) + 1).astype(np.float32)
        means.append((csg[:, i + 1] - csg[:, lo]) / cnt[None, :, None])
    return jnp.stack(means, axis=2) - u32[:, n_prev:].reshape(B, T, POOL_G, POOL_C)

def _mix_out(attn, pooled, pool_w, pool_scale, w_out, dtype):
    B, T = attn.shape[:2]
    pb = jnp.einsum('btgc,gcd->btgd', pooled, pool_w.astype(jnp.float32))
    pb = pb * pool_scale.astype(jnp.float32).reshape(POOL_G, POOL_C)
    mix = jnp.concatenate([attn.reshape(B, T, A_W), pb.reshape(B, T, POOL_W)], axis=-1)
    return mix.astype(dtype) @ w_out

def _mem_kv(mem, norm_mem_g, w_ck, w_cv, ck_norm_g):
    B, M, _ = mem.shape
    hm = _rms(mem, norm_mem_g)
    k = _rms((hm @ w_ck).reshape(B, M, X_HEADS, X_HD), ck_norm_g)
    v = (hm @ w_cv).reshape(B, M, X_HEADS, X_HD)
    return k, v

def _cross(x, mem_k, mem_v, norm_g, w_cq, cq_norm_g, w_co):
    B, T, _ = x.shape
    q = _rms((_rms(x, norm_g) @ w_cq).reshape(B, T, X_HEADS, X_HD), cq_norm_g)
    s = jnp.einsum('bthe,bmhe->bhtm', q, mem_k, preferred_element_type=jnp.float32) * X_SCALE
    p = jax.nn.softmax(s, axis=-1)
    o = jnp.einsum('bhtm,bmhe->bthe', p, mem_v.astype(jnp.float32))
    return o.reshape(B, T, X_W).astype(x.dtype) @ w_co

def _route(h, w_rg, b_rg, w_re, b_re):
    N = h.shape[0]
    lg = (h @ w_rg).astype(jnp.float32) + b_rg.astype(jnp.float32)
    g_sel = lax.top_k(lg, 1)[1][:, 0]
    p_grp = jnp.take_along_axis(jax.nn.softmax(lg, axis=-1), g_sel[:, None], axis=1)[:, 0]
    le = ((h @ w_re).astype(jnp.float32) + b_re.astype(jnp.float32)).reshape(N, N_GROUPS, E_PER_GROUP)
    le = jnp.take_along_axis(le, g_sel[:, None, None], axis=1)[:, 0]
    top_v, top_i = lax.top_k(le, TOP_K)
    gates = jax.nn.softmax(top_v, axis=-1) * p_grp[:, None]
    return g_sel[:, None] * E_PER_GROUP + top_i, gates

def _moe(x, norm_g, w_rg, b_rg, w_re, b_re, w_e_gate, w_e_up, w_e_down):
    B, T, D = x.shape
    N = B * T
    h = _rms(x, norm_g).reshape(N, D)
    experts, gates = _route(h, w_rg, b_rg, w_re, b_re)
    A = N * TOP_K
    blk = MOE_BLOCK
    while blk > 8 and blk * N_EXPERTS > 2 * A:
        blk //= 2
    n_blocks = -(-(A + N_EXPERTS * (blk - 1)) // blk)
    total = n_blocks * blk
    flat_e = experts.reshape(-1)
    flat_t = jnp.repeat(jnp.arange(N, dtype=jnp.int32), TOP_K)
    flat_g = gates.reshape(-1)
    order = jnp.argsort(flat_e)
    se, st, sg = flat_e[order], flat_t[order], flat_g[order]
    counts = jnp.zeros((N_EXPERTS,), jnp.int32).at[flat_e].add(1)
    padded = (counts + blk - 1) // blk * blk
    pend = jnp.cumsum(padded)
    pstart = pend - padded
    cstart = jnp.cumsum(counts) - counts
    dest = pstart[se] + (jnp.arange(A, dtype=jnp.int32) - cstart[se])
    buf_t = jnp.zeros((total,), jnp.int32).at[dest].set(st)
    buf_g = jnp.zeros((total,), jnp.float32).at[dest].set(sg)
    blk_e = jnp.minimum(jnp.searchsorted(pend, jnp.arange(n_blocks) * blk, side='right'), N_EXPERTS - 1)
    xb = h[buf_t].reshape(n_blocks, blk, D)

    def expert_block(args):
        xe, e = args
        a = jax.nn.silu((xe @ w_e_gate[e]).astype(jnp.float32))
        b = (xe @ w_e_up[e]).astype(jnp.float32)
        return ((a * b).astype(xe.dtype) @ w_e_down[e]).astype(jnp.float32)

    yb = lax.map(expert_block, (xb, blk_e)).reshape(total, D)
    y = jnp.zeros((N, D), jnp.float32).at[buf_t].add(yb * buf_g[:, None])
    return y.astype(x.dtype).reshape(B, T, D)

def setup_inputs(seed: int = 0) -> dict:
    key = jax.random.key(seed)
    ks = jax.random.split(key, 40)
    f32 = jnp.float32

    def nrm(k, shape, scale=1.0):
        return jax.random.normal(k, shape, f32) * scale

    def gain(k, shape):
        return 1.0 + 0.02 * jax.random.normal(k, shape, f32)

    wb = min(MAX_WIN, PAST_LEN)
    L = DEPTH
    return {
        "x_prompt": nrm(ks[0], (BATCH, SEQ, D_MODEL)),
        "x_sample": nrm(ks[1], (DEC_BATCH, DEC_SEQ, D_MODEL)),
        "cache_win_k": nrm(ks[2], (L, DEC_BATCH, wb, A_HEADS, A_HD)),
        "cache_win_v": nrm(ks[3], (L, DEC_BATCH, wb, A_HEADS, A_HD)),
        "state_pool": nrm(ks[4], (L, DEC_BATCH, POOL_HIST, POOL_W)),
        "cache_mem_k": nrm(ks[5], (L, DEC_BATCH, N_MEM, X_HEADS, X_HD)),
        "cache_mem_v": nrm(ks[6], (L, DEC_BATCH, N_MEM, X_HEADS, X_HD)),
        "mem_prompt": nrm(ks[7], (BATCH, N_MEM, D_MODEL)),
        "rel_bias": nrm(ks[8], (NUM_BUCKETS, A_HEADS), 0.5),
        "norm_mix_g": gain(ks[9], (L, D_MODEL)),
        "w_in": nrm(ks[10], (L, D_MODEL, IN_W), D_MODEL ** -0.5),
        "q_norm_g": gain(ks[11], (L, A_HD)),
        "k_norm_g": gain(ks[12], (L, A_HD)),
        "pool_w": nrm(ks[13], (L, POOL_G, POOL_C, POOL_C), POOL_C ** -0.5),
        "pool_scale": gain(ks[14], (L, POOL_W)),
        "w_out": nrm(ks[15], (L, A_W + POOL_W, D_MODEL), (A_W + POOL_W) ** -0.5),
        "norm_cross_g": gain(ks[16], (L, D_MODEL)),
        "norm_mem_g": gain(ks[17], (L, D_MODEL)),
        "w_cq": nrm(ks[18], (L, D_MODEL, X_W), D_MODEL ** -0.5),
        "w_ck": nrm(ks[19], (L, D_MODEL, X_W), D_MODEL ** -0.5),
        "w_cv": nrm(ks[20], (L, D_MODEL, X_W), D_MODEL ** -0.5),
        "cq_norm_g": gain(ks[21], (L, X_HD)),
        "ck_norm_g": gain(ks[22], (L, X_HD)),
        "w_co": nrm(ks[23], (L, X_W, D_MODEL), X_W ** -0.5),
        "norm_ffn_g": gain(ks[24], (L, D_MODEL)),
        "w_rg": nrm(ks[25], (L, D_MODEL, N_GROUPS), D_MODEL ** -0.5),
        "b_rg": nrm(ks[26], (L, N_GROUPS), 0.01),
        "w_re": nrm(ks[27], (L, D_MODEL, N_EXPERTS), D_MODEL ** -0.5),
        "b_re": nrm(ks[28], (L, N_EXPERTS), 0.01),
        "w_e_gate": nrm(ks[29], (L, N_EXPERTS, D_MODEL, D_EXPERT), D_MODEL ** -0.5),
        "w_e_up": nrm(ks[30], (L, N_EXPERTS, D_MODEL, D_EXPERT), D_MODEL ** -0.5),
        "w_e_down": nrm(ks[31], (L, N_EXPERTS, D_EXPERT, D_MODEL), D_EXPERT ** -0.5),
    }

def reference(x_prompt, x_sample, cache_win_k, cache_win_v, state_pool, cache_mem_k, cache_mem_v,
              mem_prompt, rel_bias, norm_mix_g, w_in, q_norm_g, k_norm_g, pool_w, pool_scale, w_out,
              norm_cross_g, norm_mem_g, w_cq, w_ck, w_cv, cq_norm_g, ck_norm_g, w_co,
              norm_ffn_g, w_rg, b_rg, w_re, b_re, w_e_gate, w_e_up, w_e_down):
    xp, xs = x_prompt, x_sample
    wkp, wvp, wks, wvs, plp, pls, mkp_l, mvp_l = [], [], [], [], [], [], [], []
    for l in range(DEPTH):
        qp, kp, vp, up = _mix_in(xp, norm_mix_g[l], w_in[l], q_norm_g[l], k_norm_g[l])
        qs, ksn, vsn, us = _mix_in(xs, norm_mix_g[l], w_in[l], q_norm_g[l], k_norm_g[l])
        ap = _attn_prompt(qp, kp, vp, rel_bias)
        asmp, new_k, new_v = _attn_step(qs, ksn, vsn, cache_win_k[l], cache_win_v[l], rel_bias)
        wbp = min(MAX_WIN, xp.shape[1])
        wkp.append(kp[:, -wbp:])
        wvp.append(vp[:, -wbp:])
        wks.append(new_k)
        wvs.append(new_v)
        pp = _multi_pool(up, 0, 0)
        u_ext = jnp.concatenate([state_pool[l], us], axis=1)
        ps = _multi_pool(u_ext, state_pool.shape[2], PAST_LEN)
        plp.append(up[:, -POOL_HIST:])
        pls.append(u_ext[:, -POOL_HIST:])
        xp = xp + _mix_out(ap, pp, pool_w[l], pool_scale[l], w_out[l], xp.dtype)
        xs = xs + _mix_out(asmp, ps, pool_w[l], pool_scale[l], w_out[l], xs.dtype)
        mk, mv = _mem_kv(mem_prompt, norm_mem_g[l], w_ck[l], w_cv[l], ck_norm_g[l])
        mkp_l.append(mk)
        mvp_l.append(mv)
        xp = xp + _cross(xp, mk, mv, norm_cross_g[l], w_cq[l], cq_norm_g[l], w_co[l])
        xs = xs + _cross(xs, cache_mem_k[l], cache_mem_v[l], norm_cross_g[l], w_cq[l], cq_norm_g[l], w_co[l])
        xp = xp + _moe(xp, norm_ffn_g[l], w_rg[l], b_rg[l], w_re[l], b_re[l], w_e_gate[l], w_e_up[l], w_e_down[l])
        xs = xs + _moe(xs, norm_ffn_g[l], w_rg[l], b_rg[l], w_re[l], b_re[l], w_e_gate[l], w_e_up[l], w_e_down[l])
    return (xp, xs, jnp.stack(wkp), jnp.stack(wvp), jnp.stack(wks), jnp.stack(wvs),
            jnp.stack(plp), jnp.stack(pls), jnp.stack(mkp_l), jnp.stack(mvp_l))


_drawn_inputs = setup_inputs


def setup_inputs(seed=0):
    import zlib

    import numpy as np

    out = dict(_drawn_inputs(seed))
    spreads = {}
    factors = {'q_norm_g': 6.463,
     'k_norm_g': 3.119,
     'norm_cross_g': 8.0,
     'norm_mem_g': 2.807,
     'cq_norm_g': 5.588,
     'ck_norm_g': 3.304,
     'b_rg': 49.553,
     'b_re': 19.52,
     'norm_ffn_g': 4.802}
    for name, (base, spread) in spreads.items():
        noise = np.random.default_rng([zlib.crc32(name.encode()), seed]).standard_normal(out[name].shape)
        drawn = base * np.exp(spread * noise) if base else spread * noise
        out[name] = __import__('jax').numpy.asarray(drawn.astype(out[name].dtype))
    for name, factor in factors.items():
        out[name] = (out[name] * factor).astype(out[name].dtype)
    return out
```

```python
from contextlib import ExitStack
import math

import numpy as np
import concourse.bass as bass
from concourse import mybir

F32 = mybir.dt.float32
I32 = mybir.dt.int32
U32 = mybir.dt.uint32
ALU = mybir.AluOpType
ACT = mybir.ActivationFunctionType
AX = mybir.AxisListType

P = 128
D = 2048
KT = D // P
SEQ = 256
PT = SEQ // P
NB = 8
TOK = SEQ + NB
TC = SEQ + 32
H, HD = 12, 64
AW = H * HD
POOL_WINDOWS = (2, 4, 8, 16)
PG, PC = 4, 320
PW = PG * PC
HIST = 15
IN_W = 3 * AW + PW
NCH = IN_W // 512
WB = 2048
NM = 256
XH, XD = 4, 128
XW = XH * XD
NG, EG = 4, 8
NE = NG * EG
DE = 512
EPS = 1e-6
NEG = -1e30
BLK = 32
OVB = 2 * TOK // BLK
NBLK = NE + OVB
NBUCKET, MAXD = 32, 2048
BRANCHES = ((128, 1), (512, 4), (2048, 16))


def bucket(dist):
    n = np.asarray(dist, dtype=np.int64)
    exact = NBUCKET // 2
    ratio = np.log(np.maximum(n, 1) / exact) / np.log(MAXD / exact)
    large = np.minimum(exact + (ratio * (NBUCKET - exact)).astype(np.int64), NBUCKET - 1)
    return np.where(n < exact, n, large)


def bias_columns(dist):
    dist = np.asarray(dist)
    out = np.zeros((NBUCKET + 1, len(dist)), np.float32)
    for c, d in enumerate(dist):
        mult = sum(1 for w, s in BRANCHES if 0 <= d <= w and d % s == 0)
        if mult:
            out[bucket(d), c] = 1.0
            out[NBUCKET, c] = math.log(mult)
        else:
            out[NBUCKET, c] = NEG
    return out


DEC_ROWS = (P, 97, 96)
DEC_OFF = (0, P, P + 97)
NDEC = sum(DEC_ROWS)
DEC_DIST = ([P - r for r in range(P)] + [512 - 4 * r for r in range(96)] + [0] + [2048 - 16 * r for r in range(96)])

CONST_W = dict(ident=P, tri=P, moe=NE + NE + 3 + OVB, pool=PG * 256 + PG * P, pools=2 * PG * NB,
               flip=P, mask=AW, xmask=XW, sel=4, ohp=384, ohs=NDEC)
CONST_AT = {}
_at = 0
for _k, _w in CONST_W.items():
    CONST_AT[_k] = (_at, _at + _w)
    _at += _w
CONST_N = _at


def constants():
    c = np.zeros((P, CONST_N), np.float32)

    def part(name):
        a, b = CONST_AT[name]
        return c[:, a:b]

    part("ident")[:] = np.eye(P)
    part("flip")[:] = np.eye(P)[::-1]
    part("tri")[:] = np.triu(np.ones((P, P)), 1)
    m = part("moe")
    m[:, 0:NE] = NE - np.arange(NE)
    m[:, NE:2 * NE] = BLK * np.arange(NE)
    m[:, 2 * NE:2 * NE + 3] = 1.0
    m[NB:, 2 * NE + 2] = 0.0
    m[:, 2 * NE + 3:] = np.arange(OVB)
    full = np.zeros((PG, SEQ, SEQ), np.float32)
    for g, w in enumerate(POOL_WINDOWS):
        for t in range(SEQ):
            lo = max(t + 1 - w, 0)
            full[g, lo:t + 1, t] = 1.0 / min(w, t + 1)
            full[g, t, t] -= 1.0
    pool = part("pool")
    pool[:, 0:PG * 256] = full[:, 0:P].transpose(1, 0, 2).reshape(P, -1)
    pool[:, PG * 256:] = full[:, P:, P:].transpose(1, 0, 2).reshape(P, -1)
    ps = part("pools").reshape(P, 2, PG, NB)
    for g, w in enumerate(POOL_WINDOWS):
        for b in range(NB):
            ps[b * HIST + HIST - (w - 1):b * HIST + HIST, 0, g, b] = 1.0 / w
            ps[b, 1, g, b] = 1.0 / w - 1.0
    for i in range(4):
        for h in range(H):
            part("mask")[32 * i + h, h * HD:(h + 1) * HD] = 1.0
        for h in range(XH):
            part("xmask")[32 * i + h, h * XD:(h + 1) * XD] = 1.0
        part("sel")[32 * i:32 * i + 32, i] = 1.0
    part("ohp")[0:NBUCKET + 1] = bias_columns([255 - v for v in range(384)])
    part("ohs")[0:NBUCKET + 1] = bias_columns(DEC_DIST)
    return c


def hybrid_decoder_layer(nc, a):
    with ExitStack() as ctx:
        def sem(name):
            return ctx.enter_context(nc.semaphore(name))

        def sb(name, shape, dt=F32):
            return ctx.enter_context(nc.sbuf_tensor(name, shape, dt))

        bias_dram = nc.dram_tensor("bias_rows", (H, 384), F32, kind="Internal").ap()
        xs_dram = nc.dram_tensor("moe_in", (NBLK * BLK, D), F32, kind="Internal").ap()
        ys_dram = nc.dram_tensor("moe_out", (NBLK * BLK, D), F32, kind="Internal").ap()

        ring = sb("ring", [P, 3, 8192])
        x3 = sb("x3", [P, 3, D])
        hT = sb("hT", [P, KT, TC])
        z = sb("z", [P, 3, IN_W])
        mkT = sb("mkT", [P, XH, NM])
        qkT = sb("qkT", [P, 2, H // 2, SEQ])
        ident = sb("ident", [P, P])
        tri = sb("tri", [P, P])
        dg = sb("dg", [P, 3, P])
        s_in = sb("s_in", [P, 3, 2, P])
        psm = sb("psm", [P, 2, NDEC])
        moec = sb("moec", [P, 2 * NE + 3 + OVB])
        poolsc = sb("poolsc", [P, 2, PG, NB])
        sel = sb("sel", [P, 4])
        gT = sb("gT", [P, 4, KT])
        gqk = sb("gqk", [P, 2, HD])
        gxx = sb("gxx", [P, 2, XD])
        psc = sb("psc", [P, PW // P])
        st = sb("st", [P, 152])
        slot_i = sb("slot_i", [P, 2, 3], U32)
        gates = sb("gates", [P, 2, 3])
        ov_i = sb("ov_i", [1, OVB + 1], I32)

        slot2 = ring[:, 2, :]
        mixT = slot2[:, 0:KT * TC].rearrange("p (k t) -> p k t", k=KT)
        zero_rows = slot2[:, 0:D]
        AFTER_MIX = KT * TC
        bias = slot2[:, AFTER_MIX:AFTER_MIX + H * SEQ].rearrange("p (h j) -> p h j", h=H)
        bias_flat = after_mix = slot2[:, AFTER_MIX:AFTER_MIX + H * SEQ]
        biasS = slot2[:, AFTER_MIX + H * SEQ:AFTER_MIX + H * SEQ + NDEC]
        qkt_flat = qkT[:].rearrange("p a h t -> p (a h t)")
        rb = psm[:, 0, 0:H]
        rbs = psm[:, 0, 16:144].rearrange("p (i h) -> p i h", i=4)
        flip = slot2[:, 8192 - P:8192]
        hankel = qkt_flat
        ohp = qkt_flat[:, 0:384]
        ohs = qkt_flat[:, 384:384 + NDEC]
        brow = qkt_flat[:, 768:768 + 384]
        sq = qkt_flat[:, 1536:1536 + 2 * AW]
        zf = z[:].rearrange("p t n -> p (t n)")
        POOLW, WOUT = NCH, NCH + 1
        CK, CV, CQ, CO = WOUT + 4, WOUT + 5, WOUT + 6, WOUT + 7
        pslot = ring[:, POOLW % 2, :]
        pw = pslot[:, 0:10 * PC].rearrange("p (c d) -> p c d", c=10)
        poolT = pslot[:, 3200:3200 + 10 * TOK].rearrange("p (c t) -> p c t", c=10)
        state = pslot[:, 5840:5840 + PW]
        poolc = z[:, 0, 0:2 * AW]
        poolA = poolc[:, 0:1024].rearrange("p (g t) -> p g t", g=PG)
        poolB = poolc[:, 1024:1536].rearrange("p (g t) -> p g t", g=PG)
        prb = z[:, 1, 0:768].rearrange("p (b j) -> p b j", b=2)
        prT = z[:, 1, 768:1536].rearrange("p (b j) -> p b j", b=2)
        kvb = hT[:].rearrange("p k t -> p (k t)").rearrange("p (b t n) -> p b t n", b=2, t=3)
        mask = after_mix[:, 0:AW]
        masked = after_mix[:, AW:2 * AW]
        memr = zf[:, 0:2 * D].rearrange("p (t n) -> p t n", t=2)
        hmT = zf[:, 2 * D:4 * D].rearrange("p (k t) -> p k t", k=KT)
        mk = zf[:, 4 * D:4 * D + 1024].rearrange("p (t n) -> p t n", t=2)
        mv = zf[:, 4 * D + 1024:4 * D + 2048].rearrange("p (t n) -> p t n", t=2)
        mem_dump = zf[:, 4 * D:5 * D]
        xq = zf[:, 0:3 * XW].rearrange("p (t n) -> p t n", t=3)
        xqT = zf[:, 1536:1536 + XH * SEQ].rearrange("p (h t) -> p h t", h=XH)
        xsq = zf[:, 2560:2560 + XW]
        oT = slot2[:, 0:XH * TC].rearrange("p (h t) -> p h t", h=XH)
        xprb = slot2[:, 1152:2176].rearrange("p (b j) -> p b j", b=2)
        xprT = slot2[:, 2176:3200].rearrange("p (b j) -> p b j", b=2)
        xkv = after_mix[:, 0:2048].rearrange("p (b t n) -> p b t n", b=2, t=2)
        xmask = after_mix[:, 2048:2560]
        xmasked = after_mix[:, 2560:3072]
        xn = zf[:, 0:3 * D].rearrange("p (t n) -> p t n", t=3)
        M0 = 3 * D
        ffn_dump = zf[:, M0 + 900:M0 + 900 + D]
        wr = zf[:, M0:M0 + KT * 36].rearrange("p (k n) -> p k n", k=KT)
        b36 = zf[0:36, M0 + 576:M0 + 577]
        LT = zf[0:36, M0 + 580:M0 + 580 + TOK]
        rt = zf[:, M0 + 900:M0 + 900 + 1600]
        xe = zf[:, M0 + 2560:M0 + 3072]
        XT = zf[:, M0 + 3072:M0 + 3584].rearrange("p (j s) -> p j s", j=4)
        ge, gd, gr, hid, aT = (zf[:, M0 + 3584 + 128 * i:M0 + 3712 + 128 * i] for i in range(5))
        yo = rt[:, 0:512]
        ones = ge

        pb = [ctx.enter_context(nc.psum_tensor(f"pb{i}", [P, 512], F32)) for i in range(8)]
        VB, AB = pb[0:4], pb[4:8]

        const_landed, x_landed = sem("const_landed"), sem("x_landed")
        w_landed = [sem("w_landed0"), sem("w_landed1")]
        v_filled, v_freed = sem("v_filled"), sem("v_freed")
        a_filled, a_freed = sem("a_filled"), sem("a_freed")
        dve_seq = sem("dve_seq")
        squared, mean_ready, root_ready, diag_ready = sem("squared"), sem("mean_ready"), sem("root_ready"), sem("diag_ready")
        zeros_ready, pads_ready = sem("zeros_ready"), sem("pads_ready")
        xs_zeroed = sem("xs_zeroed")
        brow_stored, bias_landed = sem("brow_stored"), sem("bias_landed")
        qk_normed, mk_normed, xq_normed = sem("qk_normed"), sem("mk_normed"), sem("xq_normed")
        rows_stored, stored = sem("rows_stored"), sem("stored")
        copied = sem("copied")
        biased, exped, probs_ready = sem("biased"), sem("exped"), sem("probs_ready")
        poolc_landed, state_landed = sem("poolc_landed"), sem("state_landed")
        kv_landed = [sem("kv_landed0"), sem("kv_landed1")]
        keys_used, vals_used = sem("keys_used"), sem("vals_used")
        s_biased, s_exped, s_probs = sem("s_biased"), sem("s_exped"), sem("s_probs")
        mask_landed = sem("mask_landed")
        mem_landed, mem_stored = sem("mem_landed"), sem("mem_stored")
        router_landed = sem("router_landed")
        xn_ready, exp_in, exp_out = sem("xn_ready"), sem("exp_in"), sem("exp_out")
        pairs_ready, over_cols_ready = sem("pairs_ready"), sem("over_cols_ready")
        slots_ready, scattered = sem("slots_ready"), sem("scattered")
        xe_landed = sem("xe_landed")
        gu_landed, gu_used = [sem("gu_landed0"), sem("gu_landed1")], [sem("gu_used0"), sem("gu_used1")]
        dn_landed, dn_used = sem("dn_landed"), sem("dn_used")
        xt_filled, xt_ready = sem("xt_filled"), sem("xt_ready")
        gate_exp, hid_seq, hid_ready = sem("gate_exp"), sem("hid_seq"), sem("hid_ready")
        hidT_filled, hidT_ready = sem("hidT_filled"), sem("hidT_ready")
        y_ready, y_stored = sem("y_ready"), sem("y_stored")
        y_gathered = [sem(f"y_gathered{i}") for i in range(6)]
        x_final = sem("x_final")

        cdr = a["const"]

        def cc(name, p=P):
            lo, hi = CONST_AT[name]
            return cdr[0:p, lo:hi]

        def wk(i):
            return ring[:, i % 2, :].rearrange("p (k n) -> p k n", k=KT)

        def piece_landed(eng, i):
            n = i // 2 + 1
            if i % 2 == POOLW % 2 and i >= POOLW:
                n += POOL_DMAS - 1
            eng.wait_ge(w_landed[i % 2], 16 * n)

        POOL_DMAS = 4
        FLIPS = H * SEQ // 512
        A_QKT = 2 * NCH + 6
        A_ATT = A_QKT + 2 * H
        A_DEC = A_ATT + 20 + 4
        A_MV = A_DEC + 2
        A_XQT = A_MV + 2 + 2 + 2
        V_IN = 2 + 12 + NCH + FLIPS
        V_WOUT = V_IN + H + 2 * NB + 2 + 4 + 12
        V_MK = V_WOUT + 8 + 1
        V_CQ = V_MK + 1 + 12 + 1
        V_CO = V_CQ + XH + NB + 2 + 2 + 12
        N_CONST = 22

        def piece_used(eng, i):
            if i < NCH:
                eng.wait_ge(v_filled, 2 + 12 + i + 1 + (FLIPS if i > 1 else 0))
            elif i == POOLW:
                eng.wait_ge(a_filled, A_ATT + 20)
            elif i < CK:
                eng.wait_ge(v_filled, V_WOUT - 12 + 3 * (i - WOUT + 1))
            else:
                eng.wait_ge(v_filled, {CK: V_MK, CV: V_MK + 1, CQ: V_CQ, CO: V_CO}[i])

        def turn_job(h):
            return 0 if h == 0 else 2 * h - 1

        block = ctx.enter_context(nc.Block())

        @block.sync
        def _(sp):
            def big(i):
                if i >= 2:
                    piece_used(sp, i - 2)
                done = w_landed[i % 2]
                if i < NCH:
                    src = a["w_in"][0][:, 512 * i:512 * i + 512].rearrange("(p k) n -> p k n", k=KT)
                elif i == POOLW:
                    g2 = a["pool_w"][0]
                    for c in range(2):
                        sp.dma_start(pw[:, 0:8, :].rearrange("p (g c) d -> p g c d", c=2)[:, :, c],
                                     g2[:, c * P:c * P + P, :].rearrange("g p d -> p g d")).then_inc(done, 16)
                    for o in range(2):
                        sp.dma_start(pw[64 * o:64 * o + 64, 8:10, :],
                                     g2[o:PG:2, 2 * P:PC, :].rearrange("g p d -> p g d")).then_inc(done, 16)
                    return
                elif i < WOUT + 4:
                    n = i - WOUT
                    src = a["w_out"][0][:, 512 * n:512 * n + 512].rearrange("(k p) n -> p k n", p=P)
                elif i < CO:
                    w = {CK: "w_ck", CV: "w_cv", CQ: "w_cq"}[i]
                    src = a[w][0].rearrange("(p k) n -> p k n", k=KT)
                else:
                    src = a["w_co"][0].rearrange("(k p) n -> p k n", p=P)
                    sp.dma_start(ring[:, i % 2, :].rearrange("p (k n) -> p k n", k=XH), src).then_inc(done, 16)
                    return
                sp.dma_start(wk(i), src).then_inc(done, 16)

            sp.dma_start(x3[:, 0:2, :], a["x_prompt"][0].rearrange("(t p) n -> p t n", p=P)).then_inc(x_landed, 16)
            sp.wait_ge(zeros_ready, 1)
            sp.dma_start(x3[0:NB, 2, :], a["x_sample"][:, 0]).then_inc(x_landed, 16)
            for dst, src in ((ident[:], cc("ident")), (rb[0:NBUCKET], a["rel_bias"]),
                             (ohp[0:33], cc("ohp", 33)), (ohs[0:33], cc("ohs", 33)),
                             (tri[:], cc("tri")), (flip, cc("flip")), (moec[:], cc("moe")),
                             (poolsc[:].rearrange("p a g b -> p (a g b)"), cc("pools")), (sel[:], cc("sel"))):
                sp.dma_start(dst, src).then_inc(const_landed, 16)
            for i in range(4):
                sp.dma_start(rbs[0:NBUCKET, i, 0:H], a["rel_bias"]).then_inc(const_landed, 16)
            big(0)
            for i, g in enumerate(("norm_mix_g", "norm_mem_g", "norm_cross_g", "norm_ffn_g")):
                sp.dma_start(gT[:, i, :], a[g][0].rearrange("(p k) -> p k", k=KT)).then_inc(const_landed, 16)
            for i, g in enumerate(("q_norm_g", "k_norm_g")):
                sp.dma_start(gqk[:, i, :], a[g].to_broadcast([P, HD])).then_inc(const_landed, 16)
            for i, g in enumerate(("cq_norm_g", "ck_norm_g")):
                sp.dma_start(gxx[:, i, :], a[g].to_broadcast([P, XD])).then_inc(const_landed, 16)
            with nc.allow_non_contiguous_dma(reason="1280 scale values, one per partition"):
                sp.dma_start(psc[:], a["pool_scale"][0].rearrange("(k p) -> p k", p=P)).then_inc(const_landed, 16)
            big(1)
            sp.wait_ge(v_freed, 2)
            sp.dma_start(bias_dram[:, :], brow[0:H, :]).then_inc(brow_stored, 16)
            sp.wait_ge(brow_stored, 16)
            sp.dma_start(hankel.rearrange("p (h j) -> p h j", h=H),
                         bass.AP(tensor=bias_dram.tensor, offset=0, ap=[[1, P], [384, H], [1, SEQ]]))\
                .then_inc(bias_landed, 16)
            for i in range(2, NCH + 1):
                big(i)
            piece_used(sp, POOLW - 2)
            sp.dma_start(state[0:NB * HIST, :], a["state_pool"][0].rearrange("b s n -> (b s) n")).then_inc(state_landed, 16)
            sp.wait_ge(qk_normed, 3)
            sp.wait_ge(a_freed, 2 * NCH)
            sp.wait_ge(v_freed, V_IN)
            for dst, src in ((a["win_k_prompt"][0, 0].rearrange("(t p) h e -> p t (h e)", p=P), z[:, 0:2, AW:2 * AW]),
                             (a["win_v_prompt"][0, 0].rearrange("(t p) h e -> p t (h e)", p=P), z[:, 0:2, 2 * AW:3 * AW]),
                             (a["win_k_sample"][0, :, WB - 1].rearrange("b h e -> b (h e)"), z[0:NB, 2, AW:2 * AW]),
                             (a["win_v_sample"][0, :, WB - 1].rearrange("b h e -> b (h e)"), z[0:NB, 2, 2 * AW:3 * AW]),
                             (a["pool_prompt"][0, 0], z[P - HIST:P, 1, 3 * AW:IN_W]),
                             (a["pool_sample"][0, :, HIST - 1], z[0:NB, 2, 3 * AW:IN_W])):
                sp.dma_start(dst, src).then_inc(rows_stored, 16)
            sp.wait_ge(rows_stored, 6 * 16)
            sp.wait_ge(a_freed, A_QKT)
            sp.dma_start(poolc, cc("pool")).then_inc(poolc_landed, 16)
            for i in range(WOUT, CO + 1):
                if i == CK:
                    piece_used(sp, WOUT)
                    sp.dma_start(memr[:], a["mem_prompt"][0].rearrange("(t p) n -> p t n", p=P)).then_inc(mem_landed, 16)
                big(i)
            sp.wait_ge(mk_normed, 3)
            sp.dma_start(a["mem_k_prompt"][0, 0].rearrange("(t p) h e -> p t (h e)", p=P), mk[:]).then_inc(mem_stored, 16)
            sp.dma_start(a["mem_v_prompt"][0, 0].rearrange("(t p) h e -> p t (h e)", p=P), mv[:]).then_inc(mem_stored, 16)

            def expert_weights(i, e):
                first = isinstance(i, int)
                for half in range(2):
                    if first:
                        piece_used(sp, CQ + half)
                    else:
                        sp.wait_ge(gu_used[half], i)
                    for m, w in enumerate(("w_e_gate", "w_e_up")):
                        src = a[w][0][e] if first else a[w][0][bass.ds(e, 1)].rearrange("o k n -> (o k) n")
                        sp.dma_start(ring[:, half, 4096 * m:4096 * m + 4096].rearrange("p (k n) -> p k n", k=8),
                                     src.rearrange("(p k) n -> p k n", k=KT)[:, 8 * half:8 * half + 8, :])\
                            .then_inc(gu_landed[half], 16)
                if not first:
                    sp.wait_ge(dn_used, i)
                src = a["w_e_down"][0][e] if first else a["w_e_down"][0][bass.ds(e, 1)].rearrange("o k n -> (o k) n")
                sp.dma_start(slot2.rearrange("p (k n) -> p k n", k=4), src.rearrange("(k p) n -> p k n", p=P))\
                    .then_inc(dn_landed, 16)

            piece_used(sp, CV)
            for w, lo, n in (("w_rg", 0, NG), ("w_re", NG, NE)):
                sp.dma_start(wr[:, :, lo:lo + n], a[w][0].rearrange("(p k) n -> p k n", k=KT)).then_inc(router_landed, 16)
            for w, lo, n in (("b_rg", 0, NG), ("b_re", NG, NE)):
                sp.dma_start(b36[lo:lo + n, :], a[w][0].rearrange("(n o) -> n o", o=1)).then_inc(router_landed, 16)
            expert_weights(0, 0)
            with sp.Fori(1, NE) as i:
                expert_weights(i, i)
            sp.wait_ge(slots_ready, 1)
            n_over = sp.value_load(ov_i[0:1, OVB:OVB + 1], min_val=0, max_val=OVB)
            with sp.If(n_over > 0):
                with sp.Fori(NE, NBLK) as i:
                    expert_weights(i, sp.value_load(ov_i[0:1, bass.ds(i - NE, 1)], min_val=0, max_val=NE - 1))
            for t in range(3):
                sp.wait_ge(x_final, t + 1)
                if t < 2:
                    sp.dma_start(a["y_prompt"][0, t * P:(t + 1) * P, :], x3[:, t, :]).then_inc(stored, 16)
                else:
                    sp.dma_start(a["y_sample"][:, 0], x3[0:NB, 2, :]).then_inc(stored, 16)
            sp.wait_ge(stored, 3 * 16)
            sp.wait_ge(copied, (2 * NB + 1) * 16)
            sp.wait_ge(rows_stored, 6 * 16)

        @block.gpsimd
        def _(pool):
            pool.wait_ge(zeros_ready, 2)
            pool.dma_start(xs_dram.rearrange("(p r) n -> p r n", p=P),
                           zero_rows.unsqueeze(1).to_broadcast([P, NBLK * BLK // P, D])).then_inc(xs_zeroed, 16)

            def cache_copy(i):
                b, kv = i // 2, i % 2
                src = a[("cache_win_k", "cache_win_v")[kv]][0, b, 1:WB].rearrange("s h e -> (s h e)")
                dst = a[("win_k_sample", "win_v_sample")[kv]][0, b, 0:WB - 1].rearrange("s h e -> (s h e)")
                pool.dma_start(dst.rearrange("(p f) -> p f", p=96), src.rearrange("(p f) -> p f", p=96)).then_inc(copied, 16)

            for i in range(5):
                piece_used(pool, i)
                cache_copy(i)
            pool.wait_ge(pads_ready, 1)
            pool.wait_ge(qk_normed, 3)
            for kv in range(2):
                cache = a[("cache_win_k", "cache_win_v")[kv]]
                new = (1 + kv) * AW
                for b in range(NB):
                    if kv == 0 and b >= 2:
                        pool.wait_ge(keys_used, b - 1)
                    if kv == 1 and b == 0:
                        pool.wait_ge(biased, H)
                        pool.dma_start(mask, cc("mask")).then_inc(mask_landed, 16)
                    if kv == 1 and b < 2:
                        pool.wait_ge(keys_used, NB - 1 + b)
                    if kv == 1 and b >= 2:
                        pool.wait_ge(vals_used, b - 1)
                    t, s = kvb[:, b % 2], kv_landed[b % 2]
                    c = cache[0, b].rearrange("s h e -> s (h e)")
                    pool.dma_start(t[:, 0], c[WB - P:WB]).then_inc(s, 16)
                    pool.dma_start(t[0:96, 1], c[WB - 512:WB - P].rearrange("(r q) n -> r q n", q=4)[:, 0]).then_inc(s, 16)
                    pool.dma_start(t[0:96, 2], c[0:1536].rearrange("(r q) n -> r q n", q=16)[:, 0]).then_inc(s, 16)
                    pool.dma_start(t[96:97, 1], z[b:b + 1, 2, new:new + AW]).then_inc(s, 16)
                    if b % 4 == 3:
                        cache_copy(5 + 2 * kv + b // 4)
            pool.dma_start(a["pool_sample"][0, :, 0:HIST - 1], a["state_pool"][0, :, 1:HIST]).then_inc(copied, 16)
            for i in range(9, 12):
                piece_used(pool, WOUT + i - 9)
                cache_copy(i)
            for kv in range(2):
                for b in range(NB):
                    if kv == 0 and b == 0:
                        pool.wait_ge(a_freed, A_DEC)
                        pool.dma_start(xmask, cc("xmask")).then_inc(mask_landed, 16)
                    if kv == 0 and b >= 2:
                        pool.wait_ge(keys_used, NB + b - 1)
                    if kv == 1 and b < 2:
                        pool.wait_ge(keys_used, 2 * NB - 1 + b)
                    if kv == 1 and b >= 2:
                        pool.wait_ge(vals_used, NB + b - 1)
                    c = a[("cache_mem_k", "cache_mem_v")[kv]][0, b].rearrange("(t p) h e -> p t (h e)", p=P)
                    pool.dma_start(xkv[:, b % 2], c).then_inc(kv_landed[b % 2], 16)
                    if b % 4 == 3:
                        cache_copy(12 + 2 * kv + b // 4)
            pool.wait_ge(xs_zeroed, 16)
            pool.wait_ge(xn_ready, 3)
            pool.wait_ge(slots_ready, 1)
            for s in range(2):
                for t in range(3):
                    n = P if t < 2 else NB
                    pool.indirect_dma_start(xs_dram[:, :], bass.IndirectOffsetOnAxis(ap=slot_i[0:n, s, t:t + 1], axis=0),
                                            xn[0:n, t, :], None).then_inc(scattered, 16)
            pool.wait_ge(scattered, 6 * 16)

            def block_rows(i):
                if not isinstance(i, int):
                    pool.wait_ge(xt_filled, i)
                rows = xs_dram[0:BLK] if isinstance(i, int) else xs_dram[bass.ds(i * BLK, BLK)]
                for c in range(4):
                    pool.dma_start(xe[32 * c:32 * c + 32, :], rows[:, 512 * c:512 * c + 512]).then_inc(xe_landed, 16)

            def gather_results(blocks):
                pool.wait_ge(y_stored, 64 * blocks)
                pool.wait_ge(dn_used, blocks)
                for t in range(3):
                    for s in range(2):
                        n = P if t < 2 else NB
                        j = 2 * t + s
                        pool.indirect_dma_start(ring[0:n, j // 4, (j % 4) * D:(j % 4 + 1) * D], None,
                                                ys_dram[0:BLK * blocks, :],
                                                bass.IndirectOffsetOnAxis(ap=slot_i[0:n, s, t:t + 1], axis=0))\
                            .then_inc(y_gathered[j], 16)

            block_rows(0)
            with pool.Fori(1, NE) as i:
                block_rows(i)
            n_over = pool.value_load(ov_i[0:1, OVB:OVB + 1], min_val=0, max_val=OVB)
            with pool.If(n_over > 0):
                with pool.Fori(NE, NBLK) as i:
                    block_rows(i)
                gather_results(NBLK)
            with pool.Else():
                gather_results(NE)

        @block.tensor
        def _(pe):
            nv = na = nd = 0
            mm = nc.tensor.matmul

            def vbank():
                nonlocal nv
                if nv >= 4:
                    pe.wait_ge(v_freed, nv - 3)
                nv += 1
                return VB[(nv - 1) % 4]

            def abank():
                nonlocal na
                if na >= 4:
                    pe.wait_ge(a_freed, na - 3)
                na += 1
                return AB[(na - 1) % 4]

            def all_emptied():
                pe.wait_ge(v_freed, nv)
                pe.wait_ge(a_freed, na)

            def norm_turn(rows, tiles):
                nonlocal nd
                nd += 1
                pe.wait_ge(diag_ready, nd)
                for t in range(tiles):
                    cols = rows[:, t, :].rearrange("p (m k) -> p k m", k=KT)
                    for j in range(4):
                        bk = vbank()
                        for k in range(4):
                            last = mm(bk[:, P * k:P * k + P], cols[:, 4 * j + k, :], dg[:, t, :], start=True, stop=True)
                        last.then_inc(v_filled, 1)

            def project(xT, w, nk, tile, bk, filled):
                for k in range(nk):
                    last = mm(bk[:, :], xT[:, k, tile * P:tile * P + P], w[:, k, :], start=(k == 0), stop=(k == nk - 1))
                last.then_inc(filled, 1)

            def project_sample(xT, w, nk, bk, filled):
                for k in range(nk):
                    for c in range(4):
                        last = mm(bk[32 * c:32 * c + 32, 0:P], xT[:, k, SEQ:TC], w[:, k, P * c:P * c + P],
                                  start=(k == 0), stop=(k == nk - 1))
                last.then_inc(filled, 1)

            pe.wait_ge(const_landed, 16 * N_CONST)
            pe.wait_ge(zeros_ready, 2)
            bk = vbank()
            mm(bk[0:H, 0:384], rb[0:33], ohp[0:33, :], start=True, stop=True).then_inc(v_filled, 1)
            bk = vbank()
            mm(bk[:, 0:NDEC], rbs[0:33].rearrange("p i h -> p (i h)"), ohs[0:33, :], start=True, stop=True)\
                .then_inc(v_filled, 1)
            norm_turn(x3, 3)
            all_emptied()
            for i in range(NCH):
                piece_landed(pe, i)
                project(hT, wk(i), KT, 0, abank(), a_filled)
                project_sample(hT, wk(i), KT, abank(), a_filled)
                project(hT, wk(i), KT, 1, vbank(), v_filled)
                if i == 1:
                    pe.wait_ge(bias_landed, 16)
                    for n in range(FLIPS):
                        mm(vbank()[:, :], flip, hankel[:, 512 * n:512 * n + 512], start=True, stop=True)\
                            .then_inc(v_filled, 1)
            pe.wait_ge(qk_normed, 3)
            for s in range(2):
                for pair in range(0, H // 2, 2):
                    bk = abank()
                    for j in range(2):
                        for t in range(2):
                            last = nc.tensor.transpose(bk[:, P * (2 * j + t):P * (2 * j + t) + P],
                                                       z[:, t, s * AW + P * (pair + j):s * AW + P * (pair + j) + P], ident[:])
                    last.then_inc(a_filled, 1)
            all_emptied()

            def attend(nh, score, turn, value):
                nonlocal probs_seen
                for s in range(nh + 2):
                    if s < nh:
                        score(s)
                    if 1 <= s <= nh:
                        probs_seen += 1
                        pe.wait_ge(probs_ready, probs_seen)
                        turn(s - 1)
                    if s >= 2:
                        value(s - 2)

            probs_seen = 0
            turned = {}

            def score_win(h):
                r = slice(64 * (h % 2), 64 * (h % 2) + 64)
                bk = vbank()
                mm(bk[:, 0:P], qkT[r, 0, h // 2, 0:P], qkT[r, 1, h // 2, 0:P], start=True, stop=True)
                mm(bk[:, P:3 * P], qkT[r, 0, h // 2, P:SEQ], qkT[r, 1, h // 2, :], start=True, stop=True)\
                    .then_inc(v_filled, 1)

            def turn_win(h):
                bk = abank()
                for j in range(3):
                    last = nc.tensor.transpose(bk[:, P * j:P * j + P], prb[:, h % 2, P * j:P * j + P], ident[:])
                last.then_inc(a_filled, 1)
                turned[h] = na

            def value_win(h):
                pe.wait_ge(a_freed, turned[h])
                bk = abank()
                r = slice(64 * (h % 2), 64 * (h % 2) + 64)
                v = slice(2 * AW + HD * h, 2 * AW + HD * h + HD)
                mm(bk[r, 0:SEQ], z[:, 0, v], prT[:, h % 2, 0:SEQ], start=True, stop=False)
                mm(bk[r, P:SEQ], z[:, 1, v], prT[:, h % 2, SEQ:3 * P], start=False, stop=True).then_inc(a_filled, 1)

            attend(H, score_win, turn_win, value_win)

            def pool_channels(c):
                bk = abank()
                parts = [(c // 2, (c % 2) * P, P, 0)] if c < 8 else [(2 * (c - 8) + o, 2 * P, 64, 64 * o) for o in range(2)]
                for g, lo, n, r in parts:
                    u = slice(3 * AW + PC * g + lo, 3 * AW + PC * g + lo + n)
                    us = slice(PC * g + lo, PC * g + lo + n)
                    o = slice(r, r + n)
                    mm(bk[o, 0:SEQ], z[:, 0, u], poolA[:, g, :], start=True, stop=False)
                    mm(bk[o, P:SEQ], z[:, 1, u], poolB[:, g, :], start=False, stop=True)
                    mm(bk[o, SEQ:TOK], state[0:NB * HIST, us], poolsc[0:NB * HIST, 0, g, :], start=True, stop=False)
                    last = mm(bk[o, SEQ:TOK], z[0:NB, 2, u], poolsc[0:NB, 1, g, :], start=False, stop=True)
                last.then_inc(a_filled, 1)

            def pool_map(kt):
                bk = abank()
                lo = kt * P
                while lo < kt * P + P:
                    g = lo // PC
                    d = lo % PC
                    n = min(PC - d, kt * P + P - lo)
                    o = slice(lo - kt * P, lo - kt * P + n)
                    for c in range(3):
                        if c < 2:
                            w, x = pw[:, 2 * g + c, d:d + n], poolT[:, 2 * g + c, :]
                        else:
                            r = slice(64 * (g % 2), 64 * (g % 2) + 64)
                            w, x = pw[r, 8 + g // 2, d:d + n], poolT[r, 8 + g // 2, :]
                        last = mm(bk[o, 0:TOK], w, x, start=(c == 0), stop=(c == 2))
                    lo += n
                last.then_inc(a_filled, 1)

            def query_row(rows, lo, n, b):
                bk = vbank()
                mm(bk[:, 0:n], ident[0:NB, b:b + 1].to_broadcast([NB, P]), rows[0:NB, 2, lo:lo + n], start=True, stop=True)\
                    .then_inc(v_filled, 1)

            piece_landed(pe, POOLW)
            pe.wait_ge(state_landed, 16)
            pe.wait_ge(poolc_landed, 16)
            for b in range(NB):
                query_row(z, 0, 512, b)
                query_row(z, 512, 256, b)
                if b < 5:
                    pool_channels(2 * b)
                    pool_channels(2 * b + 1)
                if b == 5:
                    pe.wait_ge(a_freed, na)
                if b >= 5:
                    for kt in range(3 * (b - 5), 3 * (b - 5) + 3 + (b == 7)):
                        pool_map(kt)

            def sample_softmax(tiles, offs, base):
                pe.wait_ge(keys_used, NB * (base + 1))
                for hf in range(2):
                    bk = vbank()
                    for t, n in enumerate(tiles):
                        last = nc.tensor.transpose(bk[:, offs[t]:offs[t] + n], s_in[0:n, t, hf, :], ident[0:n, 0:n])
                    last.then_inc(v_filled, 1)
                for hf in range(2):
                    pe.wait_ge(s_probs, 2 * base + hf + 1)
                    bk = abank()
                    for t, n in enumerate(tiles):
                        last = nc.tensor.transpose(bk[0:n, P * t:P * t + P], psm[:, hf, offs[t]:offs[t] + n], ident[:])
                    last.then_inc(a_filled, 1)
                pe.wait_ge(a_freed, na)

            def sample_values(tiles, widths, buf, masked_rows, landed, ktiles):
                for hf in range(2):
                    banks = [vbank() for _ in widths]
                    for i in range(4):
                        b = 4 * hf + i
                        pe.wait_ge(kv_landed[b % 2], landed(b))
                        for bk, (lo, n) in zip(banks, widths):
                            for t, k in enumerate(tiles):
                                last = mm(bk[32 * i:32 * i + 32, 0:n], s_in[0:k, t, hf, 32 * i:32 * i + 32],
                                          buf[0:k, b % 2, t, lo:lo + n], start=(t == 0), stop=(t == len(tiles) - 1))
                        if i < 3:
                            last.then_inc(vals_used, 1)
                    last.then_inc(v_filled, len(banks))
                    pe.wait_ge(v_freed, nv)
                    bk = abank()
                    for k in range(ktiles):
                        last = mm(bk[:, 4 * k:4 * k + 4], masked_rows[:, P * k:P * k + P], sel[:], start=True, stop=True)
                        if k == 0:
                            last.then_inc(vals_used, 1)
                    last.then_inc(a_filled, 1)

            sample_softmax(DEC_ROWS, DEC_OFF, 0)
            sample_values(DEC_ROWS, ((0, 512), (512, 256)), kvb, masked, lambda b: 64 * (NB // 2 + b // 2 + 1), H // 2)
            all_emptied()

            for i in range(WOUT, WOUT + 4):
                piece_landed(pe, i)
                project(mixT, wk(i), KT, 0, vbank(), v_filled)
                project(mixT, wk(i), KT, 1, vbank(), v_filled)
                project_sample(mixT, wk(i), KT, vbank(), v_filled)
            norm_turn(memr, 2)
            all_emptied()
            for i in (CK, CV):
                piece_landed(pe, i)
                project(hmT, wk(i), KT, 0, abank(), a_filled)
                project(hmT, wk(i), KT, 1, vbank(), v_filled)
            pe.wait_ge(mk_normed, 2)
            for pair in range(2):
                bk = abank()
                for j in range(2):
                    for t in range(2):
                        last = nc.tensor.transpose(bk[:, P * (2 * j + t):P * (2 * j + t) + P],
                                                   mk[:, t, P * (2 * pair + j):P * (2 * pair + j) + P], ident[:])
                last.then_inc(a_filled, 1)
            norm_turn(x3, 3)
            all_emptied()
            piece_landed(pe, CQ)
            project(hT, wk(CQ), KT, 0, abank(), a_filled)
            project_sample(hT, wk(CQ), KT, abank(), a_filled)
            project(hT, wk(CQ), KT, 1, vbank(), v_filled)
            pe.wait_ge(xq_normed, 3)
            for pair in range(2):
                bk = abank()
                for j in range(2):
                    for t in range(2):
                        last = nc.tensor.transpose(bk[:, P * (2 * j + t):P * (2 * j + t) + P],
                                                   xq[:, t, P * (2 * pair + j):P * (2 * pair + j) + P], ident[:])
                last.then_inc(a_filled, 1)
            all_emptied()

            def score_mem(h):
                bk = vbank()
                for t in range(2):
                    last = mm(bk[:, NM * t:NM * t + NM], xqT[:, h, P * t:P * t + P], mkT[:, h, :], start=True, stop=True)
                last.then_inc(v_filled, 1)

            def turn_mem(h):
                bk = abank()
                for m in range(2):
                    for t in range(2):
                        last = nc.tensor.transpose(bk[:, SEQ * m + P * t:SEQ * m + P * t + P],
                                                   xprb[:, h % 2, NM * t + P * m:NM * t + P * m + P], ident[:])
                last.then_inc(a_filled, 1)
                turned[h] = na

            def value_mem(h):
                pe.wait_ge(a_freed, turned[h])
                bk = abank()
                for m in range(2):
                    last = mm(bk[:, 0:SEQ], mv[:, m, XD * h:XD * h + XD], xprT[:, h % 2, SEQ * m:SEQ * m + SEQ],
                              start=(m == 0), stop=(m == 1))
                last.then_inc(a_filled, 1)

            attend(XH, score_mem, turn_mem, value_mem)
            for b in range(NB):
                query_row(xq, 0, XW, b)
            sample_softmax((P, P), (0, P), 1)
            sample_values((P, P), ((0, XW),), xkv, xmasked, lambda b: 64 * NB + 16 * (NB // 2 + b // 2 + 1), XH)
            all_emptied()
            piece_landed(pe, CO)
            wo = ring[:, CO % 2, :].rearrange("p (k n) -> p k n", k=XH)
            for n in range(4):
                w = wo[:, :, 512 * n:512 * n + 512]
                project(oT, w, XH, 0, vbank(), v_filled)
                project(oT, w, XH, 1, vbank(), v_filled)
                project_sample(oT, w, XH, vbank(), v_filled)

            norm_turn(x3, 3)
            all_emptied()
            pe.wait_ge(router_landed, 4 * 16)
            bk = vbank()
            for k in range(KT):
                last = mm(bk[0:36, 0:TOK], wr[:, k, :], hT[:, k, 0:TOK], start=(k == 0), stop=(k == KT - 1))
            last.then_inc(v_filled, 1)
            pe.wait_ge(v_freed, nv)
            bk = vbank()
            for t in range(3):
                n = P if t < 2 else NB
                last = nc.tensor.transpose(bk[0:n, 36 * t:36 * t + 36], LT[:, P * t:P * t + n], ident[0:36, 0:36])
            last.then_inc(v_filled, 1)
            pe.wait_ge(pairs_ready, 1)
            bk = vbank()
            pairs, before = rt[:, 0:96], rt[:, 96:224]
            mm(bk[:, 0:128], ones, before, start=True, stop=False)
            mm(bk[:, 0:96], tri[:], pairs, start=False, stop=True).then_inc(v_filled, 1)
            pe.wait_ge(over_cols_ready, 1)
            bk = vbank()
            mm(bk[:, 0:NE], ones[0:NE, :], rt[0:NE, 224:256], start=True, stop=True).then_inc(v_filled, 1)
            all_emptied()

            def expert(i):
                first = isinstance(i, int)
                pe.wait_ge(xe_landed, 64 * (i + 1))
                if not first:
                    pe.wait_ge(xt_ready, i)
                for j in range(4):
                    last = nc.tensor.transpose(pb[0][:, P * j:P * j + P], xe[:, P * j:P * j + P], ident[:])
                last.then_inc(xt_filled, 1)
                pe.wait_ge(xt_ready, i + 1)
                if not first:
                    pe.wait_ge(hid_ready, i)
                for half in range(2):
                    pe.wait_ge(gu_landed[half], 32 * (i + 1))
                    w = ring[:, half, :].rearrange("p (m k n) -> p m k n", m=2, k=8)
                    for k8 in range(8):
                        k = 8 * half + k8
                        for c in range(4):
                            last = mm(pb[1][32 * c:32 * c + 32, 0:256], XT[:, k % 4, 32 * (k // 4):32 * (k // 4) + 32],
                                      w[:, :, k8, P * c:P * c + P], start=(k == 0), stop=(k == KT - 1))
                    last.then_inc(gu_used[half], 1)
                pe.wait_ge(hid_ready, i + 1)
                if not first:
                    pe.wait_ge(hidT_ready, i)
                nc.tensor.transpose(pb[2][:, 0:P], hid, ident[:]).then_inc(hidT_filled, 1)
                pe.wait_ge(hidT_ready, i + 1)
                if not first:
                    pe.wait_ge(y_ready, i)
                pe.wait_ge(dn_landed, 16 * (i + 1))
                w = slot2.rearrange("p (k n) -> p k n", k=4)
                for f in range(4):
                    for c in range(4):
                        last = mm(pb[3][32 * c:32 * c + 32, :], aT[:, 32 * f:32 * f + 32], w[:, f, 512 * c:512 * c + 512],
                                  start=(f == 0), stop=(f == 3))
                last.then_inc(dn_used, 1)

            expert(0)
            with pe.Fori(1, NE) as i:
                expert(i)
            n_over = pe.value_load(ov_i[0:1, OVB:OVB + 1], min_val=0, max_val=OVB)
            with pe.If(n_over > 0):
                with pe.Fori(NE, NBLK) as i:
                    expert(i)

        @block.scalar
        def _(act):
            na = nroot = nsq = 0

            def filled():
                nonlocal na
                na += 1
                act.wait_ge(a_filled, na)
                return AB[(na - 1) % 4]

            def freed(ins):
                ins.then_inc(a_freed, 1)

            def norm_squares(rows, tiles, dump, col):
                nonlocal nroot, nsq
                for t in range(tiles):
                    if t:
                        act.wait_ge(squared, nsq)
                    nsq += 1
                    nc.scalar.activation(dump, rows[:, t, :], ACT.Square, accum_out=st[:, col + t:col + t + 1])\
                        .then_inc(squared, 1)
                roots(st[:, col + 3:col + 3 + tiles], st[:, col + 6:col + 6 + tiles])

            def roots(src, dst):
                nonlocal nroot
                nroot += 1
                act.wait_ge(mean_ready, nroot)
                nc.scalar.activation(dst, src, ACT.Sqrt).then_inc(root_ready, 1)

            def head_squares(rows, t, n, width, dump, heads):
                nonlocal nsq
                nsq += 1
                nc.scalar.activation(dump[0:n, 0:width], rows[0:n, t, 0:width], ACT.Square).then_inc(squared, 1)
                roots(st[0:n, 32:32 + heads], st[0:n, 64:64 + heads])

            def sample_rows(dst, bk, lo):
                for c in range(4):
                    last = nc.scalar.copy(dst[0:NB, 2, lo + P * c:lo + P * c + P], bk[32 * c:32 * c + NB, 0:P])
                freed(last)

            act.wait_ge(x_landed, 32)
            norm_squares(x3, 3, z[:, 0, 0:D], 0)
            act.wait_ge(squared, nsq)
            for i in range(NCH):
                freed(nc.scalar.copy(z[:, 0, 512 * i:512 * i + 512], filled()[:, :]))
                sample_rows(z, filled(), 512 * i)
            act.wait_ge(a_freed, na)
            act.wait_ge(v_freed, V_IN)
            for t in range(3):
                if t:
                    act.wait_ge(qk_normed, t)
                head_squares(z, t, P if t < 2 else NB, 2 * AW, sq, 2 * H)
            act.wait_ge(qk_normed, 3)
            for s in range(2):
                for pair in range(0, H // 2, 2):
                    freed(nc.scalar.copy(qkT[:, s, pair:pair + 2, :].rearrange("p j t -> p (j t)"), filled()[:, :]))

            heads_done = 0

            def attend(nh, parts, probs, turn, value):
                nonlocal heads_done
                for s in range(nh + 2):
                    if s < nh:
                        heads_done += 1
                        act.wait_ge(biased, heads_done)
                        q = 4 * (s % 2)
                        for j, (lo, hi) in enumerate(parts):
                            last = nc.scalar.activation(probs[:, s % 2, lo:hi], probs[:, s % 2, lo:hi], ACT.Exp,
                                                        bias=st[:, 96 + q + j:97 + q + j],
                                                        accum_out=st[:, 104 + q + j:105 + q + j])
                        last.then_inc(exped, 1)
                    if 1 <= s <= nh:
                        turn(s - 1)
                    if s >= 2:
                        value(s - 2)

            def value_win(h):
                r = slice(64 * (h % 2), 64 * (h % 2) + 64)
                freed(nc.scalar.copy(mixT[r, h // 2, 0:SEQ], filled()[r, 0:SEQ]))

            act.wait_ge(xs_zeroed, 16)
            attend(H, ((0, P), (P, 3 * P)), prb, lambda h: freed(nc.scalar.copy(prT[:, h % 2, :], filled()[:, 0:384])),
                   value_win)

            def pool_channels(c):
                freed(nc.scalar.copy(poolT[:, c, :], filled()[:, 0:TOK]))

            def pool_map(kt):
                freed(nc.scalar.mul(mixT[:, 6 + kt, 0:TOK], filled()[:, 0:TOK], psc[:, kt:kt + 1]))

            for c in range(10):
                pool_channels(c)
            for kt in range(10):
                pool_map(kt)

            def sample_softmax(base, width, tiles):
                for hf in range(2):
                    act.wait_ge(s_biased, 2 * base + hf + 1)
                    nc.scalar.activation(psm[:, hf, 0:width], psm[:, hf, 0:width], ACT.Exp, bias=st[:, 112 + hf:113 + hf],
                                         accum_out=st[:, 114 + hf:115 + hf]).then_inc(s_exped, 1)
                for hf in range(2):
                    bk = filled()
                    for t, n in enumerate(tiles):
                        last = nc.scalar.copy(s_in[0:n, t, hf, :], bk[0:n, P * t:P * t + P])
                    freed(last)

            def sample_out(dst, kts):
                for hf in range(2):
                    bk = filled()
                    freed(nc.scalar.copy(dst[:, 0:kts, SEQ + 4 * hf:SEQ + 4 * hf + 4],
                                         bk[:, 0:4 * kts].rearrange("p (k b) -> p k b", b=4)))

            sample_softmax(0, NDEC, DEC_ROWS)
            sample_out(mixT, H // 2)
            act.wait_ge(mem_landed, 16)
            norm_squares(memr, 2, mem_dump, 0)
            act.wait_ge(squared, nsq)
            freed(nc.scalar.copy(mk[:, 0, :], filled()[:, :]))
            act.wait_ge(a_freed, na)
            act.wait_ge(v_freed, V_MK)
            for t in range(2):
                if t:
                    act.wait_ge(mk_normed, t)
                head_squares(mk, t, P, XW, xsq, XH)
            freed(nc.scalar.copy(mv[:, 0, :], filled()[:, :]))
            for pair in range(2):
                freed(nc.scalar.copy(mkT[:, 2 * pair:2 * pair + 2, :].rearrange("p j t -> p (j t)"), filled()[:, :]))
            act.wait_ge(a_freed, na)
            act.wait_ge(v_freed, V_WOUT)
            norm_squares(x3, 3, zf[:, 0:D], 0)
            act.wait_ge(squared, nsq)
            freed(nc.scalar.copy(xq[:, 0, :], filled()[:, :]))
            sample_rows(xq, filled(), 0)
            act.wait_ge(a_freed, na)
            act.wait_ge(v_freed, V_CQ)
            for t in range(3):
                if t:
                    act.wait_ge(xq_normed, t)
                head_squares(xq, t, P if t < 2 else NB, XW, xsq, XH)
            act.wait_ge(xq_normed, 3)
            for pair in range(2):
                freed(nc.scalar.copy(xqT[:, 2 * pair:2 * pair + 2, :].rearrange("p j t -> p (j t)"), filled()[:, :]))
            attend(XH, ((0, NM), (NM, 2 * NM)), xprb, lambda h: freed(nc.scalar.copy(xprT[:, h % 2, :], filled()[:, :])),
                   lambda h: freed(nc.scalar.copy(oT[:, h, 0:SEQ], filled()[:, 0:SEQ])))
            sample_softmax(1, NM, (P, P))
            sample_out(oT, XH)
            act.wait_ge(v_freed, V_CO)
            act.wait_ge(mem_stored, 2 * 16)
            norm_squares(x3, 3, ffn_dump, 0)
            act.wait_ge(exp_in, 1)
            nc.scalar.activation(rt[:, 1300:1312], rt[:, 1300:1312], ACT.Exp).then_inc(exp_out, 1)
            act.wait_ge(exp_in, 2)
            nc.scalar.activation(rt[:, 1312:1315], rt[:, 1312:1315], ACT.Exp).then_inc(exp_out, 1)

            def expert(i):
                first = isinstance(i, int)
                act.wait_ge(gu_used[1], i + 1)
                nc.scalar.activation(ge, pb[1][:, 0:P], ACT.Exp, scale=-1.0).then_inc(gate_exp, 1)
                act.wait_ge(hidT_filled, i + 1)
                nc.scalar.copy(aT, pb[2][:, 0:P]).then_inc(hidT_ready, 1)
                act.wait_ge(dn_used, i + 1)
                if not first:
                    act.wait_ge(y_stored, 64 * i)
                nc.scalar.copy(yo, pb[3][:, :]).then_inc(y_ready, 1)
                act.wait_ge(y_ready, i + 1)
                rows = ys_dram[0:BLK] if first else ys_dram[bass.ds(i * BLK, BLK)]
                for c in range(4):
                    act.dma_start(rows[:, 512 * c:512 * c + 512], yo[32 * c:32 * c + 32, :]).then_inc(y_stored, 16)

            expert(0)
            with act.Fori(1, NE) as i:
                expert(i)
            n_over = act.value_load(ov_i[0:1, OVB:OVB + 1], min_val=0, max_val=OVB)
            with act.If(n_over > 0):
                with act.Fori(NE, NBLK) as i:
                    expert(i)

        @block.vector
        def _(dve):
            nv = nseq = nroot = nsq = 0
            V = nc.vector

            def filled():
                nonlocal nv
                nv += 1
                dve.wait_ge(v_filled, nv)
                return VB[(nv - 1) % 4]

            def link(ins):
                nonlocal nseq
                nseq += 1
                ins.then_inc(dve_seq, 1)
                dve.wait_ge(dve_seq, nseq)

            def mean_root(sums, mean, root, inv, n):
                nonlocal nroot
                V.tensor_scalar(mean, sums, 1.0 / n, EPS, ALU.mult, ALU.add).then_inc(mean_ready, 1)
                nroot += 1
                dve.wait_ge(root_ready, nroot)
                link(V.reciprocal(inv, root))

            def norm(tiles, gain, dst):
                nonlocal nsq
                nsq += tiles
                dve.wait_ge(squared, nsq)
                mean_root(st[:, 0:tiles], st[:, 3:3 + tiles], st[:, 6:6 + tiles], st[:, 9:9 + tiles], D)
                for t in range(tiles):
                    last = V.tensor_scalar(dg[:, t, :], ident[:], st[:, 9 + t:10 + t], None, ALU.mult)
                last.then_inc(diag_ready, 1)
                for t in range(tiles):
                    for j in range(4):
                        n = P if t < 2 else 32
                        src = filled()[:, :].rearrange("p (k m) -> p k m", k=4)[:, :, 0:n]
                        V.tensor_tensor(dst[:, 4 * j:4 * j + 4, P * t:P * t + n], src,
                                        gT[:, gain, 4 * j:4 * j + 4].unsqueeze(2).to_broadcast([P, 4, n]), ALU.mult)\
                            .then_inc(v_freed, 1)

            def head_norm(rows, t, n, heads, width, squares, gain, done):
                nonlocal nsq
                nsq += 1
                dve.wait_ge(squared, nsq)
                sm, mean, root, inv = (st[0:n, c:c + heads] for c in (128, 32, 64, 128))
                link(V.tensor_reduce(sm, squares[0:n, 0:heads * width].rearrange("p (h e) -> p h e", h=heads), AX.X, ALU.add))
                mean_root(sm, mean, root, inv, width)
                r3 = rows[0:n, t, 0:heads * width].rearrange("p (h e) -> p h e", h=heads)
                link(V.tensor_tensor(r3, r3, inv.unsqueeze(2).to_broadcast([n, heads, width]), ALU.mult))
                gs = [gain[0:n, g, :].unsqueeze(1) for g in (range(2) if heads == 2 * H else done[1])]
                per = heads // len(gs)
                for i, g in enumerate(gs):
                    part = r3[:, i * per:(i + 1) * per, :]
                    last = V.tensor_tensor(part, part, g.to_broadcast([n, per, width]), ALU.mult)
                last.then_inc(done[0], 1)

            V.memset(rbs[0:32].rearrange("p i h -> p (i h)"), 0.0)
            V.memset(x3[:, 2, :], 0.0).then_inc(zeros_ready, 1)
            V.memset(slot2[:, 0:AFTER_MIX], 0.0)
            V.memset(s_in[:].rearrange("p a b c -> p (a b c)"), 0.0)
            V.memset(rb[32:33], 1.0)
            link(V.memset(rbs[32:33].rearrange("p i h -> p (i h)"), 1.0))
            dve.nop().then_inc(zeros_ready, 1)
            dve.wait_ge(const_landed, 16 * N_CONST)
            V.tensor_copy(brow[0:H, :], filled()[0:H, 0:384]).then_inc(v_freed, 1)
            V.tensor_copy(biasS, filled()[:, 0:NDEC]).then_inc(v_freed, 1)
            norm(3, 0, hT)
            for i in range(NCH):
                V.tensor_copy(z[:, 1, 512 * i:512 * i + 512], filled()[:, :]).then_inc(v_freed, 1)
                for n in range(FLIPS if i == 1 else 0):
                    V.tensor_copy(bias_flat[:, 512 * n:512 * n + 512], filled()[:, :]).then_inc(v_freed, 1)
            dve.wait_ge(v_freed, nv)
            dve.wait_ge(a_freed, 2 * NCH)
            for t in range(3):
                head_norm(z, t, P if t < 2 else NB, 2 * H, HD, sq, gqk, (qk_normed, None))
            piece_used(dve, NCH - 1)
            V.memset(kvb[96:P, 0, 1:3], 0.0)
            V.memset(kvb[96:P, 1, 1:3], 0.0).then_inc(pads_ready, 1)

            heads_done = 0

            def attend(nh, parts, probs, enter, a_before):
                nonlocal heads_done
                for s in range(nh + 1):
                    if s < nh:
                        bk = filled()
                        if s >= 2:
                            dve.wait_ge(a_freed, a_before + turn_job(s - 2) + 1)
                        enter(s, bk)
                        dve.wait_ge(v_freed, nv)
                        q = 4 * (s % 2)
                        for j, (lo, hi) in enumerate(parts):
                            last = V.tensor_reduce(st[:, 116 + j:117 + j], probs[:, s % 2, lo:hi], AX.X, ALU.max)
                        link(last)
                        V.tensor_scalar(st[:, 96 + q:98 + q], st[:, 116:118], -1.0, None, ALU.mult).then_inc(biased, 1)
                    if s >= 1:
                        h = s - 1
                        heads_done += 1
                        dve.wait_ge(exped, heads_done)
                        q = 4 * (h % 2)
                        if heads_done > 1:
                            dve.wait_ge(probs_ready, heads_done - 1)
                        link(V.reciprocal(st[:, 118:120], st[:, 104 + q:106 + q]))
                        for j, (lo, hi) in enumerate(parts):
                            last = V.tensor_scalar(probs[:, h % 2, lo:hi], probs[:, h % 2, lo:hi], st[:, 118 + j:119 + j],
                                                   None, ALU.mult)
                        last.then_inc(probs_ready, 1)

            def enter_win(h, bk):
                V.scalar_tensor_tensor(out=prb[:, h % 2, 0:P], in0=bk[:, 0:P], scalar=HD ** -0.5, in1=bias[:, h, P:SEQ],
                                       op0=ALU.mult, op1=ALU.add)
                V.scalar_tensor_tensor(out=prb[:, h % 2, P:3 * P], in0=bk[:, P:3 * P], scalar=HD ** -0.5, in1=bias[:, h, :],
                                       op0=ALU.mult, op1=ALU.add).then_inc(v_freed, 1)

            dve.wait_ge(rows_stored, 6 * 16)
            dve.wait_ge(a_freed, A_QKT)
            attend(H, ((0, P), (P, 3 * P)), prb, enter_win, A_QKT)

            def sample_scores(buf, tiles, widths, heads_of, landed, width):
                for b in range(NB):
                    dve.wait_ge(kv_landed[b % 2], landed(b))
                    hf, i = b // 4, b % 4
                    for (lo, n) in widths:
                        src = buf[:, b % 2, :, lo:lo + n]
                        V.tensor_tensor(src, src, filled()[:, 0:n].unsqueeze(1).to_broadcast([P, tiles, n]), ALU.mult)\
                            .then_inc(v_freed, 1)
                    dve.wait_ge(v_freed, nv)
                    last = V.tensor_reduce(s_in[:, 0:tiles, hf, 32 * i:32 * i + heads_of],
                                           buf[:, b % 2].rearrange("p t (h e) -> p t h e", e=width), AX.X, ALU.add)
                    last.then_inc(keys_used, 1)

            def sample_softmax(base, width, scale, rows):
                for hf in range(2):
                    bk = filled()
                    if rows is not None:
                        V.scalar_tensor_tensor(out=psm[:, hf, 0:width], in0=bk[:, 0:width], scalar=scale, in1=rows,
                                               op0=ALU.mult, op1=ALU.add).then_inc(v_freed, 1)
                    else:
                        V.tensor_scalar(psm[:, hf, 0:width], bk[:, 0:width], scale, None, ALU.mult).then_inc(v_freed, 1)
                    dve.wait_ge(v_freed, nv)
                    link(V.tensor_reduce(st[:, 120:121], psm[:, hf, 0:width], AX.X, ALU.max))
                    V.tensor_scalar(st[:, 112 + hf:113 + hf], st[:, 120:121], -1.0, None, ALU.mult).then_inc(s_biased, 1)
                for hf in range(2):
                    dve.wait_ge(s_exped, 2 * base + hf + 1)
                    link(V.reciprocal(st[:, 122 + hf:123 + hf], st[:, 114 + hf:115 + hf]))
                    V.tensor_scalar(psm[:, hf, 0:width], psm[:, hf, 0:width], st[:, 122 + hf:123 + hf], None, ALU.mult)\
                        .then_inc(s_probs, 1)

            def sample_mask(widths, out, m, a_before):
                for hf in range(2):
                    if hf:
                        dve.wait_ge(a_freed, a_before + 1)
                    for j, (lo, n) in enumerate(widths):
                        last = V.tensor_tensor(out[:, lo:lo + n], filled()[:, 0:n], m[:, lo:lo + n], ALU.mult)
                        last.then_inc(v_freed, 1)

            sample_scores(kvb, 3, ((0, 512), (512, 256)), H, lambda b: 64 * (b // 2 + 1), HD)
            sample_softmax(0, NDEC, HD ** -0.5, biasS)
            dve.wait_ge(mask_landed, 16)
            sample_mask(((0, 512), (512, 256)), masked, mask, A_DEC - 2)

            def add_rows(n, p_rows):
                c = slice(512 * n, 512 * n + 512)
                for t in range(2):
                    V.tensor_tensor(x3[:, t, c], filled()[:, :], x3[:, t, c], ALU.add).then_inc(v_freed, 1)
                bk = filled()
                for j in range(4):
                    d = x3[0:NB, 2, 512 * n + P * j:512 * n + P * j + P]
                    last = V.tensor_tensor(d, bk[32 * j:32 * j + NB, 0:P], d, ALU.add)
                last.then_inc(v_freed, 1)

            for n in range(4):
                add_rows(n, None)
            dve.wait_ge(v_freed, nv)
            assert nv == V_WOUT
            V.memset(oT[:, :, TOK:TC], 0.0)
            norm(2, 1, hmT)
            V.tensor_copy(mk[:, 1, :], filled()[:, :]).then_inc(v_freed, 1)
            assert nv == V_MK
            dve.wait_ge(v_freed, nv)
            for t in range(2):
                head_norm(mk, t, P, XH, XD, xsq, gxx, (mk_normed, (1,)))
            V.tensor_copy(mv[:, 1, :], filled()[:, :]).then_inc(v_freed, 1)
            dve.wait_ge(v_freed, nv)
            dve.wait_ge(a_freed, A_MV)
            dve.nop().then_inc(mk_normed, 1)
            norm(3, 2, hT)
            V.tensor_copy(xq[:, 1, :], filled()[:, :]).then_inc(v_freed, 1)
            assert nv == V_CQ
            dve.wait_ge(v_freed, nv)
            for t in range(3):
                head_norm(xq, t, P if t < 2 else NB, XH, XD, xsq, gxx, (xq_normed, (0,)))
            attend(XH, ((0, NM), (NM, 2 * NM)), xprb,
                   lambda h, bk: V.tensor_scalar(xprb[:, h % 2, :], bk[:, :], XD ** -0.5, None, ALU.mult).then_inc(v_freed, 1),
                   A_XQT)
            sample_scores(xkv, 2, ((0, XW),), XH, lambda b: 64 * NB + 16 * (b // 2 + 1), XD)
            sample_softmax(1, NM, XD ** -0.5, None)
            dve.wait_ge(mask_landed, 32)
            sample_mask(((0, XW),), xmasked, xmask, A_XQT + 2 * XH + 2)
            for n in range(4):
                add_rows(n, None)
            dve.wait_ge(v_freed, nv)
            assert nv == V_CO
            norm(3, 3, hT)
            V.memset(ones, 1.0)
            for t in range(3):
                V.tensor_scalar(xn[:, t, :].rearrange("p (k m) -> p k m", k=KT), x3[:, t, :].rearrange("p (m k) -> p k m", k=KT),
                                st[:, 9 + t:10 + t], None, ALU.mult).then_inc(xn_ready, 1)
            dve.wait_ge(router_landed, 4 * 16)
            V.tensor_scalar(LT, filled()[0:36, 0:TOK], b36, None, ALU.add).then_inc(v_freed, 1)
            R = lambda lo, n: rt[:, lo:lo + 3 * n].rearrange("p (t n) -> p t n", t=3)
            L36 = R(260, 36)
            pen, le, eq, c1, oh1, oh2 = R(370, 4), R(384, NE), R(480, NE), R(576, NE), R(672, NE), R(768, NE)
            lg2, ohg, m1, m2, cm = R(1300, 4), R(864, 4), R(880, 1), R(884, 1), R(888, 1)
            gmax, gsum, pgrp = R(892, 1), R(896, 1), R(900, 1)
            slotE, cnt, xo, xinc, tmp, cmp = R(904, NE), rt[:, 1000:1032], rt[:, 1032:1064], rt[:, 1064:1096], R(1100, NE), rt[:, 1200:1232]
            desc = moec[:, 0:NE].unsqueeze(1).to_broadcast([P, 3, NE])
            base = moec[:, NE:2 * NE].unsqueeze(1).to_broadcast([P, 3, NE])
            valid = moec[:, 2 * NE:2 * NE + 3].unsqueeze(2).to_broadcast([P, 3, NE])
            TT = V.tensor_tensor

            def b(x, n):
                return x.to_broadcast([P, 3, n])

            link(V.memset(L36, 0.0))
            bk = filled()
            V.tensor_copy(L36[:, 0:2, :], bk[:, 0:72].rearrange("p (t n) -> p t n", t=2))
            link(V.tensor_copy(L36[0:NB, 2, :], bk[0:NB, 72:108]))
            dve.nop().then_inc(v_freed, 1)
            lg = L36[:, :, 0:NG]
            link(V.tensor_reduce(gmax, lg, AX.X, ALU.max))
            TT(lg2, lg, b(gmax, NG), ALU.subtract).then_inc(exp_in, 1)
            link(TT(ohg, lg, b(gmax, NG), ALU.is_equal))
            link(TT(ohg, ohg, moec[:, NE - NG:NE].unsqueeze(1).to_broadcast([P, 3, NG]), ALU.mult))
            link(V.tensor_reduce(cm, ohg, AX.X, ALU.max))
            link(TT(ohg, ohg, b(cm, NG), ALU.is_equal))
            link(V.tensor_scalar(pen, ohg, -NEG, NEG, ALU.mult, ALU.add))
            for t in range(3):
                last = TT(le[:, t, :].rearrange("p (g e) -> p g e", g=NG), L36[:, t, NG:36].rearrange("p (g e) -> p g e", g=NG),
                          pen[:, t, :].unsqueeze(2).to_broadcast([P, NG, EG]), ALU.add)
            link(last)

            def top(oh, m):
                link(V.tensor_reduce(m, le, AX.X, ALU.max))
                link(TT(eq, le, b(m, NE), ALU.is_equal))
                link(TT(c1, eq, desc, ALU.mult))
                link(V.tensor_reduce(cm, c1, AX.X, ALU.max))
                link(TT(oh, c1, b(cm, NE), ALU.is_equal))

            top(oh1, m1)
            link(V.scalar_tensor_tensor(out=le, in0=oh1, scalar=3 * NEG, in1=le, op0=ALU.mult, op1=ALU.add))
            top(oh2, m2)
            dve.wait_ge(exp_out, 1)
            link(V.tensor_reduce(gsum, lg2, AX.X, ALU.add))
            e2 = R(1312, 1)
            TT(e2, m2, m1, ALU.subtract).then_inc(exp_in, 1)
            pairs = R(0, NE)
            link(TT(c1, oh1, oh2, ALU.add))
            link(TT(pairs, c1, valid, ALU.mult))
            before = rt[:, 96:224]
            V.memset(before[:, 0:NE], 0.0)
            link(V.tensor_copy(before[:, NE:2 * NE], pairs[:, 0, :]))
            link(TT(before[:, 2 * NE:3 * NE], before[:, NE:2 * NE], pairs[:, 1, :], ALU.add))
            TT(before[:, 3 * NE:4 * NE], before[:, 2 * NE:3 * NE], pairs[:, 2, :], ALU.add).then_inc(pairs_ready, 1)
            dve.wait_ge(exp_out, 2)
            link(V.reciprocal(pgrp, gsum))
            link(V.tensor_scalar(m1, e2, 1.0, None, ALU.add))
            link(V.reciprocal(m2, m1))
            link(TT(gates[:, 0, :].unsqueeze(2), m2, pgrp, ALU.mult))
            link(TT(gates[:, 1, :].unsqueeze(2), gates[:, 0, :].unsqueeze(2), e2, ALU.mult))
            pos = filled()
            link(V.tensor_copy(cnt, pos[:, 96:128]))
            link(V.tensor_scalar(xo, cnt, float(BLK), None, ALU.is_gt))
            for j in range(2, -(-TOK // BLK)):
                link(V.scalar_tensor_tensor(out=xo, in0=cnt, scalar=float(BLK * j), in1=xo, op0=ALU.is_gt, op1=ALU.add))
            link(TT(tmp[0:NE, 0, :], xo[0:NE, :], ident[0:NE, 0:NE], ALU.mult))
            link(V.tensor_reduce(cm[0:NE, 0, :], tmp[0:NE, 0, :], AX.X, ALU.add))
            V.tensor_scalar(rt[0:NE, 224:256], tri[0:NE, 0:NE], cm[0:NE, 0, :], None, ALU.mult).then_inc(over_cols_ready, 1)
            xb = filled()
            link(V.tensor_scalar(cmp, xb[:, 0:NE], float(BLK), float(NE * BLK - BLK), ALU.mult, ALU.add))
            link(TT(cmp, cmp, moec[:, NE:2 * NE], ALU.subtract))
            p3 = pos[:, 0:96].rearrange("p (t n) -> p t n", t=3)
            link(V.tensor_scalar(tmp, p3, float(BLK), None, ALU.is_ge))
            link(TT(tmp, tmp, cmp.unsqueeze(1).to_broadcast([P, 3, NE]), ALU.mult))
            link(TT(tmp, tmp, base, ALU.add))
            link(TT(slotE, p3, tmp, ALU.add))
            for s, oh in enumerate((oh1, oh2)):
                link(TT(c1, oh, slotE, ALU.mult))
                link(V.tensor_reduce(cm, c1, AX.X, ALU.add))
                link(V.tensor_copy(slot_i[:, s, :], cm[:, :, 0]))
            link(TT(xinc, xb[:, 0:NE], xo, ALU.add))
            o3 = rt[0:1, 300:300 + OVB * NE].rearrange("p (o e) -> p o e", o=OVB)
            link(TT(o3, moec[0:1, 2 * NE + 3:2 * NE + 3 + OVB].unsqueeze(2).to_broadcast([1, OVB, NE]),
                    xinc[0:1, :].unsqueeze(1).to_broadcast([1, OVB, NE]), ALU.is_ge))
            link(V.tensor_reduce(rt[0:1, 1400:1400 + OVB], o3, AX.X, ALU.add))
            link(V.tensor_scalar(rt[0:1, 1400:1400 + OVB], rt[0:1, 1400:1400 + OVB], float(NE - 1), None, ALU.min))
            V.tensor_copy(ov_i[0:1, 0:OVB], rt[0:1, 1400:1400 + OVB])
            link(V.tensor_copy(ov_i[0:1, OVB:OVB + 1], xinc[0:1, NE - 1:NE]))
            dve.nop().then_inc(v_freed, 2)
            dve.nop().then_inc(slots_ready, 1)

            def expert(i):
                first = isinstance(i, int)
                dve.wait_ge(xt_filled, i + 1)
                if not first:
                    dve.wait_ge(gu_used[1], i)
                V.tensor_tensor(XT.rearrange("p j (c s) -> p j c s", c=4), pb[0][:, :].rearrange("p (j c s) -> p j c s", j=4, c=4),
                                gT[:, 3, :].rearrange("p (c j) -> p j c", j=4).unsqueeze(3).to_broadcast([P, 4, 4, 32]),
                                ALU.mult).then_inc(xt_ready, 1)
                dve.wait_ge(gate_exp, i + 1)
                V.tensor_scalar(gd, ge, 1.0, None, ALU.add).then_inc(hid_seq, 1)
                dve.wait_ge(hid_seq, 3 * i + 1)
                V.reciprocal(gr, gd).then_inc(hid_seq, 1)
                dve.wait_ge(hid_seq, 3 * i + 2)
                V.tensor_tensor(gd, pb[1][:, 0:P], gr, ALU.mult).then_inc(hid_seq, 1)
                dve.wait_ge(hid_seq, 3 * i + 3)
                V.tensor_tensor(hid, pb[1][:, P:2 * P], gd, ALU.mult).then_inc(hid_ready, 1)

            expert(0)
            with dve.Fori(1, NE) as i:
                expert(i)
            n_over = dve.value_load(ov_i[0:1, OVB:OVB + 1], min_val=0, max_val=OVB)
            with dve.If(n_over > 0):
                with dve.Fori(NE, NBLK) as i:
                    expert(i)
            for t in range(3):
                n = P if t < 2 else NB
                for s in range(2):
                    j = 2 * t + s
                    dve.wait_ge(y_gathered[j], 16)
                    ins = V.scalar_tensor_tensor(out=x3[0:n, t, :], in0=ring[0:n, j // 4, (j % 4) * D:(j % 4 + 1) * D],
                                                 scalar=gates[0:n, s, t:t + 1], in1=x3[0:n, t, :], op0=ALU.mult, op1=ALU.add)
                    if s == 0:
                        link(ins)
                    else:
                        ins.then_inc(x_final, 1)


_INS = ['x_prompt', 'x_sample', 'cache_win_k', 'cache_win_v', 'state_pool', 'cache_mem_k', 'cache_mem_v', 'mem_prompt',
        'rel_bias', 'norm_mix_g', 'w_in', 'q_norm_g', 'k_norm_g', 'pool_w', 'pool_scale', 'w_out', 'norm_cross_g',
        'norm_mem_g', 'w_cq', 'w_ck', 'w_cv', 'cq_norm_g', 'ck_norm_g', 'w_co', 'norm_ffn_g', 'w_rg', 'b_rg', 'w_re',
        'b_re', 'w_e_gate', 'w_e_up', 'w_e_down']
_OUTS = [('y_prompt', (1, SEQ, D)), ('y_sample', (NB, 1, D)),
         ('win_k_prompt', (1, 1, SEQ, H, HD)), ('win_v_prompt', (1, 1, SEQ, H, HD)),
         ('win_k_sample', (1, NB, WB, H, HD)), ('win_v_sample', (1, NB, WB, H, HD)),
         ('pool_prompt', (1, 1, HIST, PW)), ('pool_sample', (1, NB, HIST, PW)),
         ('mem_k_prompt', (1, 1, NM, XH, XD)), ('mem_v_prompt', (1, 1, NM, XH, XD))]


def kernel(**inputs):
    import concourse.bacc as _bacc
    from concourse.bass_utils import run_bass_kernel_spmd as _run

    nc = _bacc.Bacc("TRN2", target_bir_lowering=False, num_devices=1)
    arrays, args = {}, {}
    for name in _INS + ["const"]:
        arr = constants() if name == "const" else np.ascontiguousarray(inputs[name])
        arrays[f"in_{name}_dram"] = arr
        args[name] = nc.dram_tensor(f"in_{name}_dram", arr.shape, mybir.dt.from_np(arr.dtype), kind="ExternalInput").ap()
    for name, shape in _OUTS:
        args[name] = nc.dram_tensor(f"out_{name}_dram", shape, F32, kind="ExternalOutput").ap()
    hybrid_decoder_layer(nc, args)
    r = _run(nc, [arrays], core_ids=[0])
    return tuple(r.results[0][f"out_{name}_dram"] for name, _ in _OUTS)
```

```python
from contextlib import ExitStack
import math

import numpy as np
import concourse.bass as bass
from concourse import mybir

F32 = mybir.dt.float32
I32 = mybir.dt.int32
U32 = mybir.dt.uint32
ALU = mybir.AluOpType
ACT = mybir.ActivationFunctionType
AX = mybir.AxisListType

P = 128
D = 2048
KT = D // P
SEQ = 256
PT = SEQ // P
NB = 8
TOK = SEQ + NB
TC = SEQ + 32
H, HD = 12, 64
AW = H * HD
POOL_WINDOWS = (2, 4, 8, 16)
PG, PC = 4, 320
PW = PG * PC
HIST = 15
IN_W = 3 * AW + PW
NCH = IN_W // 512
WB = 2048
NM = 256
XH, XD = 4, 128
XW = XH * XD
NG, EG = 4, 8
NE = NG * EG
DE = 512
EPS = 1e-6
NEG = -1e30
BLK = 32
OVB = 2 * TOK // BLK
NBLK = NE + OVB
NBUCKET, MAXD = 32, 2048
BRANCHES = ((128, 1), (512, 4), (2048, 16))


def bucket(dist):
    n = np.asarray(dist, dtype=np.int64)
    exact = NBUCKET // 2
    ratio = np.log(np.maximum(n, 1) / exact) / np.log(MAXD / exact)
    large = np.minimum(exact + (ratio * (NBUCKET - exact)).astype(np.int64), NBUCKET - 1)
    return np.where(n < exact, n, large)


def bias_columns(dist):
    dist = np.asarray(dist)
    out = np.zeros((NBUCKET + 1, len(dist)), np.float32)
    for c, d in enumerate(dist):
        mult = sum(1 for w, s in BRANCHES if 0 <= d <= w and d % s == 0)
        if mult:
            out[bucket(d), c] = 1.0
            out[NBUCKET, c] = math.log(mult)
        else:
            out[NBUCKET, c] = NEG
    return out


DEC_ROWS = (P, 97, 96)
DEC_OFF = (0, P, P + 97)
NDEC = sum(DEC_ROWS)
DEC_DIST = ([P - r for r in range(P)] + [512 - 4 * r for r in range(96)] + [0] + [2048 - 16 * r for r in range(96)])

CONST_W = dict(ident=P, tri=P, moe=NE + NE + 3 + OVB, pool=PG * 256 + PG * P, pools=2 * PG * NB,
               flip=P, mask=AW, xmask=XW, sel=4, ohp=384, ohs=NDEC)
CONST_AT = {}
_at = 0
for _k, _w in CONST_W.items():
    CONST_AT[_k] = (_at, _at + _w)
    _at += _w
CONST_N = _at


def constants():
    c = np.zeros((P, CONST_N), np.float32)

    def part(name):
        a, b = CONST_AT[name]
        return c[:, a:b]

    part("ident")[:] = np.eye(P)
    part("flip")[:] = np.eye(P)[::-1]
    part("tri")[:] = np.triu(np.ones((P, P)), 1)
    m = part("moe")
    m[:, 0:NE] = NE - np.arange(NE)
    m[:, NE:2 * NE] = BLK * np.arange(NE)
    m[:, 2 * NE:2 * NE + 3] = 1.0
    m[NB:, 2 * NE + 2] = 0.0
    m[:, 2 * NE + 3:] = np.arange(OVB)
    full = np.zeros((PG, SEQ, SEQ), np.float32)
    for g, w in enumerate(POOL_WINDOWS):
        for t in range(SEQ):
            lo = max(t + 1 - w, 0)
            full[g, lo:t + 1, t] = 1.0 / min(w, t + 1)
            full[g, t, t] -= 1.0
    pool = part("pool")
    pool[:, 0:PG * 256] = full[:, 0:P].transpose(1, 0, 2).reshape(P, -1)
    pool[:, PG * 256:] = full[:, P:, P:].transpose(1, 0, 2).reshape(P, -1)
    ps = part("pools").reshape(P, 2, PG, NB)
    for g, w in enumerate(POOL_WINDOWS):
        for b in range(NB):
            ps[b * HIST + HIST - (w - 1):b * HIST + HIST, 0, g, b] = 1.0 / w
            ps[b, 1, g, b] = 1.0 / w - 1.0
    for i in range(4):
        for h in range(H):
            part("mask")[32 * i + h, h * HD:(h + 1) * HD] = 1.0
        for h in range(XH):
            part("xmask")[32 * i + h, h * XD:(h + 1) * XD] = 1.0
        part("sel")[32 * i:32 * i + 32, i] = 1.0
    part("ohp")[0:NBUCKET + 1] = bias_columns([255 - v for v in range(384)])
    part("ohs")[0:NBUCKET + 1] = bias_columns(DEC_DIST)
    return c


def hybrid_decoder_layer(nc, a):
    with ExitStack() as ctx:
        def sem(name):
            return ctx.enter_context(nc.semaphore(name))

        def sb(name, shape, dt=F32):
            return ctx.enter_context(nc.sbuf_tensor(name, shape, dt))

        bias_dram = nc.dram_tensor("bias_rows", (H, 384), F32, kind="Internal").ap()
        xs_dram = nc.dram_tensor("moe_in", (NBLK * BLK, D), F32, kind="Internal").ap()
        ys_dram = nc.dram_tensor("moe_out", (NBLK * BLK, D), F32, kind="Internal").ap()

        ring = sb("ring", [P, 3, 8192])
        x3 = sb("x3", [P, 3, D])
        hT = sb("hT", [P, KT, TC])
        z = sb("z", [P, 3, IN_W])
        mkT = sb("mkT", [P, XH, NM])
        qkT = sb("qkT", [P, 2, H // 2, SEQ])
        ident = sb("ident", [P, P])
        tri = sb("tri", [P, P])
        dg = sb("dg", [P, 3, P])
        s_in = sb("s_in", [P, 3, 2, P])
        psm = sb("psm", [P, 2, NDEC])
        moec = sb("moec", [P, 2 * NE + 3 + OVB])
        poolsc = sb("poolsc", [P, 2, PG, NB])
        sel = sb("sel", [P, 4])
        gT = sb("gT", [P, 4, KT])
        gqk = sb("gqk", [P, 2, HD])
        gxx = sb("gxx", [P, 2, XD])
        psc = sb("psc", [P, PW // P])
        st = sb("st", [P, 152])
        slot_i = sb("slot_i", [P, 2, 3], U32)
        gates = sb("gates", [P, 2, 3])
        ov_i = sb("ov_i", [1, OVB + 1], I32)

        slot2 = ring[:, 2, :]
        mixT = slot2[:, 0:KT * TC].rearrange("p (k t) -> p k t", k=KT)
        hmT = slot2[:, 0:KT * NM].rearrange("p (k t) -> p k t", k=KT)
        AFTER_MIX = KT * TC
        bias = slot2[:, AFTER_MIX:AFTER_MIX + H * SEQ].rearrange("p (h j) -> p h j", h=H)
        bias_flat = after_mix = slot2[:, AFTER_MIX:AFTER_MIX + H * SEQ]
        biasS = slot2[:, AFTER_MIX + H * SEQ:AFTER_MIX + H * SEQ + NDEC]
        qkt_flat = qkT[:].rearrange("p a h t -> p (a h t)")
        rb = psm[:, 0, 0:H]
        rbs = psm[:, 0, 16:144].rearrange("p (i h) -> p i h", i=4)
        flip = slot2[:, 8192 - P:8192]
        hankel = qkt_flat
        ohp = qkt_flat[:, 0:384]
        ohs = qkt_flat[:, 384:384 + NDEC]
        brow = qkt_flat[:, 768:768 + 384]
        sq = qkt_flat[:, 1536:1536 + 2 * AW]
        zf = z[:].rearrange("p t n -> p (t n)")
        CK, CV, IN0 = 0, 1, 2
        POOLW = IN0 + NCH
        WOUT = POOLW + 1
        CQ, CO = WOUT + 4, WOUT + 5
        pslot = ring[:, POOLW % 2, :]
        pw = pslot[:, 0:10 * PC].rearrange("p (c d) -> p c d", c=10)
        poolT = pslot[:, 3200:3200 + 10 * TOK].rearrange("p (c t) -> p c t", c=10)
        state = pslot[:, 5840:5840 + PW]
        poolc = z[:, 0, 0:2 * AW]
        poolA = poolc[:, 0:1024].rearrange("p (g t) -> p g t", g=PG)
        poolB = poolc[:, 1024:1536].rearrange("p (g t) -> p g t", g=PG)
        prb = z[:, 1, 0:768].rearrange("p (b j) -> p b j", b=2)
        prT = z[:, 1, 768:1536].rearrange("p (b j) -> p b j", b=2)
        h_flat = hT[:].rearrange("p k t -> p (k t)")
        KVB = 3
        kvb = [r[:, lo:lo + 3 * AW].rearrange("p (t n) -> p t n", t=3)
               for r, lo in ((h_flat, 0), (h_flat, 3 * AW), (qkt_flat, 0))]
        zero_row = s_in[:].rearrange("p a b c -> p (a b c)")[:, 0:512]
        norm_dump = h_flat[:, 0:D]
        mask = after_mix[:, 0:AW]
        masked = after_mix[:, AW:2 * AW]
        memr = zf[:, 0:2 * D].rearrange("p (t n) -> p t n", t=2)
        msq = zf[:, 2 * D:2 * D + XW]
        mk = z[:, 2, IN_W - 4 * XW:IN_W - 2 * XW].rearrange("p (t n) -> p t n", t=2)
        mv = z[:, 2, IN_W - 2 * XW:IN_W].rearrange("p (t n) -> p t n", t=2)
        xq = zf[:, 0:3 * XW].rearrange("p (t n) -> p t n", t=3)
        xqT = zf[:, 1536:1536 + XH * SEQ].rearrange("p (h t) -> p h t", h=XH)
        xsq = zf[:, 2560:2560 + XW]
        oT = slot2[:, 0:XH * TC].rearrange("p (h t) -> p h t", h=XH)
        xprb = slot2[:, 1152:2176].rearrange("p (b j) -> p b j", b=2)
        xprT = slot2[:, 2176:3200].rearrange("p (b j) -> p b j", b=2)
        xkv = [zf[:, lo:lo + 2 * XW].rearrange("p (t n) -> p t n", t=2) for lo in (3072, 4096, 5120, 7168, 8192)]
        XKVB = len(xkv)
        xmask = after_mix[:, 2048:2560]
        xmasked = after_mix[:, 2560:3072]
        xn = zf[:, 0:3 * D].rearrange("p (t n) -> p t n", t=3)
        M0 = 3 * D
        ffn_dump = zf[:, M0 + 900:M0 + 900 + D]
        wr = zf[:, M0:M0 + KT * 36].rearrange("p (k n) -> p k n", k=KT)
        b36 = zf[0:36, M0 + 576:M0 + 577]
        LT = zf[0:36, M0 + 580:M0 + 580 + TOK]
        rt = zf[:, M0 + 900:M0 + 900 + 1600]
        xe = zf[:, M0 + 2560:M0 + 3072]
        XT = zf[:, M0 + 3072:M0 + 3584].rearrange("p (j s) -> p j s", j=4)
        ge, gd, gr, hid, aT = (zf[:, M0 + 3584 + 128 * i:M0 + 3712 + 128 * i] for i in range(5))
        yo = rt[:, 0:512]
        ones = ge

        pb = [ctx.enter_context(nc.psum_tensor(f"pb{i}", [P, 512], F32)) for i in range(8)]
        VB, AB = pb[0:4], pb[4:8]

        const_landed, x_landed = sem("const_landed"), sem("x_landed")
        w_landed = [sem("w_landed0"), sem("w_landed1")]
        v_filled, v_freed = sem("v_filled"), sem("v_freed")
        a_filled, a_freed = sem("a_filled"), sem("a_freed")
        dve_seq = sem("dve_seq")
        squared, mean_ready, root_ready, diag_ready = sem("squared"), sem("mean_ready"), sem("root_ready"), sem("diag_ready")
        zeros_ready, pads_ready = sem("zeros_ready"), sem("pads_ready")
        xs_zeroed = sem("xs_zeroed")
        brow_stored, bias_landed = sem("brow_stored"), sem("bias_landed")
        qk_normed, mk_normed, xq_normed = sem("qk_normed"), sem("mk_normed"), sem("xq_normed")
        keys_stored, rows_stored, stored = sem("keys_stored"), sem("rows_stored"), sem("stored")
        copied = sem("copied")
        biased, exped, probs_ready = sem("biased"), sem("exped"), sem("probs_ready")
        poolc_landed, state_landed = sem("poolc_landed"), sem("state_landed")
        kv_landed = [sem(f"kv_landed{i}") for i in range(KVB)]
        xkv_landed = [sem(f"xkv_landed{i}") for i in range(XKVB)]
        keys_used, vals_used = sem("keys_used"), sem("vals_used")
        s_biased, s_exped, s_probs = sem("s_biased"), sem("s_exped"), sem("s_probs")
        mask_landed = sem("mask_landed")
        mem_landed, mem_stored, mv_landed = sem("mem_landed"), sem("mem_stored"), sem("mv_landed")
        router_landed = sem("router_landed")
        xn_ready, exp_in, exp_out = sem("xn_ready"), sem("exp_in"), sem("exp_out")
        pairs_ready, over_cols_ready = sem("pairs_ready"), sem("over_cols_ready")
        slots_ready, scattered = sem("slots_ready"), sem("scattered")
        xe_landed = sem("xe_landed")
        gu_landed, gu_used = [sem("gu_landed0"), sem("gu_landed1")], [sem("gu_used0"), sem("gu_used1")]
        dn_landed, dn_used = sem("dn_landed"), sem("dn_used")
        xt_filled, xt_ready = sem("xt_filled"), sem("xt_ready")
        gate_exp, hid_seq, hid_ready = sem("gate_exp"), sem("hid_seq"), sem("hid_ready")
        hidT_filled, hidT_ready = sem("hidT_filled"), sem("hidT_ready")
        y_ready, y_stored = sem("y_ready"), sem("y_stored")
        y_gathered = [sem(f"y_gathered{i}") for i in range(6)]
        x_final = sem("x_final")

        cdr = a["const"]

        def cc(name, p=P):
            lo, hi = CONST_AT[name]
            return cdr[0:p, lo:hi]

        def wk(i):
            return ring[:, i % 2, :].rearrange("p (k n) -> p k n", k=KT)

        def piece_landed(eng, i):
            n = i // 2 + 1
            if i % 2 == POOLW % 2 and i >= POOLW:
                n += POOL_DMAS - 1
            eng.wait_ge(w_landed[i % 2], 16 * n)

        POOL_DMAS = 4
        FLIPS = H * SEQ // 512
        A_MEM = 4
        A_QKT = A_MEM + 2 * NCH + 6
        A_ATT = A_QKT + 2 * H
        A_DEC = A_ATT + 20 + 4
        A_XQT = A_DEC + 2 + 2
        V_MK = 2 + 8 + 1
        V_PRE = V_MK + 1 + 12
        V_IN = V_PRE + NCH + FLIPS
        V_WOUT = V_IN + H + 2 * NB + 2 + 4 + 12
        V_CQ = V_WOUT + 12 + 1
        V_CO = V_CQ + XH + NB + 2 + 2 + 12
        N_CONST = 22

        def piece_used(eng, i):
            if i < IN0:
                eng.wait_ge(v_filled, V_MK + i)
            elif i < POOLW:
                eng.wait_ge(v_filled, V_PRE + i - IN0 + 1 + (FLIPS if i - IN0 > 1 else 0))
            elif i == POOLW:
                eng.wait_ge(a_filled, A_ATT + 20)
            elif i < CQ:
                eng.wait_ge(v_filled, V_WOUT - 12 + 3 * (i - WOUT + 1))
            else:
                eng.wait_ge(v_filled, {CQ: V_CQ, CO: V_CO}[i])

        def kv_ready(eng, j):
            eng.wait_ge(kv_landed[j % KVB], 64 * (j // KVB + 1))

        def xkv_ready(eng, j):
            eng.wait_ge(xkv_landed[j % XKVB], 16 * (j // XKVB + 1))

        def turn_job(h):
            return 0 if h == 0 else 2 * h - 1

        block = ctx.enter_context(nc.Block())

        @block.sync
        def _(sp):
            def big(i):
                if i >= 2:
                    piece_used(sp, i - 2)
                done = w_landed[i % 2]
                if IN0 <= i < POOLW:
                    n = i - IN0
                    src = a["w_in"][0][:, 512 * n:512 * n + 512].rearrange("(p k) n -> p k n", k=KT)
                elif i == POOLW:
                    g2 = a["pool_w"][0]
                    for c in range(2):
                        sp.dma_start(pw[:, 0:8, :].rearrange("p (g c) d -> p g c d", c=2)[:, :, c],
                                     g2[:, c * P:c * P + P, :].rearrange("g p d -> p g d")).then_inc(done, 16)
                    for o in range(2):
                        sp.dma_start(pw[64 * o:64 * o + 64, 8:10, :],
                                     g2[o:PG:2, 2 * P:PC, :].rearrange("g p d -> p g d")).then_inc(done, 16)
                    return
                elif WOUT <= i < CQ:
                    n = i - WOUT
                    src = a["w_out"][0][:, 512 * n:512 * n + 512].rearrange("(k p) n -> p k n", p=P)
                elif i < CO:
                    w = {CK: "w_ck", CV: "w_cv", CQ: "w_cq"}[i]
                    src = a[w][0].rearrange("(p k) n -> p k n", k=KT)
                else:
                    src = a["w_co"][0].rearrange("(k p) n -> p k n", p=P)
                    sp.dma_start(ring[:, i % 2, :].rearrange("p (k n) -> p k n", k=XH), src).then_inc(done, 16)
                    return
                sp.dma_start(wk(i), src).then_inc(done, 16)

            sp.dma_start(memr, a["mem_prompt"][0].rearrange("(t p) n -> p t n", p=P)).then_inc(mem_landed, 16)
            sp.dma_start(x3[:, 0:2, :], a["x_prompt"][0].rearrange("(t p) n -> p t n", p=P)).then_inc(x_landed, 16)
            sp.wait_ge(zeros_ready, 1)
            sp.dma_start(x3[0:NB, 2, :], a["x_sample"][:, 0]).then_inc(x_landed, 16)
            for dst, src in ((ident[:], cc("ident")), (rb[0:NBUCKET], a["rel_bias"]),
                             (ohp[0:33], cc("ohp", 33)), (ohs[0:33], cc("ohs", 33)),
                             (tri[:], cc("tri")), (flip, cc("flip")), (moec[:], cc("moe")),
                             (poolsc[:].rearrange("p a g b -> p (a g b)"), cc("pools")), (sel[:], cc("sel"))):
                sp.dma_start(dst, src).then_inc(const_landed, 16)
            for i in range(4):
                sp.dma_start(rbs[0:NBUCKET, i, 0:H], a["rel_bias"]).then_inc(const_landed, 16)
            big(0)
            for i, g in enumerate(("norm_mix_g", "norm_mem_g", "norm_cross_g", "norm_ffn_g")):
                sp.dma_start(gT[:, i, :], a[g][0].rearrange("(p k) -> p k", k=KT)).then_inc(const_landed, 16)
            for i, g in enumerate(("q_norm_g", "k_norm_g")):
                sp.dma_start(gqk[:, i, :], a[g].to_broadcast([P, HD])).then_inc(const_landed, 16)
            for i, g in enumerate(("cq_norm_g", "ck_norm_g")):
                sp.dma_start(gxx[:, i, :], a[g].to_broadcast([P, XD])).then_inc(const_landed, 16)
            with nc.allow_non_contiguous_dma(reason="1280 scale values, one per partition"):
                sp.dma_start(psc[:], a["pool_scale"][0].rearrange("(k p) -> p k", p=P)).then_inc(const_landed, 16)
            big(1)
            sp.wait_ge(v_freed, 2)
            sp.dma_start(bias_dram[:, :], brow[0:H, :]).then_inc(brow_stored, 16)
            sp.wait_ge(brow_stored, 16)
            sp.dma_start(hankel.rearrange("p (h j) -> p h j", h=H),
                         bass.AP(tensor=bias_dram.tensor, offset=0, ap=[[1, P], [384, H], [1, SEQ]]))\
                .then_inc(bias_landed, 16)
            big(IN0)
            sp.wait_ge(mk_normed, 3)
            sp.dma_start(a["mem_k_prompt"][0, 0].rearrange("(t p) h e -> p t (h e)", p=P), mk).then_inc(mem_stored, 16)
            sp.dma_start(a["mem_v_prompt"][0, 0].rearrange("(t p) h e -> p t (h e)", p=P), mv).then_inc(mem_stored, 16)
            for i in range(IN0 + 1, IN0 + 6):
                big(i)
            sp.wait_ge(qk_normed, 3)
            for dst, src in ((a["win_k_prompt"][0, 0].rearrange("(t p) h e -> p t (h e)", p=P), z[:, 0:2, AW:2 * AW]),
                             (a["win_k_sample"][0, :, WB - 1].rearrange("b h e -> b (h e)"), z[0:NB, 2, AW:2 * AW])):
                sp.dma_start(dst, src).then_inc(keys_stored, 16)
            for i in range(IN0 + 6, POOLW + 1):
                big(i)
            piece_used(sp, POOLW - 2)
            sp.dma_start(state[0:NB * HIST, :], a["state_pool"][0].rearrange("b s n -> (b s) n")).then_inc(state_landed, 16)
            sp.wait_ge(a_freed, A_MEM + 2 * NCH)
            sp.wait_ge(v_freed, V_IN)
            for dst, src in ((a["win_v_prompt"][0, 0].rearrange("(t p) h e -> p t (h e)", p=P), z[:, 0:2, 2 * AW:3 * AW]),
                             (a["win_v_sample"][0, :, WB - 1].rearrange("b h e -> b (h e)"), z[0:NB, 2, 2 * AW:3 * AW]),
                             (a["pool_prompt"][0, 0], z[P - HIST:P, 1, 3 * AW:IN_W]),
                             (a["pool_sample"][0, :, HIST - 1], z[0:NB, 2, 3 * AW:IN_W])):
                sp.dma_start(dst, src).then_inc(rows_stored, 16)
            sp.wait_ge(keys_stored, 2 * 16)
            sp.wait_ge(a_freed, A_QKT)
            sp.dma_start(poolc, cc("pool")).then_inc(poolc_landed, 16)
            for i in range(WOUT, CO + 1):
                big(i)
                if i == WOUT + 2:
                    sp.wait_ge(mem_stored, 2 * 16)
                    sp.dma_start(mv, a["mem_v_prompt"][0, 0].rearrange("(t p) h e -> p t (h e)", p=P)).then_inc(mv_landed, 16)
                    for w, lo, n in (("w_rg", 0, NG), ("w_re", NG, NE)):
                        sp.dma_start(wr[:, :, lo:lo + n], a[w][0].rearrange("(p k) n -> p k n", k=KT)).then_inc(router_landed, 16)
                    for w, lo, n in (("b_rg", 0, NG), ("b_re", NG, NE)):
                        sp.dma_start(b36[lo:lo + n, :], a[w][0].rearrange("(n o) -> n o", o=1)).then_inc(router_landed, 16)

            def expert_weights(i, e):
                first = isinstance(i, int)
                for half in range(2):
                    if first:
                        piece_used(sp, CQ + half)
                    else:
                        sp.wait_ge(gu_used[half], i)
                    for m, w in enumerate(("w_e_gate", "w_e_up")):
                        src = a[w][0][e] if first else a[w][0][bass.ds(e, 1)].rearrange("o k n -> (o k) n")
                        sp.dma_start(ring[:, half, 4096 * m:4096 * m + 4096].rearrange("p (k n) -> p k n", k=8),
                                     src.rearrange("(p k) n -> p k n", k=KT)[:, 8 * half:8 * half + 8, :])\
                            .then_inc(gu_landed[half], 16)
                if not first:
                    sp.wait_ge(dn_used, i)
                src = a["w_e_down"][0][e] if first else a["w_e_down"][0][bass.ds(e, 1)].rearrange("o k n -> (o k) n")
                sp.dma_start(slot2.rearrange("p (k n) -> p k n", k=4), src.rearrange("(k p) n -> p k n", p=P))\
                    .then_inc(dn_landed, 16)

            expert_weights(0, 0)
            with sp.Fori(1, NE) as i:
                expert_weights(i, i)
            sp.wait_ge(slots_ready, 1)
            n_over = sp.value_load(ov_i[0:1, OVB:OVB + 1], min_val=0, max_val=OVB)
            with sp.If(n_over > 0):
                with sp.Fori(NE, NBLK) as i:
                    expert_weights(i, sp.value_load(ov_i[0:1, bass.ds(i - NE, 1)], min_val=0, max_val=NE - 1))
            for t in range(3):
                sp.wait_ge(x_final, t + 1)
                if t < 2:
                    sp.dma_start(a["y_prompt"][0, t * P:(t + 1) * P, :], x3[:, t, :]).then_inc(stored, 16)
                else:
                    sp.dma_start(a["y_sample"][:, 0], x3[0:NB, 2, :]).then_inc(stored, 16)
            sp.wait_ge(stored, 3 * 16)
            sp.wait_ge(copied, (2 * NB + 1) * 16)
            sp.wait_ge(keys_stored, 2 * 16)
            sp.wait_ge(rows_stored, 4 * 16)
            sp.wait_ge(mem_stored, 2 * 16)

        @block.gpsimd
        def _(pool):
            pool.wait_ge(zeros_ready, 2)
            piece_used(pool, CK)
            pool.dma_start(xs_dram.rearrange("(p r) n -> p (r n)", p=P).rearrange("p (r n) -> p r n", n=512),
                           zero_row.unsqueeze(1).to_broadcast([P, NBLK * BLK // P * D // 512, 512])).then_inc(xs_zeroed, 16)

            def cache_copy(i):
                b, kv = i // 2, i % 2
                src = a[("cache_win_k", "cache_win_v")[kv]][0, b, 1:WB].rearrange("s h e -> (s h e)")
                dst = a[("win_k_sample", "win_v_sample")[kv]][0, b, 0:WB - 1].rearrange("s h e -> (s h e)")
                pool.dma_start(dst.rearrange("(p f) -> p f", p=96), src.rearrange("(p f) -> p f", p=96)).then_inc(copied, 16)

            for i in range(6):
                piece_used(pool, IN0 + i)
                cache_copy(i)
            for j in range(2 * NB):
                kv, b = j // NB, j % NB
                if j == 0:
                    pool.wait_ge(pads_ready, 1)
                if j == 2:
                    for i in range(6, 8):
                        cache_copy(i)
                    pool.wait_ge(pads_ready, 2)
                if j >= KVB:
                    if j - KVB < NB:
                        pool.wait_ge(keys_used, j - KVB + 1)
                    else:
                        pool.wait_ge(vals_used, j - KVB - NB + 1)
                if j == NB:
                    pool.wait_ge(biased, H)
                    pool.dma_start(mask, cc("mask")).then_inc(mask_landed, 16)
                if j == NB + 3:
                    cache_copy(8)
                t, landed, new = kvb[j % KVB], kv_landed[j % KVB], (1 + kv) * AW
                c = a[("cache_win_k", "cache_win_v")[kv]][0, b].rearrange("s h e -> s (h e)")
                pool.dma_start(t[:, 0], c[WB - P:WB]).then_inc(landed, 16)
                pool.dma_start(t[0:96, 1], c[WB - 512:WB - P].rearrange("(r q) n -> r q n", q=4)[:, 0]).then_inc(landed, 16)
                pool.dma_start(t[0:96, 2], c[0:1536].rearrange("(r q) n -> r q n", q=16)[:, 0]).then_inc(landed, 16)
                pool.dma_start(t[96:97, 1], z[b:b + 1, 2, new:new + AW]).then_inc(landed, 16)
            pool.dma_start(a["pool_sample"][0, :, 0:HIST - 1], a["state_pool"][0, :, 1:HIST]).then_inc(copied, 16)
            pool.wait_ge(a_freed, A_DEC)
            pool.dma_start(xmask, cc("xmask")).then_inc(mask_landed, 16)
            cache_copy(9)
            piece_used(pool, WOUT)
            for j in range(2 * NB):
                kv, b = j // NB, j % NB
                if j == XKVB:
                    for i in range(10, 14):
                        piece_used(pool, WOUT + i - 9)
                        cache_copy(i)
                if j >= XKVB:
                    if j - XKVB < NB:
                        pool.wait_ge(keys_used, NB + j - XKVB + 1)
                    else:
                        pool.wait_ge(vals_used, j - XKVB + 1)
                c = a[("cache_mem_k", "cache_mem_v")[kv]][0, b].rearrange("(t p) h e -> p t (h e)", p=P)
                pool.dma_start(xkv[j % XKVB], c).then_inc(xkv_landed[j % XKVB], 16)
            for i in range(14, 16):
                cache_copy(i)
            pool.wait_ge(xs_zeroed, 16)
            pool.wait_ge(xn_ready, 3)
            pool.wait_ge(slots_ready, 1)
            for s in range(2):
                for t in range(3):
                    n = P if t < 2 else NB
                    pool.indirect_dma_start(xs_dram[:, :], bass.IndirectOffsetOnAxis(ap=slot_i[0:n, s, t:t + 1], axis=0),
                                            xn[0:n, t, :], None).then_inc(scattered, 16)
            pool.wait_ge(scattered, 6 * 16)

            def block_rows(i):
                if not isinstance(i, int):
                    pool.wait_ge(xt_filled, i)
                rows = xs_dram[0:BLK] if isinstance(i, int) else xs_dram[bass.ds(i * BLK, BLK)]
                for c in range(4):
                    pool.dma_start(xe[32 * c:32 * c + 32, :], rows[:, 512 * c:512 * c + 512]).then_inc(xe_landed, 16)

            def gather_results(blocks):
                pool.wait_ge(y_stored, 64 * blocks)
                pool.wait_ge(dn_used, blocks)
                for t in range(3):
                    for s in range(2):
                        n = P if t < 2 else NB
                        j = 2 * t + s
                        pool.indirect_dma_start(ring[0:n, j // 4, (j % 4) * D:(j % 4 + 1) * D], None,
                                                ys_dram[0:BLK * blocks, :],
                                                bass.IndirectOffsetOnAxis(ap=slot_i[0:n, s, t:t + 1], axis=0))\
                            .then_inc(y_gathered[j], 16)

            block_rows(0)
            with pool.Fori(1, NE) as i:
                block_rows(i)
            n_over = pool.value_load(ov_i[0:1, OVB:OVB + 1], min_val=0, max_val=OVB)
            with pool.If(n_over > 0):
                with pool.Fori(NE, NBLK) as i:
                    block_rows(i)
                gather_results(NBLK)
            with pool.Else():
                gather_results(NE)

        @block.tensor
        def _(pe):
            nv = na = nd = 0
            mm = nc.tensor.matmul

            def vbank():
                nonlocal nv
                if nv >= 4:
                    pe.wait_ge(v_freed, nv - 3)
                nv += 1
                return VB[(nv - 1) % 4]

            def abank():
                nonlocal na
                if na >= 4:
                    pe.wait_ge(a_freed, na - 3)
                na += 1
                return AB[(na - 1) % 4]

            def all_emptied():
                pe.wait_ge(v_freed, nv)
                pe.wait_ge(a_freed, na)

            def norm_turn(rows, tiles):
                nonlocal nd
                nd += 1
                pe.wait_ge(diag_ready, nd)
                for t in range(tiles):
                    cols = rows[:, t, :].rearrange("p (m k) -> p k m", k=KT)
                    for j in range(4):
                        bk = vbank()
                        for k in range(4):
                            last = mm(bk[:, P * k:P * k + P], cols[:, 4 * j + k, :], dg[:, t, :], start=True, stop=True)
                        last.then_inc(v_filled, 1)

            def project(xT, w, nk, tile, bk, filled):
                for k in range(nk):
                    last = mm(bk[:, :], xT[:, k, tile * P:tile * P + P], w[:, k, :], start=(k == 0), stop=(k == nk - 1))
                last.then_inc(filled, 1)

            def project_sample(xT, w, nk, bk, filled):
                for k in range(nk):
                    for c in range(4):
                        last = mm(bk[32 * c:32 * c + 32, 0:P], xT[:, k, SEQ:TC], w[:, k, P * c:P * c + P],
                                  start=(k == 0), stop=(k == nk - 1))
                last.then_inc(filled, 1)

            pe.wait_ge(const_landed, 16 * N_CONST)
            pe.wait_ge(zeros_ready, 2)
            bk = vbank()
            mm(bk[0:H, 0:384], rb[0:33], ohp[0:33, :], start=True, stop=True).then_inc(v_filled, 1)
            bk = vbank()
            mm(bk[:, 0:NDEC], rbs[0:33].rearrange("p i h -> p (i h)"), ohs[0:33, :], start=True, stop=True)\
                .then_inc(v_filled, 1)
            norm_turn(memr, 2)
            all_emptied()
            for i in (CK, CV):
                piece_landed(pe, i)
                project(hmT, wk(i), KT, 0, abank(), a_filled)
                project(hmT, wk(i), KT, 1, vbank(), v_filled)
            norm_turn(x3, 3)
            pe.wait_ge(mk_normed, 2)
            for pair in range(2):
                bk = abank()
                for j in range(2):
                    for t in range(2):
                        last = nc.tensor.transpose(bk[:, P * (2 * j + t):P * (2 * j + t) + P],
                                                   mk[:, t, P * (2 * pair + j):P * (2 * pair + j) + P], ident[:])
                last.then_inc(a_filled, 1)
            all_emptied()
            for n in range(NCH):
                i = IN0 + n
                piece_landed(pe, i)
                project(hT, wk(i), KT, 0, abank(), a_filled)
                project_sample(hT, wk(i), KT, abank(), a_filled)
                project(hT, wk(i), KT, 1, vbank(), v_filled)
                if n == 1:
                    pe.wait_ge(bias_landed, 16)
                    for f in range(FLIPS):
                        mm(vbank()[:, :], flip, hankel[:, 512 * f:512 * f + 512], start=True, stop=True)\
                            .then_inc(v_filled, 1)
            pe.wait_ge(qk_normed, 3)
            for s in range(2):
                for pair in range(0, H // 2, 2):
                    bk = abank()
                    for j in range(2):
                        for t in range(2):
                            last = nc.tensor.transpose(bk[:, P * (2 * j + t):P * (2 * j + t) + P],
                                                       z[:, t, s * AW + P * (pair + j):s * AW + P * (pair + j) + P], ident[:])
                    last.then_inc(a_filled, 1)
            all_emptied()

            def attend(nh, score, turn, value):
                nonlocal probs_seen
                for s in range(nh + 2):
                    if s < nh:
                        score(s)
                    if 1 <= s <= nh:
                        probs_seen += 1
                        pe.wait_ge(probs_ready, probs_seen)
                        turn(s - 1)
                    if s >= 2:
                        value(s - 2)

            probs_seen = 0
            turned = {}

            def score_win(h):
                r = slice(64 * (h % 2), 64 * (h % 2) + 64)
                bk = vbank()
                mm(bk[:, 0:P], qkT[r, 0, h // 2, 0:P], qkT[r, 1, h // 2, 0:P], start=True, stop=True)
                mm(bk[:, P:3 * P], qkT[r, 0, h // 2, P:SEQ], qkT[r, 1, h // 2, :], start=True, stop=True)\
                    .then_inc(v_filled, 1)

            def turn_win(h):
                bk = abank()
                for j in range(3):
                    last = nc.tensor.transpose(bk[:, P * j:P * j + P], prb[:, h % 2, P * j:P * j + P], ident[:])
                last.then_inc(a_filled, 1)
                turned[h] = na

            def value_win(h):
                pe.wait_ge(a_freed, turned[h])
                bk = abank()
                r = slice(64 * (h % 2), 64 * (h % 2) + 64)
                v = slice(2 * AW + HD * h, 2 * AW + HD * h + HD)
                mm(bk[r, 0:SEQ], z[:, 0, v], prT[:, h % 2, 0:SEQ], start=True, stop=False)
                mm(bk[r, P:SEQ], z[:, 1, v], prT[:, h % 2, SEQ:3 * P], start=False, stop=True).then_inc(a_filled, 1)

            attend(H, score_win, turn_win, value_win)

            def pool_channels(c):
                bk = abank()
                parts = [(c // 2, (c % 2) * P, P, 0)] if c < 8 else [(2 * (c - 8) + o, 2 * P, 64, 64 * o) for o in range(2)]
                for g, lo, n, r in parts:
                    u = slice(3 * AW + PC * g + lo, 3 * AW + PC * g + lo + n)
                    us = slice(PC * g + lo, PC * g + lo + n)
                    o = slice(r, r + n)
                    mm(bk[o, 0:SEQ], z[:, 0, u], poolA[:, g, :], start=True, stop=False)
                    mm(bk[o, P:SEQ], z[:, 1, u], poolB[:, g, :], start=False, stop=True)
                    mm(bk[o, SEQ:TOK], state[0:NB * HIST, us], poolsc[0:NB * HIST, 0, g, :], start=True, stop=False)
                    last = mm(bk[o, SEQ:TOK], z[0:NB, 2, u], poolsc[0:NB, 1, g, :], start=False, stop=True)
                last.then_inc(a_filled, 1)

            def pool_map(kt):
                bk = abank()
                lo = kt * P
                while lo < kt * P + P:
                    g = lo // PC
                    d = lo % PC
                    n = min(PC - d, kt * P + P - lo)
                    o = slice(lo - kt * P, lo - kt * P + n)
                    for c in range(3):
                        if c < 2:
                            w, x = pw[:, 2 * g + c, d:d + n], poolT[:, 2 * g + c, :]
                        else:
                            r = slice(64 * (g % 2), 64 * (g % 2) + 64)
                            w, x = pw[r, 8 + g // 2, d:d + n], poolT[r, 8 + g // 2, :]
                        last = mm(bk[o, 0:TOK], w, x, start=(c == 0), stop=(c == 2))
                    lo += n
                last.then_inc(a_filled, 1)

            def query_row(rows, lo, n, b):
                bk = vbank()
                mm(bk[:, 0:n], ident[0:NB, b:b + 1].to_broadcast([NB, P]), rows[0:NB, 2, lo:lo + n], start=True, stop=True)\
                    .then_inc(v_filled, 1)

            piece_landed(pe, POOLW)
            pe.wait_ge(state_landed, 16)
            pe.wait_ge(poolc_landed, 16)
            for b in range(NB):
                query_row(z, 0, 512, b)
                query_row(z, 512, 256, b)
                if b < 5:
                    pool_channels(2 * b)
                    pool_channels(2 * b + 1)
                if b == 5:
                    pe.wait_ge(a_freed, na)
                if b >= 5:
                    for kt in range(3 * (b - 5), 3 * (b - 5) + 3 + (b == 7)):
                        pool_map(kt)

            def sample_softmax(tiles, offs, base):
                pe.wait_ge(keys_used, NB * (base + 1))
                for hf in range(2):
                    bk = vbank()
                    for t, n in enumerate(tiles):
                        last = nc.tensor.transpose(bk[:, offs[t]:offs[t] + n], s_in[0:n, t, hf, :], ident[0:n, 0:n])
                    last.then_inc(v_filled, 1)
                for hf in range(2):
                    pe.wait_ge(s_probs, 2 * base + hf + 1)
                    bk = abank()
                    for t, n in enumerate(tiles):
                        last = nc.tensor.transpose(bk[0:n, P * t:P * t + P], psm[:, hf, offs[t]:offs[t] + n], ident[:])
                    last.then_inc(a_filled, 1)
                pe.wait_ge(a_freed, na)

            def sample_values(tiles, widths, buf, masked_rows, landed, ktiles):
                for hf in range(2):
                    banks = [vbank() for _ in widths]
                    for i in range(4):
                        b = 4 * hf + i
                        landed(pe, NB + b)
                        for bk, (lo, n) in zip(banks, widths):
                            for t, k in enumerate(tiles):
                                last = mm(bk[32 * i:32 * i + 32, 0:n], s_in[0:k, t, hf, 32 * i:32 * i + 32],
                                          buf[(NB + b) % len(buf)][0:k, t, lo:lo + n], start=(t == 0), stop=(t == len(tiles) - 1))
                        if i < 3:
                            last.then_inc(vals_used, 1)
                    last.then_inc(v_filled, len(banks))
                    pe.wait_ge(v_freed, nv)
                    bk = abank()
                    for k in range(ktiles):
                        last = mm(bk[:, 4 * k:4 * k + 4], masked_rows[:, P * k:P * k + P], sel[:], start=True, stop=True)
                        if k == 0:
                            last.then_inc(vals_used, 1)
                    last.then_inc(a_filled, 1)

            sample_softmax(DEC_ROWS, DEC_OFF, 0)
            sample_values(DEC_ROWS, ((0, 512), (512, 256)), kvb, masked, kv_ready, H // 2)
            all_emptied()

            for i in range(WOUT, WOUT + 4):
                piece_landed(pe, i)
                project(mixT, wk(i), KT, 0, vbank(), v_filled)
                project(mixT, wk(i), KT, 1, vbank(), v_filled)
                project_sample(mixT, wk(i), KT, vbank(), v_filled)
            norm_turn(x3, 3)
            all_emptied()
            piece_landed(pe, CQ)
            project(hT, wk(CQ), KT, 0, abank(), a_filled)
            project_sample(hT, wk(CQ), KT, abank(), a_filled)
            project(hT, wk(CQ), KT, 1, vbank(), v_filled)
            pe.wait_ge(xq_normed, 3)
            for pair in range(2):
                bk = abank()
                for j in range(2):
                    for t in range(2):
                        last = nc.tensor.transpose(bk[:, P * (2 * j + t):P * (2 * j + t) + P],
                                                   xq[:, t, P * (2 * pair + j):P * (2 * pair + j) + P], ident[:])
                last.then_inc(a_filled, 1)
            all_emptied()

            def score_mem(h):
                bk = vbank()
                for t in range(2):
                    last = mm(bk[:, NM * t:NM * t + NM], xqT[:, h, P * t:P * t + P], mkT[:, h, :], start=True, stop=True)
                last.then_inc(v_filled, 1)

            def turn_mem(h):
                bk = abank()
                for m in range(2):
                    for t in range(2):
                        last = nc.tensor.transpose(bk[:, SEQ * m + P * t:SEQ * m + P * t + P],
                                                   xprb[:, h % 2, NM * t + P * m:NM * t + P * m + P], ident[:])
                last.then_inc(a_filled, 1)
                turned[h] = na

            def value_mem(h):
                if h == 0:
                    pe.wait_ge(mv_landed, 16)
                pe.wait_ge(a_freed, turned[h])
                bk = abank()
                for m in range(2):
                    last = mm(bk[:, 0:SEQ], mv[:, m, XD * h:XD * h + XD], xprT[:, h % 2, SEQ * m:SEQ * m + SEQ],
                              start=(m == 0), stop=(m == 1))
                last.then_inc(a_filled, 1)

            attend(XH, score_mem, turn_mem, value_mem)
            for b in range(NB):
                query_row(xq, 0, XW, b)
            sample_softmax((P, P), (0, P), 1)
            sample_values((P, P), ((0, XW),), xkv, xmasked, xkv_ready, XH)
            all_emptied()
            piece_landed(pe, CO)
            wo = ring[:, CO % 2, :].rearrange("p (k n) -> p k n", k=XH)
            for n in range(4):
                w = wo[:, :, 512 * n:512 * n + 512]
                project(oT, w, XH, 0, vbank(), v_filled)
                project(oT, w, XH, 1, vbank(), v_filled)
                project_sample(oT, w, XH, vbank(), v_filled)

            norm_turn(x3, 3)
            all_emptied()
            pe.wait_ge(router_landed, 4 * 16)
            bk = vbank()
            for k in range(KT):
                last = mm(bk[0:36, 0:TOK], wr[:, k, :], hT[:, k, 0:TOK], start=(k == 0), stop=(k == KT - 1))
            last.then_inc(v_filled, 1)
            pe.wait_ge(v_freed, nv)
            bk = vbank()
            for t in range(3):
                n = P if t < 2 else NB
                last = nc.tensor.transpose(bk[0:n, 36 * t:36 * t + 36], LT[:, P * t:P * t + n], ident[0:36, 0:36])
            last.then_inc(v_filled, 1)
            pe.wait_ge(pairs_ready, 1)
            bk = vbank()
            pairs, before = rt[:, 0:96], rt[:, 96:224]
            mm(bk[:, 0:128], ones, before, start=True, stop=False)
            mm(bk[:, 0:96], tri[:], pairs, start=False, stop=True).then_inc(v_filled, 1)
            pe.wait_ge(over_cols_ready, 1)
            bk = vbank()
            mm(bk[:, 0:NE], ones[0:NE, :], rt[0:NE, 224:256], start=True, stop=True).then_inc(v_filled, 1)
            all_emptied()

            def expert(i):
                first = isinstance(i, int)
                pe.wait_ge(xe_landed, 64 * (i + 1))
                if not first:
                    pe.wait_ge(xt_ready, i)
                for j in range(4):
                    last = nc.tensor.transpose(pb[0][:, P * j:P * j + P], xe[:, P * j:P * j + P], ident[:])
                last.then_inc(xt_filled, 1)
                pe.wait_ge(xt_ready, i + 1)
                if not first:
                    pe.wait_ge(hid_ready, i)
                for half in range(2):
                    pe.wait_ge(gu_landed[half], 32 * (i + 1))
                    w = ring[:, half, :].rearrange("p (m k n) -> p m k n", m=2, k=8)
                    for k8 in range(8):
                        k = 8 * half + k8
                        for c in range(4):
                            last = mm(pb[1][32 * c:32 * c + 32, 0:256], XT[:, k % 4, 32 * (k // 4):32 * (k // 4) + 32],
                                      w[:, :, k8, P * c:P * c + P], start=(k == 0), stop=(k == KT - 1))
                    last.then_inc(gu_used[half], 1)
                pe.wait_ge(hid_ready, i + 1)
                if not first:
                    pe.wait_ge(hidT_ready, i)
                nc.tensor.transpose(pb[2][:, 0:P], hid, ident[:]).then_inc(hidT_filled, 1)
                pe.wait_ge(hidT_ready, i + 1)
                if not first:
                    pe.wait_ge(y_ready, i)
                pe.wait_ge(dn_landed, 16 * (i + 1))
                w = slot2.rearrange("p (k n) -> p k n", k=4)
                for f in range(4):
                    for c in range(4):
                        last = mm(pb[3][32 * c:32 * c + 32, :], aT[:, 32 * f:32 * f + 32], w[:, f, 512 * c:512 * c + 512],
                                  start=(f == 0), stop=(f == 3))
                last.then_inc(dn_used, 1)

            expert(0)
            with pe.Fori(1, NE) as i:
                expert(i)
            n_over = pe.value_load(ov_i[0:1, OVB:OVB + 1], min_val=0, max_val=OVB)
            with pe.If(n_over > 0):
                with pe.Fori(NE, NBLK) as i:
                    expert(i)

        @block.scalar
        def _(act):
            na = nroot = nsq = 0

            def filled():
                nonlocal na
                na += 1
                act.wait_ge(a_filled, na)
                return AB[(na - 1) % 4]

            def freed(ins):
                ins.then_inc(a_freed, 1)

            def norm_squares(rows, tiles, dump, col):
                nonlocal nroot, nsq
                for t in range(tiles):
                    if t:
                        act.wait_ge(squared, nsq)
                    nsq += 1
                    nc.scalar.activation(dump, rows[:, t, :], ACT.Square, accum_out=st[:, col + t:col + t + 1])\
                        .then_inc(squared, 1)
                roots(st[:, col + 3:col + 3 + tiles], st[:, col + 6:col + 6 + tiles])

            def roots(src, dst):
                nonlocal nroot
                nroot += 1
                act.wait_ge(mean_ready, nroot)
                nc.scalar.activation(dst, src, ACT.Sqrt).then_inc(root_ready, 1)

            def head_squares(rows, t, n, width, dump, heads):
                nonlocal nsq
                nsq += 1
                nc.scalar.activation(dump[0:n, 0:width], rows[0:n, t, 0:width], ACT.Square).then_inc(squared, 1)
                roots(st[0:n, 32:32 + heads], st[0:n, 64:64 + heads])

            def sample_rows(dst, bk, lo):
                for c in range(4):
                    last = nc.scalar.copy(dst[0:NB, 2, lo + P * c:lo + P * c + P], bk[32 * c:32 * c + NB, 0:P])
                freed(last)

            act.wait_ge(mem_landed, 16)
            norm_squares(memr, 2, norm_dump, 12)
            act.wait_ge(x_landed, 32)
            act.wait_ge(squared, nsq)
            norm_squares(x3, 3, norm_dump, 0)
            freed(nc.scalar.copy(mk[:, 0, :], filled()[:, :]))
            act.wait_ge(a_freed, na)
            act.wait_ge(v_freed, V_MK)
            for t in range(2):
                if t:
                    act.wait_ge(mk_normed, t)
                head_squares(mk, t, P, XW, msq, XH)
            freed(nc.scalar.copy(mv[:, 0, :], filled()[:, :]))
            for pair in range(2):
                freed(nc.scalar.copy(mkT[:, 2 * pair:2 * pair + 2, :].rearrange("p j t -> p (j t)"), filled()[:, :]))
            for n in range(NCH):
                if n == 3:
                    act.wait_ge(a_freed, na)
                    act.wait_ge(v_freed, V_PRE + 3 + FLIPS)
                    for t in range(3):
                        if t:
                            act.wait_ge(qk_normed, t)
                        head_squares(z, t, P if t < 2 else NB, 2 * AW, sq, 2 * H)
                    act.wait_ge(mem_stored, 2 * 16)
                freed(nc.scalar.copy(z[:, 0, 512 * n:512 * n + 512], filled()[:, :]))
                sample_rows(z, filled(), 512 * n)
            act.wait_ge(qk_normed, 3)
            for s in range(2):
                for pair in range(0, H // 2, 2):
                    freed(nc.scalar.copy(qkT[:, s, pair:pair + 2, :].rearrange("p j t -> p (j t)"), filled()[:, :]))

            heads_done = 0

            def attend(nh, parts, probs, turn, value):
                nonlocal heads_done
                for s in range(nh + 2):
                    if s < nh:
                        heads_done += 1
                        act.wait_ge(biased, heads_done)
                        q = 4 * (s % 2)
                        for j, (lo, hi) in enumerate(parts):
                            last = nc.scalar.activation(probs[:, s % 2, lo:hi], probs[:, s % 2, lo:hi], ACT.Exp,
                                                        bias=st[:, 96 + q + j:97 + q + j],
                                                        accum_out=st[:, 104 + q + j:105 + q + j])
                        last.then_inc(exped, 1)
                    if 1 <= s <= nh:
                        turn(s - 1)
                    if s >= 2:
                        value(s - 2)

            def value_win(h):
                r = slice(64 * (h % 2), 64 * (h % 2) + 64)
                freed(nc.scalar.copy(mixT[r, h // 2, 0:SEQ], filled()[r, 0:SEQ]))

            attend(H, ((0, P), (P, 3 * P)), prb, lambda h: freed(nc.scalar.copy(prT[:, h % 2, :], filled()[:, 0:384])),
                   value_win)

            def pool_channels(c):
                freed(nc.scalar.copy(poolT[:, c, :], filled()[:, 0:TOK]))

            def pool_map(kt):
                freed(nc.scalar.mul(mixT[:, 6 + kt, 0:TOK], filled()[:, 0:TOK], psc[:, kt:kt + 1]))

            for c in range(10):
                pool_channels(c)
            for kt in range(10):
                pool_map(kt)

            def sample_softmax(base, width, tiles):
                for hf in range(2):
                    act.wait_ge(s_biased, 2 * base + hf + 1)
                    nc.scalar.activation(psm[:, hf, 0:width], psm[:, hf, 0:width], ACT.Exp, bias=st[:, 112 + hf:113 + hf],
                                         accum_out=st[:, 114 + hf:115 + hf]).then_inc(s_exped, 1)
                for hf in range(2):
                    bk = filled()
                    for t, n in enumerate(tiles):
                        last = nc.scalar.copy(s_in[0:n, t, hf, :], bk[0:n, P * t:P * t + P])
                    freed(last)

            def sample_out(dst, kts):
                for hf in range(2):
                    bk = filled()
                    freed(nc.scalar.copy(dst[:, 0:kts, SEQ + 4 * hf:SEQ + 4 * hf + 4],
                                         bk[:, 0:4 * kts].rearrange("p (k b) -> p k b", b=4)))

            sample_softmax(0, NDEC, DEC_ROWS)
            sample_out(mixT, H // 2)
            act.wait_ge(v_freed, V_WOUT)
            norm_squares(x3, 3, zf[:, 0:D], 0)
            act.wait_ge(squared, nsq)
            freed(nc.scalar.copy(xq[:, 0, :], filled()[:, :]))
            sample_rows(xq, filled(), 0)
            act.wait_ge(a_freed, na)
            act.wait_ge(v_freed, V_CQ)
            for t in range(3):
                if t:
                    act.wait_ge(xq_normed, t)
                head_squares(xq, t, P if t < 2 else NB, XW, xsq, XH)
            act.wait_ge(xq_normed, 3)
            for pair in range(2):
                freed(nc.scalar.copy(xqT[:, 2 * pair:2 * pair + 2, :].rearrange("p j t -> p (j t)"), filled()[:, :]))
            attend(XH, ((0, NM), (NM, 2 * NM)), xprb, lambda h: freed(nc.scalar.copy(xprT[:, h % 2, :], filled()[:, :])),
                   lambda h: freed(nc.scalar.copy(oT[:, h, 0:SEQ], filled()[:, 0:SEQ])))
            sample_softmax(1, NM, (P, P))
            sample_out(oT, XH)
            act.wait_ge(v_freed, V_CO)
            norm_squares(x3, 3, ffn_dump, 0)
            act.wait_ge(exp_in, 1)
            nc.scalar.activation(rt[:, 1300:1312], rt[:, 1300:1312], ACT.Exp).then_inc(exp_out, 1)
            act.wait_ge(exp_in, 2)
            nc.scalar.activation(rt[:, 1312:1315], rt[:, 1312:1315], ACT.Exp).then_inc(exp_out, 1)

            def expert(i):
                first = isinstance(i, int)
                act.wait_ge(gu_used[1], i + 1)
                nc.scalar.activation(ge, pb[1][:, 0:P], ACT.Exp, scale=-1.0).then_inc(gate_exp, 1)
                act.wait_ge(hidT_filled, i + 1)
                nc.scalar.copy(aT, pb[2][:, 0:P]).then_inc(hidT_ready, 1)
                act.wait_ge(dn_used, i + 1)
                if not first:
                    act.wait_ge(y_stored, 64 * i)
                nc.scalar.copy(yo, pb[3][:, :]).then_inc(y_ready, 1)
                act.wait_ge(y_ready, i + 1)
                rows = ys_dram[0:BLK] if first else ys_dram[bass.ds(i * BLK, BLK)]
                for c in range(4):
                    act.dma_start(rows[:, 512 * c:512 * c + 512], yo[32 * c:32 * c + 32, :]).then_inc(y_stored, 16)

            expert(0)
            with act.Fori(1, NE) as i:
                expert(i)
            n_over = act.value_load(ov_i[0:1, OVB:OVB + 1], min_val=0, max_val=OVB)
            with act.If(n_over > 0):
                with act.Fori(NE, NBLK) as i:
                    expert(i)

        @block.vector
        def _(dve):
            nv = nseq = nroot = nsq = 0
            V = nc.vector

            def filled():
                nonlocal nv
                nv += 1
                dve.wait_ge(v_filled, nv)
                return VB[(nv - 1) % 4]

            def link(ins):
                nonlocal nseq
                nseq += 1
                ins.then_inc(dve_seq, 1)
                dve.wait_ge(dve_seq, nseq)

            def mean_root(sums, mean, root, inv, n):
                nonlocal nroot
                V.tensor_scalar(mean, sums, 1.0 / n, EPS, ALU.mult, ALU.add).then_inc(mean_ready, 1)
                nroot += 1
                dve.wait_ge(root_ready, nroot)
                link(V.reciprocal(inv, root))

            def norm_scales(tiles, col=0):
                nonlocal nsq
                nsq += tiles
                dve.wait_ge(squared, nsq)
                mean_root(*(st[:, col + c:col + c + tiles] for c in (0, 3, 6, 9)), D)
                for t in range(tiles):
                    last = V.tensor_scalar(dg[:, t, :], ident[:], st[:, col + 9 + t:col + 10 + t], None, ALU.mult)
                last.then_inc(diag_ready, 1)

            def norm_rows(tiles, gain, dst):
                for t in range(tiles):
                    for j in range(4):
                        n = P if t < 2 else 32
                        src = filled()[:, :].rearrange("p (k m) -> p k m", k=4)[:, :, 0:n]
                        V.tensor_tensor(dst[:, 4 * j:4 * j + 4, P * t:P * t + n], src,
                                        gT[:, gain, 4 * j:4 * j + 4].unsqueeze(2).to_broadcast([P, 4, n]), ALU.mult)\
                            .then_inc(v_freed, 1)

            def head_norm(rows, t, n, heads, width, squares, gain, done):
                nonlocal nsq
                nsq += 1
                dve.wait_ge(squared, nsq)
                sm, mean, root, inv = (st[0:n, c:c + heads] for c in (128, 32, 64, 128))
                link(V.tensor_reduce(sm, squares[0:n, 0:heads * width].rearrange("p (h e) -> p h e", h=heads), AX.X, ALU.add))
                mean_root(sm, mean, root, inv, width)
                r3 = rows[0:n, t, 0:heads * width].rearrange("p (h e) -> p h e", h=heads)
                link(V.tensor_tensor(r3, r3, inv.unsqueeze(2).to_broadcast([n, heads, width]), ALU.mult))
                gs = [gain[0:n, g, :].unsqueeze(1) for g in (range(2) if heads == 2 * H else done[1])]
                per = heads // len(gs)
                for i, g in enumerate(gs):
                    part = r3[:, i * per:(i + 1) * per, :]
                    last = V.tensor_tensor(part, part, g.to_broadcast([n, per, width]), ALU.mult)
                last.then_inc(done[0], 1)

            V.memset(rbs[0:32].rearrange("p i h -> p (i h)"), 0.0)
            V.memset(x3[:, 2, :], 0.0).then_inc(zeros_ready, 1)
            V.memset(s_in[:].rearrange("p a b c -> p (a b c)"), 0.0)
            V.memset(rb[32:33], 1.0)
            link(V.memset(rbs[32:33].rearrange("p i h -> p (i h)"), 1.0))
            dve.nop().then_inc(zeros_ready, 1)
            dve.wait_ge(const_landed, 16 * N_CONST)
            V.tensor_copy(brow[0:H, :], filled()[0:H, 0:384]).then_inc(v_freed, 1)
            V.tensor_copy(biasS, filled()[:, 0:NDEC]).then_inc(v_freed, 1)
            norm_scales(2, 12)
            norm_rows(2, 1, hmT)
            norm_scales(3)
            V.tensor_copy(mk[:, 1, :], filled()[:, :]).then_inc(v_freed, 1)
            assert nv == V_MK
            dve.wait_ge(v_freed, nv)
            for t in range(2):
                head_norm(mk, t, P, XH, XD, msq, gxx, (mk_normed, (1,)))
            V.tensor_copy(mv[:, 1, :], filled()[:, :]).then_inc(v_freed, 1)
            dve.wait_ge(v_freed, nv)
            dve.wait_ge(a_freed, 2)
            dve.nop().then_inc(mk_normed, 1)
            norm_rows(3, 0, hT)
            assert nv == V_PRE
            for i in range(NCH):
                V.tensor_copy(z[:, 1, 512 * i:512 * i + 512], filled()[:, :]).then_inc(v_freed, 1)
                for n in range(FLIPS if i == 1 else 0):
                    V.tensor_copy(bias_flat[:, 512 * n:512 * n + 512], filled()[:, :]).then_inc(v_freed, 1)
                if i == 2:
                    dve.wait_ge(v_freed, nv)
                    dve.wait_ge(a_freed, A_MEM + 2 * 3)
                    for t in range(3):
                        head_norm(z, t, P if t < 2 else NB, 2 * H, HD, sq, gqk, (qk_normed, None))
            V.memset(mixT[:, :, TOK:TC], 0.0)
            piece_used(dve, POOLW - 1)
            V.memset(kvb[0][96:P, 1:3], 0.0)
            V.memset(kvb[1][96:P, 1:3], 0.0).then_inc(pads_ready, 1)

            heads_done = 0

            def attend(nh, parts, probs, enter, a_before):
                nonlocal heads_done
                for s in range(nh + 1):
                    if s < nh:
                        bk = filled()
                        if s >= 2:
                            dve.wait_ge(a_freed, a_before + turn_job(s - 2) + 1)
                        enter(s, bk)
                        dve.wait_ge(v_freed, nv)
                        q = 4 * (s % 2)
                        for j, (lo, hi) in enumerate(parts):
                            last = V.tensor_reduce(st[:, 116 + j:117 + j], probs[:, s % 2, lo:hi], AX.X, ALU.max)
                        link(last)
                        V.tensor_scalar(st[:, 96 + q:98 + q], st[:, 116:118], -1.0, None, ALU.mult).then_inc(biased, 1)
                    if s >= 1:
                        h = s - 1
                        heads_done += 1
                        dve.wait_ge(exped, heads_done)
                        q = 4 * (h % 2)
                        if heads_done > 1:
                            dve.wait_ge(probs_ready, heads_done - 1)
                        link(V.reciprocal(st[:, 118:120], st[:, 104 + q:106 + q]))
                        for j, (lo, hi) in enumerate(parts):
                            last = V.tensor_scalar(probs[:, h % 2, lo:hi], probs[:, h % 2, lo:hi], st[:, 118 + j:119 + j],
                                                   None, ALU.mult)
                        last.then_inc(probs_ready, 1)

            def enter_win(h, bk):
                V.scalar_tensor_tensor(out=prb[:, h % 2, 0:P], in0=bk[:, 0:P], scalar=HD ** -0.5, in1=bias[:, h, P:SEQ],
                                       op0=ALU.mult, op1=ALU.add)
                V.scalar_tensor_tensor(out=prb[:, h % 2, P:3 * P], in0=bk[:, P:3 * P], scalar=HD ** -0.5, in1=bias[:, h, :],
                                       op0=ALU.mult, op1=ALU.add).then_inc(v_freed, 1)

            dve.wait_ge(keys_stored, 2 * 16)
            dve.wait_ge(a_freed, A_QKT)
            attend(H, ((0, P), (P, 3 * P)), prb, enter_win, A_QKT)

            dve.wait_ge(a_freed, A_QKT + 2 * H)
            V.memset(kvb[2][96:P, 1:3], 0.0).then_inc(pads_ready, 1)
            dve.wait_ge(xs_zeroed, 16)

            def sample_scores(buf, tiles, widths, heads_of, landed, width):
                for b in range(NB):
                    landed(dve, b)
                    rows = buf[b % len(buf)]
                    hf, i = b // 4, b % 4
                    for (lo, n) in widths:
                        src = rows[:, :, lo:lo + n]
                        V.tensor_tensor(src, src, filled()[:, 0:n].unsqueeze(1).to_broadcast([P, tiles, n]), ALU.mult)\
                            .then_inc(v_freed, 1)
                    dve.wait_ge(v_freed, nv)
                    last = V.tensor_reduce(s_in[:, 0:tiles, hf, 32 * i:32 * i + heads_of],
                                           rows.rearrange("p t (h e) -> p t h e", e=width), AX.X, ALU.add)
                    last.then_inc(keys_used, 1)

            def sample_softmax(base, width, scale, rows):
                for hf in range(2):
                    bk = filled()
                    if rows is not None:
                        V.scalar_tensor_tensor(out=psm[:, hf, 0:width], in0=bk[:, 0:width], scalar=scale, in1=rows,
                                               op0=ALU.mult, op1=ALU.add).then_inc(v_freed, 1)
                    else:
                        V.tensor_scalar(psm[:, hf, 0:width], bk[:, 0:width], scale, None, ALU.mult).then_inc(v_freed, 1)
                    dve.wait_ge(v_freed, nv)
                    link(V.tensor_reduce(st[:, 120:121], psm[:, hf, 0:width], AX.X, ALU.max))
                    V.tensor_scalar(st[:, 112 + hf:113 + hf], st[:, 120:121], -1.0, None, ALU.mult).then_inc(s_biased, 1)
                for hf in range(2):
                    dve.wait_ge(s_exped, 2 * base + hf + 1)
                    link(V.reciprocal(st[:, 122 + hf:123 + hf], st[:, 114 + hf:115 + hf]))
                    V.tensor_scalar(psm[:, hf, 0:width], psm[:, hf, 0:width], st[:, 122 + hf:123 + hf], None, ALU.mult)\
                        .then_inc(s_probs, 1)

            def sample_mask(widths, out, m, a_before):
                for hf in range(2):
                    if hf:
                        dve.wait_ge(a_freed, a_before + 1)
                    for j, (lo, n) in enumerate(widths):
                        last = V.tensor_tensor(out[:, lo:lo + n], filled()[:, 0:n], m[:, lo:lo + n], ALU.mult)
                        last.then_inc(v_freed, 1)

            sample_scores(kvb, 3, ((0, 512), (512, 256)), H, kv_ready, HD)
            sample_softmax(0, NDEC, HD ** -0.5, biasS)
            dve.wait_ge(mask_landed, 16)
            sample_mask(((0, 512), (512, 256)), masked, mask, A_DEC - 2)

            def add_rows(n, p_rows):
                c = slice(512 * n, 512 * n + 512)
                for t in range(2):
                    V.tensor_tensor(x3[:, t, c], filled()[:, :], x3[:, t, c], ALU.add).then_inc(v_freed, 1)
                bk = filled()
                for j in range(4):
                    d = x3[0:NB, 2, 512 * n + P * j:512 * n + P * j + P]
                    last = V.tensor_tensor(d, bk[32 * j:32 * j + NB, 0:P], d, ALU.add)
                last.then_inc(v_freed, 1)

            for n in range(4):
                add_rows(n, None)
            dve.wait_ge(v_freed, nv)
            assert nv == V_WOUT
            V.memset(oT[:, :, TOK:TC], 0.0)
            norm_scales(3)
            norm_rows(3, 2, hT)
            V.tensor_copy(xq[:, 1, :], filled()[:, :]).then_inc(v_freed, 1)
            assert nv == V_CQ
            dve.wait_ge(v_freed, nv)
            for t in range(3):
                head_norm(xq, t, P if t < 2 else NB, XH, XD, xsq, gxx, (xq_normed, (0,)))
            attend(XH, ((0, NM), (NM, 2 * NM)), xprb,
                   lambda h, bk: V.tensor_scalar(xprb[:, h % 2, :], bk[:, :], XD ** -0.5, None, ALU.mult).then_inc(v_freed, 1),
                   A_XQT)
            sample_scores(xkv, 2, ((0, XW),), XH, xkv_ready, XD)
            sample_softmax(1, NM, XD ** -0.5, None)
            dve.wait_ge(mask_landed, 32)
            sample_mask(((0, XW),), xmasked, xmask, A_XQT + 2 * XH + 2)
            for n in range(4):
                add_rows(n, None)
            dve.wait_ge(v_freed, nv)
            assert nv == V_CO
            norm_scales(3)
            norm_rows(3, 3, hT)
            V.memset(ones, 1.0)
            for t in range(3):
                V.tensor_scalar(xn[:, t, :].rearrange("p (k m) -> p k m", k=KT), x3[:, t, :].rearrange("p (m k) -> p k m", k=KT),
                                st[:, 9 + t:10 + t], None, ALU.mult).then_inc(xn_ready, 1)
            dve.wait_ge(router_landed, 4 * 16)
            V.tensor_scalar(LT, filled()[0:36, 0:TOK], b36, None, ALU.add).then_inc(v_freed, 1)
            R = lambda lo, n: rt[:, lo:lo + 3 * n].rearrange("p (t n) -> p t n", t=3)
            L36 = R(260, 36)
            pen, le, eq, c1, oh1, oh2 = R(370, 4), R(384, NE), R(480, NE), R(576, NE), R(672, NE), R(768, NE)
            lg2, ohg, m1, m2, cm = R(1300, 4), R(864, 4), R(880, 1), R(884, 1), R(888, 1)
            gmax, gsum, pgrp = R(892, 1), R(896, 1), R(900, 1)
            slotE, cnt, xo, xinc, tmp, cmp = R(904, NE), rt[:, 1000:1032], rt[:, 1032:1064], rt[:, 1064:1096], R(1100, NE), rt[:, 1200:1232]
            desc = moec[:, 0:NE].unsqueeze(1).to_broadcast([P, 3, NE])
            base = moec[:, NE:2 * NE].unsqueeze(1).to_broadcast([P, 3, NE])
            valid = moec[:, 2 * NE:2 * NE + 3].unsqueeze(2).to_broadcast([P, 3, NE])
            TT = V.tensor_tensor

            def b(x, n):
                return x.to_broadcast([P, 3, n])

            link(V.memset(L36, 0.0))
            bk = filled()
            V.tensor_copy(L36[:, 0:2, :], bk[:, 0:72].rearrange("p (t n) -> p t n", t=2))
            link(V.tensor_copy(L36[0:NB, 2, :], bk[0:NB, 72:108]))
            dve.nop().then_inc(v_freed, 1)
            lg = L36[:, :, 0:NG]
            link(V.tensor_reduce(gmax, lg, AX.X, ALU.max))
            TT(lg2, lg, b(gmax, NG), ALU.subtract).then_inc(exp_in, 1)
            link(TT(ohg, lg, b(gmax, NG), ALU.is_equal))
            link(TT(ohg, ohg, moec[:, NE - NG:NE].unsqueeze(1).to_broadcast([P, 3, NG]), ALU.mult))
            link(V.tensor_reduce(cm, ohg, AX.X, ALU.max))
            link(TT(ohg, ohg, b(cm, NG), ALU.is_equal))
            link(V.tensor_scalar(pen, ohg, -NEG, NEG, ALU.mult, ALU.add))
            for t in range(3):
                last = TT(le[:, t, :].rearrange("p (g e) -> p g e", g=NG), L36[:, t, NG:36].rearrange("p (g e) -> p g e", g=NG),
                          pen[:, t, :].unsqueeze(2).to_broadcast([P, NG, EG]), ALU.add)
            link(last)

            def top(oh, m):
                link(V.tensor_reduce(m, le, AX.X, ALU.max))
                link(TT(eq, le, b(m, NE), ALU.is_equal))
                link(TT(c1, eq, desc, ALU.mult))
                link(V.tensor_reduce(cm, c1, AX.X, ALU.max))
                link(TT(oh, c1, b(cm, NE), ALU.is_equal))

            top(oh1, m1)
            link(V.scalar_tensor_tensor(out=le, in0=oh1, scalar=3 * NEG, in1=le, op0=ALU.mult, op1=ALU.add))
            top(oh2, m2)
            dve.wait_ge(exp_out, 1)
            link(V.tensor_reduce(gsum, lg2, AX.X, ALU.add))
            e2 = R(1312, 1)
            TT(e2, m2, m1, ALU.subtract).then_inc(exp_in, 1)
            pairs = R(0, NE)
            link(TT(c1, oh1, oh2, ALU.add))
            link(TT(pairs, c1, valid, ALU.mult))
            before = rt[:, 96:224]
            V.memset(before[:, 0:NE], 0.0)
            link(V.tensor_copy(before[:, NE:2 * NE], pairs[:, 0, :]))
            link(TT(before[:, 2 * NE:3 * NE], before[:, NE:2 * NE], pairs[:, 1, :], ALU.add))
            TT(before[:, 3 * NE:4 * NE], before[:, 2 * NE:3 * NE], pairs[:, 2, :], ALU.add).then_inc(pairs_ready, 1)
            dve.wait_ge(exp_out, 2)
            link(V.reciprocal(pgrp, gsum))
            link(V.tensor_scalar(m1, e2, 1.0, None, ALU.add))
            link(V.reciprocal(m2, m1))
            link(TT(gates[:, 0, :].unsqueeze(2), m2, pgrp, ALU.mult))
            link(TT(gates[:, 1, :].unsqueeze(2), gates[:, 0, :].unsqueeze(2), e2, ALU.mult))
            pos = filled()
            link(V.tensor_copy(cnt, pos[:, 96:128]))
            link(V.tensor_scalar(xo, cnt, float(BLK), None, ALU.is_gt))
            for j in range(2, -(-TOK // BLK)):
                link(V.scalar_tensor_tensor(out=xo, in0=cnt, scalar=float(BLK * j), in1=xo, op0=ALU.is_gt, op1=ALU.add))
            link(TT(tmp[0:NE, 0, :], xo[0:NE, :], ident[0:NE, 0:NE], ALU.mult))
            link(V.tensor_reduce(cm[0:NE, 0, :], tmp[0:NE, 0, :], AX.X, ALU.add))
            V.tensor_scalar(rt[0:NE, 224:256], tri[0:NE, 0:NE], cm[0:NE, 0, :], None, ALU.mult).then_inc(over_cols_ready, 1)
            xb = filled()
            link(V.tensor_scalar(cmp, xb[:, 0:NE], float(BLK), float(NE * BLK - BLK), ALU.mult, ALU.add))
            link(TT(cmp, cmp, moec[:, NE:2 * NE], ALU.subtract))
            p3 = pos[:, 0:96].rearrange("p (t n) -> p t n", t=3)
            link(V.tensor_scalar(tmp, p3, float(BLK), None, ALU.is_ge))
            link(TT(tmp, tmp, cmp.unsqueeze(1).to_broadcast([P, 3, NE]), ALU.mult))
            link(TT(tmp, tmp, base, ALU.add))
            link(TT(slotE, p3, tmp, ALU.add))
            for s, oh in enumerate((oh1, oh2)):
                link(TT(c1, oh, slotE, ALU.mult))
                link(V.tensor_reduce(cm, c1, AX.X, ALU.add))
                link(V.tensor_copy(slot_i[:, s, :], cm[:, :, 0]))
            link(TT(xinc, xb[:, 0:NE], xo, ALU.add))
            o3 = rt[0:1, 300:300 + OVB * NE].rearrange("p (o e) -> p o e", o=OVB)
            link(TT(o3, moec[0:1, 2 * NE + 3:2 * NE + 3 + OVB].unsqueeze(2).to_broadcast([1, OVB, NE]),
                    xinc[0:1, :].unsqueeze(1).to_broadcast([1, OVB, NE]), ALU.is_ge))
            link(V.tensor_reduce(rt[0:1, 1400:1400 + OVB], o3, AX.X, ALU.add))
            link(V.tensor_scalar(rt[0:1, 1400:1400 + OVB], rt[0:1, 1400:1400 + OVB], float(NE - 1), None, ALU.min))
            V.tensor_copy(ov_i[0:1, 0:OVB], rt[0:1, 1400:1400 + OVB])
            link(V.tensor_copy(ov_i[0:1, OVB:OVB + 1], xinc[0:1, NE - 1:NE]))
            dve.nop().then_inc(v_freed, 2)
            dve.nop().then_inc(slots_ready, 1)

            def expert(i):
                first = isinstance(i, int)
                dve.wait_ge(xt_filled, i + 1)
                if not first:
                    dve.wait_ge(gu_used[1], i)
                V.tensor_tensor(XT.rearrange("p j (c s) -> p j c s", c=4), pb[0][:, :].rearrange("p (j c s) -> p j c s", j=4, c=4),
                                gT[:, 3, :].rearrange("p (c j) -> p j c", j=4).unsqueeze(3).to_broadcast([P, 4, 4, 32]),
                                ALU.mult).then_inc(xt_ready, 1)
                dve.wait_ge(gate_exp, i + 1)
                V.tensor_scalar(gd, ge, 1.0, None, ALU.add).then_inc(hid_seq, 1)
                dve.wait_ge(hid_seq, 3 * i + 1)
                V.reciprocal(gr, gd).then_inc(hid_seq, 1)
                dve.wait_ge(hid_seq, 3 * i + 2)
                V.tensor_tensor(gd, pb[1][:, 0:P], gr, ALU.mult).then_inc(hid_seq, 1)
                dve.wait_ge(hid_seq, 3 * i + 3)
                V.tensor_tensor(hid, pb[1][:, P:2 * P], gd, ALU.mult).then_inc(hid_ready, 1)

            expert(0)
            with dve.Fori(1, NE) as i:
                expert(i)
            n_over = dve.value_load(ov_i[0:1, OVB:OVB + 1], min_val=0, max_val=OVB)
            with dve.If(n_over > 0):
                with dve.Fori(NE, NBLK) as i:
                    expert(i)
            for t in range(3):
                n = P if t < 2 else NB
                for s in range(2):
                    j = 2 * t + s
                    dve.wait_ge(y_gathered[j], 16)
                    ins = V.scalar_tensor_tensor(out=x3[0:n, t, :], in0=ring[0:n, j // 4, (j % 4) * D:(j % 4 + 1) * D],
                                                 scalar=gates[0:n, s, t:t + 1], in1=x3[0:n, t, :], op0=ALU.mult, op1=ALU.add)
                    if s == 0:
                        link(ins)
                    else:
                        ins.then_inc(x_final, 1)


_INS = ['x_prompt', 'x_sample', 'cache_win_k', 'cache_win_v', 'state_pool', 'cache_mem_k', 'cache_mem_v', 'mem_prompt',
        'rel_bias', 'norm_mix_g', 'w_in', 'q_norm_g', 'k_norm_g', 'pool_w', 'pool_scale', 'w_out', 'norm_cross_g',
        'norm_mem_g', 'w_cq', 'w_ck', 'w_cv', 'cq_norm_g', 'ck_norm_g', 'w_co', 'norm_ffn_g', 'w_rg', 'b_rg', 'w_re',
        'b_re', 'w_e_gate', 'w_e_up', 'w_e_down']
_OUTS = [('y_prompt', (1, SEQ, D)), ('y_sample', (NB, 1, D)),
         ('win_k_prompt', (1, 1, SEQ, H, HD)), ('win_v_prompt', (1, 1, SEQ, H, HD)),
         ('win_k_sample', (1, NB, WB, H, HD)), ('win_v_sample', (1, NB, WB, H, HD)),
         ('pool_prompt', (1, 1, HIST, PW)), ('pool_sample', (1, NB, HIST, PW)),
         ('mem_k_prompt', (1, 1, NM, XH, XD)), ('mem_v_prompt', (1, 1, NM, XH, XD))]


def kernel(**inputs):
    import concourse.bacc as _bacc
    from concourse.bass_utils import run_bass_kernel_spmd as _run

    nc = _bacc.Bacc("TRN2", target_bir_lowering=False, num_devices=1)
    arrays, args = {}, {}
    for name in _INS + ["const"]:
        arr = constants() if name == "const" else np.ascontiguousarray(inputs[name])
        arrays[f"in_{name}_dram"] = arr
        args[name] = nc.dram_tensor(f"in_{name}_dram", arr.shape, mybir.dt.from_np(arr.dtype), kind="ExternalInput").ap()
    for name, shape in _OUTS:
        args[name] = nc.dram_tensor(f"out_{name}_dram", shape, F32, kind="ExternalOutput").ap()
    hybrid_decoder_layer(nc, args)
    r = _run(nc, [arrays], core_ids=[0])
    return tuple(r.results[0][f"out_{name}_dram"] for name, _ in _OUTS)
```

```python
from contextlib import ExitStack
import math

import numpy as np
import concourse.bass as bass
from concourse import mybir

F32 = mybir.dt.float32
I32 = mybir.dt.int32
U32 = mybir.dt.uint32
ALU = mybir.AluOpType
ACT = mybir.ActivationFunctionType
AX = mybir.AxisListType

P = 128
D = 2048
KT = D // P
SEQ = 256
PT = SEQ // P
NB = 8
TOK = SEQ + NB
TC = SEQ + 32
H, HD = 12, 64
AW = H * HD
POOL_WINDOWS = (2, 4, 8, 16)
PG, PC = 4, 320
PW = PG * PC
HIST = 15
IN_W = 3 * AW + PW
NCH = IN_W // 512
WB = 2048
NM = 256
XH, XD = 4, 128
XW = XH * XD
NG, EG = 4, 8
NE = NG * EG
DE = 512
EPS = 1e-6
NEG = -1e30
BLK = 32
OVB = 2 * TOK // BLK
NBLK = NE + OVB
NBUCKET, MAXD = 32, 2048
BRANCHES = ((128, 1), (512, 4), (2048, 16))


def bucket(dist):
    n = np.asarray(dist, dtype=np.int64)
    exact = NBUCKET // 2
    ratio = np.log(np.maximum(n, 1) / exact) / np.log(MAXD / exact)
    large = np.minimum(exact + (ratio * (NBUCKET - exact)).astype(np.int64), NBUCKET - 1)
    return np.where(n < exact, n, large)


def bias_columns(dist):
    dist = np.asarray(dist)
    out = np.zeros((NBUCKET + 1, len(dist)), np.float32)
    for c, d in enumerate(dist):
        mult = sum(1 for w, s in BRANCHES if 0 <= d <= w and d % s == 0)
        if mult:
            out[bucket(d), c] = 1.0
            out[NBUCKET, c] = math.log(mult)
        else:
            out[NBUCKET, c] = NEG
    return out


DEC_ROWS = (P, 97, 96)
DEC_OFF = (0, P, P + 97)
NDEC = sum(DEC_ROWS)
DEC_DIST = ([P - r for r in range(P)] + [512 - 4 * r for r in range(96)] + [0] + [2048 - 16 * r for r in range(96)])

CONST_W = dict(ident=P, tri=P, moe=NE + NE + 3 + OVB + 12, pool=PG * 256 + PG * P, pools=2 * PG * NB,
               flip=P, mask=AW, xmask=XW, sel=4, ohp=384, ohs=NDEC)
CONST_AT = {}
_at = 0
for _k, _w in CONST_W.items():
    CONST_AT[_k] = (_at, _at + _w)
    _at += _w
CONST_N = _at


def constants():
    c = np.zeros((P, CONST_N), np.float32)

    def part(name):
        a, b = CONST_AT[name]
        return c[:, a:b]

    part("ident")[:] = np.eye(P)
    part("flip")[:] = np.eye(P)[::-1]
    part("tri")[:] = np.triu(np.ones((P, P)), 1)
    m = part("moe")
    m[:, 0:NE] = NE - np.arange(NE)
    m[:, NE:2 * NE] = BLK * np.arange(NE)
    m[:, 2 * NE:2 * NE + 3] = 1.0
    m[NB:, 2 * NE + 2] = 0.0
    m[:, 2 * NE + 3:2 * NE + 3 + OVB] = np.arange(OVB)
    m[:, 2 * NE + 3 + OVB:] = (4 * (np.arange(P)[:, None, None] + P * np.arange(3)[:, None]) + np.arange(4)).reshape(P, 12)
    full = np.zeros((PG, SEQ, SEQ), np.float32)
    for g, w in enumerate(POOL_WINDOWS):
        for t in range(SEQ):
            lo = max(t + 1 - w, 0)
            full[g, lo:t + 1, t] = 1.0 / min(w, t + 1)
            full[g, t, t] -= 1.0
    pool = part("pool")
    pool[:, 0:PG * 256] = full[:, 0:P].transpose(1, 0, 2).reshape(P, -1)
    pool[:, PG * 256:] = full[:, P:, P:].transpose(1, 0, 2).reshape(P, -1)
    ps = part("pools").reshape(P, 2, PG, NB)
    for g, w in enumerate(POOL_WINDOWS):
        for b in range(NB):
            ps[b * HIST + HIST - (w - 1):b * HIST + HIST, 0, g, b] = 1.0 / w
            ps[b, 1, g, b] = 1.0 / w - 1.0
    for i in range(4):
        for h in range(H):
            part("mask")[32 * i + h, h * HD:(h + 1) * HD] = 1.0
        for h in range(XH):
            part("xmask")[32 * i + h, h * XD:(h + 1) * XD] = 1.0
        part("sel")[32 * i:32 * i + 32, i] = 1.0
    part("ohp")[0:NBUCKET + 1] = bias_columns([255 - v for v in range(384)])
    part("ohs")[0:NBUCKET + 1] = bias_columns(DEC_DIST)
    return c


def hybrid_decoder_layer(nc, a):
    with ExitStack() as ctx:
        def sem(name):
            return ctx.enter_context(nc.semaphore(name))

        def sb(name, shape, dt=F32):
            return ctx.enter_context(nc.sbuf_tensor(name, shape, dt))

        bias_dram = nc.dram_tensor("bias_rows", (H, 384), F32, kind="Internal").ap()
        xn_dram = nc.dram_tensor("moe_in", (4 * TOK, D // 4), F32, kind="Internal").ap()
        TABLE = 2 * P * -(-(NBLK + 1) * BLK // (2 * P))
        table = nc.dram_tensor("moe_table", (TABLE, 4), U32, kind="Internal").ap()
        ys_dram = nc.dram_tensor("moe_out", (NBLK * BLK, D), F32, kind="Internal").ap()

        ring = sb("ring", [P, 3, 8192])
        x3 = sb("x3", [P, 3, D])
        hT = sb("hT", [P, KT, TC])
        z = sb("z", [P, 3, IN_W])
        qkm = sb("qkm", [P, 4096])
        mkT = qkm[:, H * SEQ:].rearrange("p (h m) -> p h m", h=XH)
        qkT = qkm[:, 0:H * SEQ].rearrange("p (a h t) -> p a h t", a=2, h=H // 2)
        ident = sb("ident", [P, P])
        tri = sb("tri", [P, P])
        dg = sb("dg", [P, 3, P])
        s_in = sb("s_in", [P, 3, 2, P])
        psm = sb("psm", [P, 2, NDEC])
        moec = sb("moec", [P, 2 * NE + 3 + OVB + 12])
        quarters = sb("quarters", [P, 3, 4], U32)
        row_i = sb("row_i", [P, 1], U32)
        zero_i = sb("zero_i", [P, TABLE // P * 4], U32)
        poolsc = sb("poolsc", [P, 2, PG, NB])
        sel = sb("sel", [P, 4])
        gT = sb("gT", [P, 4, KT])
        gqk = sb("gqk", [P, 2, HD])
        gxx = sb("gxx", [P, 2, XD])
        psc = sb("psc", [P, PW // P])
        st = sb("st", [P, 152])
        slot_i = sb("slot_i", [P, 2, 3], U32)
        gates = sb("gates", [P, 2, 3])
        ov_i = sb("ov_i", [1, OVB + 1], I32)

        slot2 = ring[:, 2, :]
        mixT = slot2[:, 0:KT * TC].rearrange("p (k t) -> p k t", k=KT)
        hmT = slot2[:, 0:KT * NM].rearrange("p (k t) -> p k t", k=KT)
        AFTER_MIX = KT * TC
        bias = slot2[:, AFTER_MIX:AFTER_MIX + H * SEQ].rearrange("p (h j) -> p h j", h=H)
        bias_flat = after_mix = slot2[:, AFTER_MIX:AFTER_MIX + H * SEQ]
        biasS = slot2[:, AFTER_MIX + H * SEQ:AFTER_MIX + H * SEQ + NDEC]
        qkt_flat = qkm[:, 0:H * SEQ]
        rb = psm[:, 0, 0:H]
        rbs = psm[:, 0, 16:144].rearrange("p (i h) -> p i h", i=4)
        flip = slot2[:, 8192 - P:8192]
        hankel = qkt_flat
        ohp = qkt_flat[:, 0:384]
        ohs = qkt_flat[:, 384:384 + NDEC]
        brow = qkt_flat[:, 768:768 + 384]
        sq = qkt_flat[:, 1536:1536 + 2 * AW]
        zf = z[:].rearrange("p t n -> p (t n)")
        CK, CV, IN0 = 0, 1, 2
        POOLW = IN0 + NCH
        WOUT = POOLW + 1
        CQ, CO = WOUT + 4, WOUT + 5
        pslot = ring[:, POOLW % 2, :]
        pw = pslot[:, 0:10 * PC].rearrange("p (c d) -> p c d", c=10)
        poolT = pslot[:, 3200:3200 + 10 * TOK].rearrange("p (c t) -> p c t", c=10)
        state = pslot[:, 5840:5840 + PW]
        poolc = z[:, 0, 0:2 * AW]
        poolA = poolc[:, 0:1024].rearrange("p (g t) -> p g t", g=PG)
        poolB = poolc[:, 1024:1536].rearrange("p (g t) -> p g t", g=PG)
        prb = z[:, 1, 0:768].rearrange("p (b j) -> p b j", b=2)
        prT = z[:, 1, 768:1536].rearrange("p (b j) -> p b j", b=2)
        h_flat = hT[:].rearrange("p k t -> p (k t)")
        kbuf, vbuf = ([r[:, lo:lo + 3 * AW].rearrange("p (t n) -> p t n", t=3) for r, lo in rs]
                      for rs in (((slot2, 0), (slot2, 3 * AW)), ((h_flat, 0), (h_flat, 3 * AW), (qkt_flat, 0))))
        norm_dump = h_flat[:, 0:D]
        mask = after_mix[:, 0:AW]
        masked = after_mix[:, AW:2 * AW]
        memr = zf[:, 0:2 * D].rearrange("p (t n) -> p t n", t=2)
        msq = zf[:, 2 * D:2 * D + XW]
        mk = z[:, 2, IN_W - 4 * XW:IN_W - 2 * XW].rearrange("p (t n) -> p t n", t=2)
        mv = z[:, 2, IN_W - 2 * XW:IN_W].rearrange("p (t n) -> p t n", t=2)
        xq = zf[:, 0:3 * XW].rearrange("p (t n) -> p t n", t=3)
        xqT = zf[:, 1536:1536 + XH * SEQ].rearrange("p (h t) -> p h t", h=XH)
        xsq = zf[:, 2560:2560 + XW]
        oT = slot2[:, 0:XH * TC].rearrange("p (h t) -> p h t", h=XH)
        xprb = slot2[:, 1152:2176].rearrange("p (b j) -> p b j", b=2)
        xprT = slot2[:, 2176:3200].rearrange("p (b j) -> p b j", b=2)
        xkv = [zf[:, lo:lo + 2 * XW].rearrange("p (t n) -> p t n", t=2) for lo in (3072, 4096, 5120, 7168, 8192)]
        XKVB = len(xkv)
        chunk_dump = after_mix[:, 1536:2048]
        xmask = after_mix[:, 2048:2560]
        xmasked = after_mix[:, 2560:3072]
        xn = zf[:, 0:3 * D].rearrange("p (t n) -> p t n", t=3)
        M0 = 3 * D
        wr = zf[:, M0:M0 + KT * 36].rearrange("p (k n) -> p k n", k=KT)
        b36 = zf[0:36, M0 + 576:M0 + 577]
        LT = zf[0:36, M0 + 580:M0 + 580 + TOK]
        rt = zf[:, M0 + 900:M0 + 900 + 1600]
        xe = zf[:, M0 + 2560:M0 + 3072]
        XT = zf[:, M0 + 3072:M0 + 3584].rearrange("p (j s) -> p j s", j=4)
        ge, gd, gr, hid, aT = (zf[:, M0 + 3584 + 128 * i:M0 + 3712 + 128 * i] for i in range(5))
        yo = rt[:, 0:512]
        ones = ge
        down1 = [r.rearrange("p (k n) -> p k n", k=2) for r in (qkm[:, :], h_flat[:, 0:4096])]
        gu1 = zf[:, 0:4096].rearrange("p (m k n) -> p m k n", m=2, k=4)

        pb = [ctx.enter_context(nc.psum_tensor(f"pb{i}", [P, 512], F32)) for i in range(8)]
        VB, AB = pb[0:4], pb[4:8]

        const_landed, x_landed = sem("const_landed"), sem("x_landed")
        w_landed = [sem("w_landed0"), sem("w_landed1")]
        v_filled, v_freed = sem("v_filled"), sem("v_freed")
        a_filled, a_freed = sem("a_filled"), sem("a_freed")
        dve_seq = sem("dve_seq")
        squared, mean_ready, root_ready, diag_ready = sem("squared"), sem("mean_ready"), sem("root_ready"), sem("diag_ready")
        zeros_ready, pads_ready = sem("zeros_ready"), sem("pads_ready")
        table_zeroed, xn_stored, row_i_landed = sem("table_zeroed"), [sem("xn_stored0"), sem("xn_stored1")], sem("row_i_landed")
        block_known = sem("block_known")
        brow_stored, bias_landed = sem("brow_stored"), sem("bias_landed")
        qk_normed, mk_normed, xq_normed = sem("qk_normed"), sem("mk_normed"), sem("xq_normed")
        keys_stored, rows_stored, stored = sem("keys_stored"), sem("rows_stored"), sem("stored")
        copied = sem("copied")
        biased, exped, probs_ready = sem("biased"), sem("exped"), sem("probs_ready")
        poolc_landed, state_landed = sem("poolc_landed"), sem("state_landed")
        key_landed = [sem(f"key_landed{i}") for i in range(2)]
        val_landed = [sem(f"val_landed{i}") for i in range(3)]
        xkv_landed = [sem(f"xkv_landed{i}") for i in range(XKVB)]
        keys_used, vals_used = sem("keys_used"), sem("vals_used")
        s_biased, s_exped, s_probs = sem("s_biased"), sem("s_exped"), sem("s_probs")
        mask_landed = sem("mask_landed")
        mem_landed = [sem("mem_landed0"), sem("mem_landed1")]
        mem_stored, mv_landed = sem("mem_stored"), sem("mv_landed")
        router_landed = sem("router_landed")
        xn_ready, exp_in, exp_out = sem("xn_ready"), sem("exp_in"), sem("exp_out")
        pairs_ready, over_cols_ready = sem("pairs_ready"), sem("over_cols_ready")
        slots_ready, scattered = sem("slots_ready"), sem("scattered")
        xe_landed = sem("xe_landed")
        gu_landed, gu_used = [sem("gu_landed0"), sem("gu_landed1")], [sem("gu_used0"), sem("gu_used1")]
        dn_landed, dn1_landed, dn_used = sem("dn_landed"), sem("dn1_landed"), sem("dn_used")
        gu1_landed = sem("gu1_landed")
        xt_filled, xt_ready = sem("xt_filled"), sem("xt_ready")
        gate_exp, hid_seq, hid_ready = sem("gate_exp"), sem("hid_seq"), sem("hid_ready")
        hidT_filled, hidT_ready = sem("hidT_filled"), sem("hidT_ready")
        y_ready, y_stored = sem("y_ready"), sem("y_stored")
        y_gathered = [sem(f"y_gathered{i}") for i in range(6)]
        x_final = sem("x_final")

        cdr = a["const"]

        def cc(name, p=P):
            lo, hi = CONST_AT[name]
            return cdr[0:p, lo:hi]

        def wk(i):
            return ring[:, i % 2, :].rearrange("p (k n) -> p k n", k=KT)

        def piece_landed(eng, i):
            n = i // 2 + 1
            if i % 2 == POOLW % 2 and i >= POOLW:
                n += POOL_DMAS - 1
            eng.wait_ge(w_landed[i % 2], 16 * n)

        POOL_DMAS = 4
        FLIPS = H * SEQ // 512
        A_MEM = 4
        A_QKT = A_MEM + 2 * NCH + 6
        A_ATT = A_QKT + 2 * H
        A_SEL = A_ATT + 2 + 10 + 2 + 1
        A_DEC = A_ATT + 2 + 20 + 2
        A_XQT = A_DEC + 2 + 2
        V_MK = 2 + 8 + 1
        V_PRE = V_MK + 1 + 12
        QUERIES = {4: (0, 1, 2), 5: (3, 4, 5), 6: (6, 7)}
        V_QUERY = {4: 2 * 2, 5: 2 * 5, 6: 2 * 8}
        V_IN = V_PRE + NCH + FLIPS + 2 * NB
        V_WOUT = V_IN + 2 + H + 4 + 12
        V_CQ = V_WOUT + 12 + 1
        V_XP = V_CQ + XH
        V_XR = V_XP + 8 + NB + 2 + 8 + 2
        V_CO = V_XR + 4
        N_CONST = 22
        N_SQUARED = 2 + 3 + 2 + 3 + 3 + 12 + 12

        def piece_used(eng, i):
            if i < IN0:
                eng.wait_ge(v_filled, V_MK + i)
            elif i < POOLW:
                n = i - IN0
                eng.wait_ge(v_filled, V_PRE + n + 1 + (FLIPS if n > 1 else 0) + V_QUERY.get(n, 0))
            elif i == POOLW:
                eng.wait_ge(a_filled, A_DEC - 1)
            elif i < CQ:
                eng.wait_ge(v_filled, V_WOUT - 12 + 3 * (i - WOUT + 1))
            else:
                eng.wait_ge(v_filled, {CQ: V_CQ, CO: V_CO}[i])

        def key_ready(eng, b):
            eng.wait_ge(key_landed[b % 2], 64 * (b // 2 + 1))

        def val_ready(eng, b):
            eng.wait_ge(val_landed[b % 3], 64 * (b // 3 + 1))

        def xkv_ready(eng, j):
            eng.wait_ge(xkv_landed[j % XKVB], 16 * (j // XKVB + 1))

        def turn_job(h):
            return 0 if h == 0 else 2 * h - 1

        block = ctx.enter_context(nc.Block())

        @block.sync
        def _(sp):
            def big(i):
                if i >= 2:
                    piece_used(sp, i - 2)
                done = w_landed[i % 2]
                if IN0 <= i < POOLW:
                    n = i - IN0
                    src = a["w_in"][0][:, 512 * n:512 * n + 512].rearrange("(p k) n -> p k n", k=KT)
                elif i == POOLW:
                    g2 = a["pool_w"][0]
                    for c in range(2):
                        sp.dma_start(pw[:, 0:8, :].rearrange("p (g c) d -> p g c d", c=2)[:, :, c],
                                     g2[:, c * P:c * P + P, :].rearrange("g p d -> p g d")).then_inc(done, 16)
                    for o in range(2):
                        sp.dma_start(pw[64 * o:64 * o + 64, 8:10, :],
                                     g2[o:PG:2, 2 * P:PC, :].rearrange("g p d -> p g d")).then_inc(done, 16)
                    return
                elif WOUT <= i < CQ:
                    n = i - WOUT
                    src = a["w_out"][0][:, 512 * n:512 * n + 512].rearrange("(k p) n -> p k n", p=P)
                elif i < CO:
                    w = {CK: "w_ck", CV: "w_cv", CQ: "w_cq"}[i]
                    src = a[w][0].rearrange("(p k) n -> p k n", k=KT)
                else:
                    src = a["w_co"][0].rearrange("(k p) n -> p k n", p=P)
                    sp.dma_start(ring[:, i % 2, :].rearrange("p (k n) -> p k n", k=XH), src).then_inc(done, 16)
                    return
                sp.dma_start(wk(i), src).then_inc(done, 16)

            for t in range(2):
                sp.dma_start(memr[:, t], a["mem_prompt"][0, P * t:P * t + P]).then_inc(mem_landed[t], 16)
            for dst, src in ((ident[:], cc("ident")), (rb[0:NBUCKET], a["rel_bias"]),
                             (ohp[0:33], cc("ohp", 33)), (ohs[0:33], cc("ohs", 33)),
                             (tri[:], cc("tri")), (flip, cc("flip")), (moec[:], cc("moe")),
                             (poolsc[:].rearrange("p a g b -> p (a g b)"), cc("pools")), (sel[:], cc("sel"))):
                sp.dma_start(dst, src).then_inc(const_landed, 16)
            sp.wait_ge(zeros_ready, 1)
            for i in range(4):
                sp.dma_start(rbs[0:NBUCKET, i, 0:H], a["rel_bias"]).then_inc(const_landed, 16)
            for i, g in enumerate(("norm_mix_g", "norm_mem_g", "norm_cross_g", "norm_ffn_g")):
                sp.dma_start(gT[:, i, :], a[g][0].rearrange("(p k) -> p k", k=KT)).then_inc(const_landed, 16)
            for i, g in enumerate(("q_norm_g", "k_norm_g")):
                sp.dma_start(gqk[:, i, :], a[g].to_broadcast([P, HD])).then_inc(const_landed, 16)
            for i, g in enumerate(("cq_norm_g", "ck_norm_g")):
                sp.dma_start(gxx[:, i, :], a[g].to_broadcast([P, XD])).then_inc(const_landed, 16)
            with nc.allow_non_contiguous_dma(reason="1280 scale values, one per partition"):
                sp.dma_start(psc[:], a["pool_scale"][0].rearrange("(k p) -> p k", p=P)).then_inc(const_landed, 16)
            big(0)
            sp.dma_start(x3[:, 0:2, :], a["x_prompt"][0].rearrange("(t p) n -> p t n", p=P)).then_inc(x_landed, 16)
            sp.wait_ge(zeros_ready, 2)
            sp.dma_start(x3[0:NB, 2, :], a["x_sample"][:, 0]).then_inc(x_landed, 16)
            big(1)
            sp.wait_ge(v_freed, 2)
            sp.dma_start(bias_dram[:, :], brow[0:H, :]).then_inc(brow_stored, 16)
            sp.wait_ge(brow_stored, 16)
            sp.dma_start(hankel.rearrange("p (h j) -> p h j", h=H),
                         bass.AP(tensor=bias_dram.tensor, offset=0, ap=[[1, P], [384, H], [1, SEQ]]))\
                .then_inc(bias_landed, 16)
            big(IN0)
            sp.wait_ge(mk_normed, 3)
            sp.dma_start(a["mem_k_prompt"][0, 0].rearrange("(t p) h e -> p t (h e)", p=P), mk).then_inc(mem_stored, 16)
            sp.dma_start(a["mem_v_prompt"][0, 0].rearrange("(t p) h e -> p t (h e)", p=P), mv).then_inc(mem_stored, 16)
            for i in range(IN0 + 1, IN0 + 6):
                big(i)
            sp.wait_ge(qk_normed, 3)
            for dst, src in ((a["win_k_prompt"][0, 0].rearrange("(t p) h e -> p t (h e)", p=P), z[:, 0:2, AW:2 * AW]),
                             (a["win_k_sample"][0, :, WB - 1].rearrange("b h e -> b (h e)"), z[0:NB, 2, AW:2 * AW])):
                sp.dma_start(dst, src).then_inc(keys_stored, 16)
            for i in range(IN0 + 6, POOLW + 1):
                big(i)
            piece_used(sp, POOLW - 2)
            sp.dma_start(state[0:NB * HIST, :], a["state_pool"][0].rearrange("b s n -> (b s) n")).then_inc(state_landed, 16)
            sp.wait_ge(a_freed, A_MEM + 2 * NCH)
            sp.wait_ge(v_freed, V_IN)
            for dst, src in ((a["win_v_prompt"][0, 0].rearrange("(t p) h e -> p t (h e)", p=P), z[:, 0:2, 2 * AW:3 * AW]),
                             (a["win_v_sample"][0, :, WB - 1].rearrange("b h e -> b (h e)"), z[0:NB, 2, 2 * AW:3 * AW]),
                             (a["pool_prompt"][0, 0], z[P - HIST:P, 1, 3 * AW:IN_W]),
                             (a["pool_sample"][0, :, HIST - 1], z[0:NB, 2, 3 * AW:IN_W])):
                sp.dma_start(dst, src).then_inc(rows_stored, 16)
            sp.wait_ge(keys_stored, 2 * 16)
            sp.wait_ge(a_freed, A_QKT)
            sp.dma_start(poolc, cc("pool")).then_inc(poolc_landed, 16)
            sp.wait_ge(rows_stored, 4 * 16)
            for i in range(WOUT, CO + 1):
                big(i)
                if i == WOUT + 2:
                    sp.wait_ge(mem_stored, 2 * 16)
                    sp.dma_start(mv, a["mem_v_prompt"][0, 0].rearrange("(t p) h e -> p t (h e)", p=P)).then_inc(mv_landed, 16)
                    for w, lo, n in (("w_rg", 0, NG), ("w_re", NG, NE)):
                        sp.dma_start(wr[:, :, lo:lo + n], a[w][0].rearrange("(p k) n -> p k n", k=KT)).then_inc(router_landed, 16)
                    for w, lo, n in (("b_rg", 0, NG), ("b_re", NG, NE)):
                        sp.dma_start(b36[lo:lo + n, :], a[w][0].rearrange("(n o) -> n o", o=1)).then_inc(router_landed, 16)

            def gate_up(i, e, half, k0=0):
                for m in range(2):
                    w = a[("w_e_gate", "w_e_up")[m]][0]
                    src = w[e] if isinstance(i, int) else w[bass.ds(e, 1)].rearrange("o k n -> (o k) n")
                    sp.dma_start(ring[:, half, 4096 * m:4096 * m + 4096].rearrange("p (k n) -> p k n", k=8)[:, k0:],
                                 src.rearrange("(p k) n -> p k n", k=KT)[:, 8 * half + k0:8 * half + 8, :])\
                        .then_inc(gu_landed[half], 16)

            def down(i, e):
                src = a["w_e_down"][0][e] if isinstance(i, int) else a["w_e_down"][0][bass.ds(e, 1)].rearrange("o k n -> (o k) n")
                sp.dma_start(slot2.rearrange("p (k n) -> p k n", k=4), src.rearrange("(k p) n -> p k n", p=P))\
                    .then_inc(dn_landed, 16)

            def expert_weights(i, e):
                for half in range(2):
                    sp.wait_ge(gu_used[half], i)
                    gate_up(i, e, half)
                sp.wait_ge(dn_used, i)
                down(i, e)

            w1 = a["w_e_down"][0][1].rearrange("(k p) n -> p k n", p=P)
            piece_used(sp, CQ)
            gate_up(0, 0, 0)
            sp.wait_ge(a_freed, A_XQT + 2 * XH)
            sp.dma_start(down1[0], w1[:, 0:2]).then_inc(dn1_landed, 16)
            piece_used(sp, CO)
            gate_up(0, 0, 1)
            sp.wait_ge(squared, N_SQUARED)
            down(0, 0)
            sp.wait_ge(xn_stored[0], 16)
            for m, w in enumerate(("w_e_gate", "w_e_up")):
                sp.dma_start(gu1[:, m], a[w][0][1].rearrange("(p k) n -> p k n", k=KT)[:, 0:4, :]).then_inc(gu1_landed, 16)
            sp.wait_ge(v_freed, V_CO + 4 + 1)
            sp.dma_start(down1[1], w1[:, 2:4]).then_inc(dn1_landed, 16)
            sp.wait_ge(gu_used[0], 1)
            gate_up(1, 1, 0, 4)
            sp.wait_ge(gu_used[1], 1)
            gate_up(1, 1, 1)
            with sp.Fori(2, NE) as i:
                expert_weights(i, i)
            sp.wait_ge(slots_ready, 1)
            n_over = sp.value_load(ov_i[0:1, OVB:OVB + 1], min_val=0, max_val=OVB)
            with sp.If(n_over > 0):
                with sp.Fori(NE, NBLK) as i:
                    expert_weights(i, sp.value_load(ov_i[0:1, bass.ds(i - NE, 1)], min_val=0, max_val=NE - 1))
            for t in range(3):
                sp.wait_ge(x_final, t + 1)
                if t < 2:
                    sp.dma_start(a["y_prompt"][0, t * P:(t + 1) * P, :], x3[:, t, :]).then_inc(stored, 16)
                else:
                    sp.dma_start(a["y_sample"][:, 0], x3[0:NB, 2, :]).then_inc(stored, 16)
            sp.wait_ge(stored, 3 * 16)
            sp.wait_ge(copied, (2 * NB + 1) * 16)
            sp.wait_ge(keys_stored, 2 * 16)
            sp.wait_ge(rows_stored, 4 * 16)
            sp.wait_ge(mem_stored, 2 * 16)

        @block.gpsimd
        def _(pool):
            pool.wait_ge(zeros_ready, 3)
            pool.dma_start(table.rearrange("(p r) c -> p (r c)", p=P), zero_i[:]).then_inc(table_zeroed, 16)

            def cache_copy(i):
                b, kv = i // 2, i % 2
                src = a[("cache_win_k", "cache_win_v")[kv]][0, b, 1:WB].rearrange("s h e -> (s h e)")
                dst = a[("win_k_sample", "win_v_sample")[kv]][0, b, 0:WB - 1].rearrange("s h e -> (s h e)")
                pool.dma_start(dst.rearrange("(p f) -> p f", p=96), src.rearrange("(p f) -> p f", p=96)).then_inc(copied, 16)

            for i in range(5):
                piece_used(pool, CK + i)
                cache_copy(i)

            def window_rows(kv, b, buf, landed):
                c = a[("cache_win_k", "cache_win_v")[kv]][0, b].rearrange("s h e -> s (h e)")
                new = (1 + kv) * AW
                pool.dma_start(buf[:, 0], c[WB - P:WB]).then_inc(landed, 16)
                pool.dma_start(buf[0:96, 1], c[WB - 512:WB - P].rearrange("(r q) n -> r q n", q=4)[:, 0]).then_inc(landed, 16)
                pool.dma_start(buf[0:96, 2], c[0:1536].rearrange("(r q) n -> r q n", q=16)[:, 0]).then_inc(landed, 16)
                pool.dma_start(buf[96:97, 1], z[b:b + 1, 2, new:new + AW]).then_inc(landed, 16)

            pool.wait_ge(pads_ready, 1)
            pool.wait_ge(qk_normed, 3)
            for b in range(NB):
                if b >= 2:
                    pool.wait_ge(keys_used, b - 1)
                window_rows(0, b, kbuf[b % 2], key_landed[b % 2])
                if b == 1:
                    cache_copy(5)
            cache_copy(6)
            piece_used(pool, POOLW - 1)
            pool.wait_ge(a_freed, A_MEM + 2 * NCH)
            for b in range(NB):
                if b == 2:
                    cache_copy(7)
                    pool.wait_ge(biased, H)
                    pool.dma_start(mask, cc("mask")).then_inc(mask_landed, 16)
                    pool.wait_ge(a_freed, A_ATT)
                if b >= 3:
                    pool.wait_ge(vals_used, b - 2)
                window_rows(1, b, vbuf[b % 3], val_landed[b % 3])
            pool.dma_start(a["pool_sample"][0, :, 0:HIST - 1], a["state_pool"][0, :, 1:HIST]).then_inc(copied, 16)
            pool.wait_ge(a_freed, A_DEC)
            pool.dma_start(xmask, cc("xmask")).then_inc(mask_landed, 16)
            for i in range(8, 10):
                cache_copy(i)
            piece_used(pool, WOUT)
            for j in range(2 * NB):
                kv, b = j // NB, j % NB
                if j == XKVB:
                    for i in range(10, 16):
                        piece_used(pool, WOUT + (0, 1, 2, 3, 3, 4)[i - 10])
                        cache_copy(i)
                if j >= XKVB:
                    if j - XKVB < NB:
                        pool.wait_ge(keys_used, NB + j - XKVB + 1)
                    else:
                        pool.wait_ge(vals_used, j - XKVB + 1)
                c = a[("cache_mem_k", "cache_mem_v")[kv]][0, b].rearrange("(t p) h e -> p t (h e)", p=P)
                pool.dma_start(xkv[j % XKVB], c).then_inc(xkv_landed[j % XKVB], 16)
            pool.wait_ge(xn_ready, 2)
            pool.dma_start(xn_dram[0:4 * SEQ].rearrange("(t p c) n -> p t (c n)", t=2, c=4), xn[:, 0:2, :]).then_inc(xn_stored[0], 16)
            pool.wait_ge(xn_ready, 3)
            pool.dma_start(xn_dram[4 * SEQ:].rearrange("(p c) n -> p (c n)", c=4), xn[0:NB, 2, :]).then_inc(xn_stored[1], 16)
            pool.wait_ge(table_zeroed, 16)
            pool.wait_ge(slots_ready, 1)
            for s in range(2):
                for t in range(3):
                    n = P if t < 2 else NB
                    pool.indirect_dma_start(table[:, :], bass.IndirectOffsetOnAxis(ap=slot_i[0:n, s, t:t + 1], axis=0),
                                            quarters[0:n, t, :], None).then_inc(scattered, 16)
            pool.wait_ge(scattered, 6 * 16)
            for s in xn_stored:
                pool.wait_ge(s, 16)

            def load_rows_of(block):
                with nc.allow_non_contiguous_dma(reason="128 numbers, one per partition"):
                    for c in range(4):
                        pool.dma_start(row_i[32 * c:32 * c + 32, :], table[block, c:c + 1]).then_inc(row_i_landed, 16)

            def block_rows(i):
                if not isinstance(i, int):
                    pool.wait_ge(xt_filled, i)
                pool.wait_ge(row_i_landed, 64 * (i + 1))
                pool.nop().then_inc(block_known, 1)
                pool.indirect_dma_start(xe, None, xn_dram[:, :], bass.IndirectOffsetOnAxis(ap=row_i[:, 0:1], axis=0))\
                    .then_inc(xe_landed, 16)
                pool.wait_ge(xe_landed, 16 * (i + 1))
                load_rows_of(slice(BLK, 2 * BLK) if isinstance(i, int) else bass.ds((i + 1) * BLK, BLK))

            def gather_results(blocks):
                pool.wait_ge(y_stored, 64 * blocks)
                pool.wait_ge(dn_used, blocks)
                for t in range(3):
                    for s in range(2):
                        n = P if t < 2 else NB
                        j = 2 * t + s
                        pool.indirect_dma_start(ring[0:n, j // 4, (j % 4) * D:(j % 4 + 1) * D], None,
                                                ys_dram[0:BLK * blocks, :],
                                                bass.IndirectOffsetOnAxis(ap=slot_i[0:n, s, t:t + 1], axis=0))\
                            .then_inc(y_gathered[j], 16)

            load_rows_of(slice(0, BLK))
            block_rows(0)
            with pool.Fori(1, NE) as i:
                block_rows(i)
            n_over = pool.value_load(ov_i[0:1, OVB:OVB + 1], min_val=0, max_val=OVB)
            with pool.If(n_over > 0):
                with pool.Fori(NE, NBLK) as i:
                    block_rows(i)
                gather_results(NBLK)
            with pool.Else():
                gather_results(NE)

        @block.tensor
        def _(pe):
            nv = na = nd = 0
            mm = nc.tensor.matmul

            def vbank():
                nonlocal nv
                if nv >= 4:
                    pe.wait_ge(v_freed, nv - 3)
                nv += 1
                return VB[(nv - 1) % 4]

            def abank():
                nonlocal na
                if na >= 4:
                    pe.wait_ge(a_freed, na - 3)
                na += 1
                return AB[(na - 1) % 4]

            def all_emptied():
                pe.wait_ge(v_freed, nv)
                pe.wait_ge(a_freed, na)

            def norm_turn(rows, first, end, parts=range(4), new_scales=True):
                nonlocal nd
                if new_scales:
                    nd += 1
                    pe.wait_ge(diag_ready, nd)
                for t in range(first, end):
                    cols = rows[:, t, :].rearrange("p (m k) -> p k m", k=KT)
                    for j in parts:
                        bk = vbank()
                        for k in range(4):
                            last = mm(bk[:, P * k:P * k + P], cols[:, 4 * j + k, :], dg[:, t, :], start=True, stop=True)
                        last.then_inc(v_filled, 1)

            def project(xT, w, nk, tile, bk, filled):
                for k in range(nk):
                    last = mm(bk[:, :], xT[:, k, tile * P:tile * P + P], w[:, k, :], start=(k == 0), stop=(k == nk - 1))
                last.then_inc(filled, 1)

            def project_sample(xT, w, nk, bk, filled):
                for k in range(nk):
                    for c in range(4):
                        last = mm(bk[32 * c:32 * c + 32, 0:P], xT[:, k, SEQ:TC], w[:, k, P * c:P * c + P],
                                  start=(k == 0), stop=(k == nk - 1))
                last.then_inc(filled, 1)

            pe.wait_ge(const_landed, 16 * N_CONST)
            pe.wait_ge(zeros_ready, 3)
            bk = vbank()
            mm(bk[0:H, 0:384], rb[0:33], ohp[0:33, :], start=True, stop=True).then_inc(v_filled, 1)
            bk = vbank()
            mm(bk[:, 0:NDEC], rbs[0:33].rearrange("p i h -> p (i h)"), ohs[0:33, :], start=True, stop=True)\
                .then_inc(v_filled, 1)
            norm_turn(memr, 0, 2)
            all_emptied()
            for i in (CK, CV):
                piece_landed(pe, i)
                project(hmT, wk(i), KT, 0, abank(), a_filled)
                project(hmT, wk(i), KT, 1, vbank(), v_filled)
            norm_turn(x3, 0, 3)
            pe.wait_ge(mk_normed, 2)
            for pair in range(2):
                bk = abank()
                for j in range(2):
                    for t in range(2):
                        last = nc.tensor.transpose(bk[:, P * (2 * j + t):P * (2 * j + t) + P],
                                                   mk[:, t, P * (2 * pair + j):P * (2 * pair + j) + P], ident[:])
                last.then_inc(a_filled, 1)
            all_emptied()
            def query_row(rows, lo, n, b):
                bk = vbank()
                mm(bk[:, 0:n], ident[:, b:b + 1].to_broadcast([P, P]), rows[:, 2, lo:lo + n], start=True, stop=True)\
                    .then_inc(v_filled, 1)

            for n in range(NCH):
                i = IN0 + n
                queries = iter(QUERIES.get(n, ()))

                def next_query():
                    for b in queries:
                        query_row(z, 0, 512, b)
                        query_row(z, 512, AW - 512, b)
                        break

                if n == min(QUERIES):
                    pe.wait_ge(qk_normed, 3)
                piece_landed(pe, i)
                project(hT, wk(i), KT, 0, abank(), a_filled)
                next_query()
                project_sample(hT, wk(i), KT, abank(), a_filled)
                next_query()
                project(hT, wk(i), KT, 1, vbank(), v_filled)
                next_query()
                if n == 1:
                    pe.wait_ge(bias_landed, 16)
                    for f in range(FLIPS):
                        mm(vbank()[:, :], flip, hankel[:, 512 * f:512 * f + 512], start=True, stop=True)\
                            .then_inc(v_filled, 1)

            def turn_scores(tiles, offs, base):
                pe.wait_ge(keys_used, NB * (base + 1))
                for hf in range(2):
                    bk = vbank()
                    for t, n in enumerate(tiles):
                        last = nc.tensor.transpose(bk[:, offs[t]:offs[t] + n], s_in[0:n, t, hf, :], ident[0:n, 0:n])
                    last.then_inc(v_filled, 1)

            def turn_probs(tiles, offs, base):
                for hf in range(2):
                    pe.wait_ge(s_probs, 2 * base + hf + 1)
                    bk = abank()
                    for t, n in enumerate(tiles):
                        last = nc.tensor.transpose(bk[0:n, P * t:P * t + P], psm[:, hf, offs[t]:offs[t] + n], ident[:])
                    last.then_inc(a_filled, 1)

            turn_scores(DEC_ROWS, DEC_OFF, 0)
            pe.wait_ge(qk_normed, 3)
            for s in range(2):
                for pair in range(0, H // 2, 2):
                    bk = abank()
                    for j in range(2):
                        for t in range(2):
                            last = nc.tensor.transpose(bk[:, P * (2 * j + t):P * (2 * j + t) + P],
                                                       z[:, t, s * AW + P * (pair + j):s * AW + P * (pair + j) + P], ident[:])
                    last.then_inc(a_filled, 1)
            all_emptied()

            def attend(nh, score, turn, value):
                nonlocal probs_seen
                score(0)
                for s in range(nh + 2):
                    if s + 1 < nh:
                        score(s + 1)
                    if 1 <= s <= nh:
                        probs_seen += 1
                        pe.wait_ge(probs_ready, probs_seen)
                        turn(s - 1)
                    if s >= 2:
                        value(s - 2)

            probs_seen = 0
            turned = {}

            def score_win(h):
                r = slice(64 * (h % 2), 64 * (h % 2) + 64)
                bk = vbank()
                mm(bk[:, 0:P], qkT[r, 0, h // 2, 0:P], qkT[r, 1, h // 2, 0:P], start=True, stop=True)
                mm(bk[:, P:3 * P], qkT[r, 0, h // 2, P:SEQ], qkT[r, 1, h // 2, :], start=True, stop=True)\
                    .then_inc(v_filled, 1)

            def turn_win(h):
                bk = abank()
                for j in range(3):
                    last = nc.tensor.transpose(bk[:, P * j:P * j + P], prb[:, h % 2, P * j:P * j + P], ident[:])
                last.then_inc(a_filled, 1)
                turned[h] = na

            def value_win(h):
                pe.wait_ge(a_freed, turned[h])
                bk = abank()
                r = slice(64 * (h % 2), 64 * (h % 2) + 64)
                v = slice(2 * AW + HD * h, 2 * AW + HD * h + HD)
                mm(bk[r, 0:SEQ], z[:, 0, v], prT[:, h % 2, 0:SEQ], start=True, stop=False)
                mm(bk[r, P:SEQ], z[:, 1, v], prT[:, h % 2, SEQ:3 * P], start=False, stop=True).then_inc(a_filled, 1)

            attend(H, score_win, turn_win, value_win)

            def pool_channels(c):
                bk = abank()
                parts = [(c // 2, (c % 2) * P, P, 0)] if c < 8 else [(2 * (c - 8) + o, 2 * P, 64, 64 * o) for o in range(2)]
                for g, lo, n, r in parts:
                    u = slice(3 * AW + PC * g + lo, 3 * AW + PC * g + lo + n)
                    us = slice(PC * g + lo, PC * g + lo + n)
                    o = slice(r, r + n)
                    mm(bk[o, 0:SEQ], z[:, 0, u], poolA[:, g, :], start=True, stop=False)
                    mm(bk[o, P:SEQ], z[:, 1, u], poolB[:, g, :], start=False, stop=True)
                    mm(bk[o, SEQ:TOK], state[0:NB * HIST, us], poolsc[0:NB * HIST, 0, g, :], start=True, stop=False)
                    last = mm(bk[o, SEQ:TOK], z[0:NB, 2, u], poolsc[0:NB, 1, g, :], start=False, stop=True)
                last.then_inc(a_filled, 1)

            def pool_map(kt):
                bk = abank()
                lo = kt * P
                while lo < kt * P + P:
                    g = lo // PC
                    d = lo % PC
                    n = min(PC - d, kt * P + P - lo)
                    o = slice(lo - kt * P, lo - kt * P + n)
                    for c in range(3):
                        if c < 2:
                            w, x = pw[:, 2 * g + c, d:d + n], poolT[:, 2 * g + c, :]
                        else:
                            r = slice(64 * (g % 2), 64 * (g % 2) + 64)
                            w, x = pw[r, 8 + g // 2, d:d + n], poolT[r, 8 + g // 2, :]
                        last = mm(bk[o, 0:TOK], w, x, start=(c == 0), stop=(c == 2))
                    lo += n
                last.then_inc(a_filled, 1)

            def values_of(b, tiles, widths, buf, banks):
                i, hf = b % 4, b // 4
                for bk, (lo, n) in zip(banks, widths):
                    for t, k in enumerate(tiles):
                        last = mm(bk[32 * i:32 * i + 32, 0:n], s_in[0:k, t, hf, 32 * i:32 * i + 32],
                                  buf[0:k, t, lo:lo + n], start=(t == 0), stop=(t == len(tiles) - 1))
                if i < 3:
                    last.then_inc(vals_used, 1)
                else:
                    last.then_inc(v_filled, len(banks))

            def own_heads(masked_rows, ktiles, job):
                pe.wait_ge(v_freed, job)
                bk = abank()
                for k in range(ktiles):
                    last = mm(bk[:, 4 * k:4 * k + 4], masked_rows[:, P * k:P * k + P], sel[:], start=True, stop=True)
                    if k == 0:
                        last.then_inc(vals_used, 1)
                last.then_inc(a_filled, 1)

            turn_probs(DEC_ROWS, DEC_OFF, 0)
            piece_landed(pe, POOLW)
            pe.wait_ge(state_landed, 16)
            pe.wait_ge(poolc_landed, 16)
            pool_channels(0)
            pool_channels(1)
            pe.wait_ge(a_freed, A_ATT + 2)
            for b in range(NB):
                if b % 4 == 0:
                    banks = [vbank(), vbank()]
                val_ready(pe, b)
                values_of(b, DEC_ROWS, ((0, 512), (512, 256)), vbuf[b % 3], banks)
                if b < 4:
                    pool_channels(2 * b + 2)
                    pool_channels(2 * b + 3)
                if b == 3:
                    pe.wait_ge(a_freed, na)
                if b >= 3:
                    pool_map(2 * b - 6)
                    pool_map(2 * b - 5)
                if b == 3:
                    own_heads(masked, H // 2, nv)
            own_heads(masked, H // 2, nv)
            all_emptied()

            for i in range(WOUT, WOUT + 4):
                piece_landed(pe, i)
                project(mixT, wk(i), KT, 0, vbank(), v_filled)
                project(mixT, wk(i), KT, 1, vbank(), v_filled)
                project_sample(mixT, wk(i), KT, vbank(), v_filled)
            norm_turn(x3, 0, 3)
            all_emptied()
            piece_landed(pe, CQ)
            project(hT, wk(CQ), KT, 0, abank(), a_filled)
            project_sample(hT, wk(CQ), KT, abank(), a_filled)
            project(hT, wk(CQ), KT, 1, vbank(), v_filled)
            pe.wait_ge(xq_normed, 3)
            for pair in range(2):
                bk = abank()
                for j in range(2):
                    for t in range(2):
                        last = nc.tensor.transpose(bk[:, P * (2 * j + t):P * (2 * j + t) + P],
                                                   xq[:, t, P * (2 * pair + j):P * (2 * pair + j) + P], ident[:])
                last.then_inc(a_filled, 1)
            all_emptied()

            def score_mem(h):
                bk = vbank()
                for t in range(2):
                    last = mm(bk[:, NM * t:NM * t + NM], xqT[:, h, P * t:P * t + P], mkT[:, h, :], start=True, stop=True)
                last.then_inc(v_filled, 1)

            def turn_mem(h):
                bk = abank()
                for m in range(2):
                    for t in range(2):
                        last = nc.tensor.transpose(bk[:, SEQ * m + P * t:SEQ * m + P * t + P],
                                                   xprb[:, h % 2, NM * t + P * m:NM * t + P * m + P], ident[:])
                last.then_inc(a_filled, 1)
                turned[h] = na

            def value_mem(h):
                if h == 0:
                    pe.wait_ge(mv_landed, 16)
                pe.wait_ge(a_freed, turned[h])
                bk = abank()
                for m in range(2):
                    last = mm(bk[:, 0:SEQ], mv[:, m, XD * h:XD * h + XD], xprT[:, h % 2, SEQ * m:SEQ * m + SEQ],
                              start=(m == 0), stop=(m == 1))
                last.then_inc(a_filled, 1)

            attend(XH, score_mem, turn_mem, value_mem)
            pe.wait_ge(a_freed, na)
            piece_landed(pe, CO)
            wo = ring[:, CO % 2, :].rearrange("p (k n) -> p k n", k=XH)
            for n in range(4):
                for t in range(2):
                    project(oT, wo[:, :, 512 * n:512 * n + 512], XH, t, vbank(), v_filled)
                    query_row(xq, 0, XW, 2 * n + t)
            turn_scores((P, P), (0, P), 1)
            norm_turn(x3, 0, 1)
            turn_probs((P, P), (0, P), 1)
            pe.wait_ge(a_freed, na)
            for b in range(NB):
                if b % 4 == 0:
                    banks = [vbank()]
                xkv_ready(pe, NB + b)
                values_of(b, (P, P), ((0, XW),), xkv[(NB + b) % XKVB], banks)
                if b % 4 == 3:
                    job = nv
                    norm_turn(x3, 1, 2, (0, 1) if b == 3 else (2, 3), new_scales=False)
                    own_heads(xmasked, XH, job)
            all_emptied()
            for n in range(4):
                project_sample(oT, wo[:, :, 512 * n:512 * n + 512], XH, vbank(), v_filled)
            norm_turn(x3, 2, 3)
            all_emptied()
            pe.wait_ge(router_landed, 4 * 16)
            bk = vbank()
            for k in range(KT):
                last = mm(bk[0:36, 0:TOK], wr[:, k, :], hT[:, k, 0:TOK], start=(k == 0), stop=(k == KT - 1))
            last.then_inc(v_filled, 1)
            pe.wait_ge(v_freed, nv)
            bk = vbank()
            for t in range(3):
                n = P if t < 2 else NB
                last = nc.tensor.transpose(bk[0:n, 36 * t:36 * t + 36], LT[:, P * t:P * t + n], ident[0:36, 0:36])
            last.then_inc(v_filled, 1)
            pe.wait_ge(pairs_ready, 1)
            bk = vbank()
            pairs, before = rt[:, 0:96], rt[:, 96:224]
            mm(bk[:, 0:128], ones, before, start=True, stop=False)
            mm(bk[:, 0:96], tri[:], pairs, start=False, stop=True).then_inc(v_filled, 1)
            pe.wait_ge(over_cols_ready, 1)
            bk = vbank()
            mm(bk[:, 0:NE], ones[0:NE, :], rt[0:NE, 224:256], start=True, stop=True).then_inc(v_filled, 1)
            all_emptied()

            def expert(i):
                first = isinstance(i, int) and i == 0
                pe.wait_ge(xe_landed, 16 * (i + 1))
                if not first:
                    pe.wait_ge(xt_ready, i)
                for j in range(4):
                    last = nc.tensor.transpose(pb[0][:, P * j:P * j + P], xe[:, P * j:P * j + P], ident[:])
                last.then_inc(xt_filled, 1)
                pe.wait_ge(xt_ready, i + 1)
                if not first:
                    pe.wait_ge(hid_ready, i)
                for half in range(2):
                    pe.wait_ge(gu_landed[half], 32 * (i + 1))
                    w = ring[:, half, :].rearrange("p (m k n) -> p m k n", m=2, k=8)
                    block1 = isinstance(i, int) and i == 1 and half == 0
                    if block1:
                        pe.wait_ge(gu1_landed, 2 * 16)
                    for k8 in range(8):
                        k = 8 * half + k8
                        for c in range(4):
                            wk8 = (gu1 if block1 and k8 < 4 else w)[:, :, k8, P * c:P * c + P]
                            last = mm(pb[1][32 * c:32 * c + 32, 0:256], XT[:, k % 4, 32 * (k // 4):32 * (k // 4) + 32],
                                      wk8, start=(k == 0), stop=(k == KT - 1))
                    last.then_inc(gu_used[half], 1)
                pe.wait_ge(hid_ready, i + 1)
                if not first:
                    pe.wait_ge(hidT_ready, i)
                nc.tensor.transpose(pb[2][:, 0:P], hid, ident[:]).then_inc(hidT_filled, 1)
                pe.wait_ge(hidT_ready, i + 1)
                if not first:
                    pe.wait_ge(y_ready, i)
                w = [slot2[:, D * f:D * f + D] for f in range(4)]
                if first:
                    pe.wait_ge(dn_landed, 16)
                elif isinstance(i, int):
                    pe.wait_ge(dn1_landed, 2 * 16)
                    w = [down1[f // 2][:, f % 2] for f in range(4)]
                else:
                    pe.wait_ge(dn_landed, 16 * i)
                for f in range(4):
                    for c in range(4):
                        last = mm(pb[3][32 * c:32 * c + 32, :], aT[:, 32 * f:32 * f + 32], w[f][:, 512 * c:512 * c + 512],
                                  start=(f == 0), stop=(f == 3))
                last.then_inc(dn_used, 1)

            expert(0)
            expert(1)
            with pe.Fori(2, NE) as i:
                expert(i)
            n_over = pe.value_load(ov_i[0:1, OVB:OVB + 1], min_val=0, max_val=OVB)
            with pe.If(n_over > 0):
                with pe.Fori(NE, NBLK) as i:
                    expert(i)

        @block.scalar
        def _(act):
            na = nroot = nsq = 0

            def filled():
                nonlocal na
                na += 1
                act.wait_ge(a_filled, na)
                return AB[(na - 1) % 4]

            def freed(ins):
                ins.then_inc(a_freed, 1)

            def norm_squares(rows, tiles, dump, col, landed=()):
                nonlocal nroot, nsq
                for t in range(tiles):
                    if t:
                        act.wait_ge(squared, nsq)
                    if landed:
                        act.wait_ge(landed[t], 16)
                    nsq += 1
                    nc.scalar.activation(dump, rows[:, t, :], ACT.Square, accum_out=st[:, col + t:col + t + 1])\
                        .then_inc(squared, 1)
                roots(st[:, col + 3:col + 3 + tiles], st[:, col + 6:col + 6 + tiles])

            def roots(src, dst):
                nonlocal nroot
                nroot += 1
                act.wait_ge(mean_ready, nroot)
                nc.scalar.activation(dst, src, ACT.Sqrt).then_inc(root_ready, 1)

            def head_squares(rows, t, n, width, dump, heads):
                nonlocal nsq
                nsq += 1
                nc.scalar.activation(dump[0:n, 0:width], rows[0:n, t, 0:width], ACT.Square).then_inc(squared, 1)
                roots(st[0:n, 32:32 + heads], st[0:n, 64:64 + heads])

            def sample_rows(dst, bk, lo):
                for c in range(4):
                    last = nc.scalar.copy(dst[0:NB, 2, lo + P * c:lo + P * c + P], bk[32 * c:32 * c + NB, 0:P])
                freed(last)

            norm_squares(memr, 2, norm_dump, 12, mem_landed)
            act.wait_ge(x_landed, 32)
            act.wait_ge(squared, nsq)
            norm_squares(x3, 3, norm_dump, 0)
            freed(nc.scalar.copy(mk[:, 0, :], filled()[:, :]))
            act.wait_ge(a_freed, na)
            act.wait_ge(v_freed, V_MK)
            for t in range(2):
                if t:
                    act.wait_ge(mk_normed, t)
                head_squares(mk, t, P, XW, msq, XH)
            freed(nc.scalar.copy(mv[:, 0, :], filled()[:, :]))
            for pair in range(2):
                freed(nc.scalar.copy(mkT[:, 2 * pair:2 * pair + 2, :].rearrange("p j t -> p (j t)"), filled()[:, :]))
            for n in range(NCH):
                if n == 3:
                    act.wait_ge(a_freed, na)
                    act.wait_ge(v_freed, V_PRE + 3 + FLIPS)
                    for t in range(3):
                        if t:
                            act.wait_ge(qk_normed, t)
                        head_squares(z, t, P if t < 2 else NB, 2 * AW, sq, 2 * H)
                    act.wait_ge(mem_stored, 2 * 16)
                freed(nc.scalar.copy(z[:, 0, 512 * n:512 * n + 512], filled()[:, :]))
                sample_rows(z, filled(), 512 * n)
            act.wait_ge(qk_normed, 3)
            for s in range(2):
                for pair in range(0, H // 2, 2):
                    freed(nc.scalar.copy(qkT[:, s, pair:pair + 2, :].rearrange("p j t -> p (j t)"), filled()[:, :]))

            def sample_exps(base, width):
                for hf in range(2):
                    act.wait_ge(s_biased, 2 * base + hf + 1)
                    nc.scalar.activation(psm[:, hf, 0:width], psm[:, hf, 0:width], ACT.Exp, bias=st[:, 112 + hf:113 + hf],
                                         accum_out=st[:, 114 + hf:115 + hf]).then_inc(s_exped, 1)

            sample_exps(0, NDEC)
            heads_done = 0

            def attend(nh, parts, probs, turn, value):
                nonlocal heads_done
                for s in range(nh + 2):
                    if s < nh:
                        heads_done += 1
                        act.wait_ge(biased, heads_done)
                        q = 4 * (s % 2)
                        for j, (lo, hi) in enumerate(parts):
                            last = nc.scalar.activation(probs[:, s % 2, lo:hi], probs[:, s % 2, lo:hi], ACT.Exp,
                                                        bias=st[:, 96 + q + j:97 + q + j],
                                                        accum_out=st[:, 104 + q + j:105 + q + j])
                        last.then_inc(exped, 1)
                    if 1 <= s <= nh:
                        turn(s - 1)
                    if s >= 2:
                        value(s - 2)

            def value_win(h):
                r = slice(64 * (h % 2), 64 * (h % 2) + 64)
                freed(nc.scalar.copy(mixT[r, h // 2, 0:SEQ], filled()[r, 0:SEQ]))

            attend(H, ((0, P), (P, 3 * P)), prb, lambda h: freed(nc.scalar.copy(prT[:, h % 2, :], filled()[:, 0:384])),
                   value_win)

            def pool_channels(c):
                freed(nc.scalar.copy(poolT[:, c, :], filled()[:, 0:TOK]))

            def pool_map(kt):
                freed(nc.scalar.mul(mixT[:, 6 + kt, 0:TOK], filled()[:, 0:TOK], psc[:, kt:kt + 1]))

            def probs_back(tiles):
                for hf in range(2):
                    bk = filled()
                    for t, n in enumerate(tiles):
                        last = nc.scalar.copy(s_in[0:n, t, hf, :], bk[0:n, P * t:P * t + P])
                    freed(last)

            def sample_out(dst, kts, hf):
                bk = filled()
                freed(nc.scalar.copy(dst[:, 0:kts, SEQ + 4 * hf:SEQ + 4 * hf + 4],
                                     bk[:, 0:4 * kts].rearrange("p (k b) -> p k b", b=4)))

            probs_back(DEC_ROWS)
            for c in range(10):
                pool_channels(c)
            for kt in range(10):
                pool_map(kt)
                if kt == 1:
                    sample_out(mixT, H // 2, 0)
            sample_out(mixT, H // 2, 1)

            def chunk_squares(n, tiles):
                nonlocal nsq
                for t in tiles:
                    act.wait_ge(squared, nsq)
                    nsq += 1
                    nc.scalar.activation(chunk_dump, x3[:, t, 512 * n:512 * n + 512], ACT.Square,
                                         accum_out=st[:, 12 + 4 * t + n:13 + 4 * t + n]).then_inc(squared, 1)

            for n in range(4):
                act.wait_ge(v_freed, V_WOUT - 12 + 3 * (n + 1))
                chunk_squares(n, range(3))
            roots(st[:, 3:6], st[:, 6:9])
            freed(nc.scalar.copy(xq[:, 0, :], filled()[:, :]))
            sample_rows(xq, filled(), 0)
            act.wait_ge(a_freed, na)
            for done, t in enumerate((0, 2, 1)):
                if done:
                    act.wait_ge(xq_normed, done)
                if t == 1:
                    act.wait_ge(v_freed, V_CQ)
                head_squares(xq, t, P if t < 2 else NB, XW, xsq, XH)
            act.wait_ge(xq_normed, 3)
            for pair in range(2):
                freed(nc.scalar.copy(xqT[:, 2 * pair:2 * pair + 2, :].rearrange("p j t -> p (j t)"), filled()[:, :]))
            attend(XH, ((0, NM), (NM, 2 * NM)), xprb, lambda h: freed(nc.scalar.copy(xprT[:, h % 2, :], filled()[:, :])),
                   lambda h: freed(nc.scalar.copy(oT[:, h, 0:SEQ], filled()[:, 0:SEQ])))
            for n in range(4):
                act.wait_ge(v_freed, V_XP + 4 * n + 3)
                chunk_squares(n, range(2))
            sample_exps(1, NM)
            roots(st[:, 3:5], st[:, 6:8])
            probs_back((P, P))
            for hf in range(2):
                sample_out(oT, XH, hf)
            for n in range(4):
                act.wait_ge(v_freed, V_XR + n + 1)
                chunk_squares(n, range(2, 3))
            roots(st[:, 5:6], st[:, 8:9])
            assert nsq == N_SQUARED
            act.wait_ge(exp_in, 1)
            nc.scalar.activation(rt[:, 1300:1312], rt[:, 1300:1312], ACT.Exp).then_inc(exp_out, 1)
            act.wait_ge(exp_in, 2)
            nc.scalar.activation(rt[:, 1312:1315], rt[:, 1312:1315], ACT.Exp).then_inc(exp_out, 1)

            def expert(i):
                first = isinstance(i, int)
                act.wait_ge(gu_used[1], i + 1)
                nc.scalar.activation(ge, pb[1][:, 0:P], ACT.Exp, scale=-1.0).then_inc(gate_exp, 1)
                act.wait_ge(hidT_filled, i + 1)
                nc.scalar.copy(aT, pb[2][:, 0:P]).then_inc(hidT_ready, 1)
                act.wait_ge(dn_used, i + 1)
                if not first:
                    act.wait_ge(y_stored, 64 * i)
                nc.scalar.copy(yo, pb[3][:, :]).then_inc(y_ready, 1)
                act.wait_ge(y_ready, i + 1)
                rows = ys_dram[0:BLK] if first else ys_dram[bass.ds(i * BLK, BLK)]
                for c in range(4):
                    act.dma_start(rows[:, 512 * c:512 * c + 512], yo[32 * c:32 * c + 32, :]).then_inc(y_stored, 16)

            expert(0)
            with act.Fori(1, NE) as i:
                expert(i)
            n_over = act.value_load(ov_i[0:1, OVB:OVB + 1], min_val=0, max_val=OVB)
            with act.If(n_over > 0):
                with act.Fori(NE, NBLK) as i:
                    expert(i)

        @block.vector
        def _(dve):
            nv = nseq = nroot = nsq = 0
            V = nc.vector

            def filled():
                nonlocal nv
                nv += 1
                dve.wait_ge(v_filled, nv)
                return VB[(nv - 1) % 4]

            def link(ins):
                nonlocal nseq
                nseq += 1
                ins.then_inc(dve_seq, 1)
                dve.wait_ge(dve_seq, nseq)

            def mean_root(sums, mean, root, inv, n):
                nonlocal nroot
                V.tensor_scalar(mean, sums, 1.0 / n, EPS, ALU.mult, ALU.add).then_inc(mean_ready, 1)
                nroot += 1
                dve.wait_ge(root_ready, nroot)
                link(V.reciprocal(inv, root))

            def norm_scales(first, end, col=0, chunks=1):
                nonlocal nsq
                nsq += (end - first) * chunks
                dve.wait_ge(squared, nsq)
                if chunks > 1:
                    link(V.tensor_reduce(st[:, first:end], st[:, 12 + 4 * first:12 + 4 * end].rearrange("p (t n) -> p t n", n=4),
                                         AX.X, ALU.add))
                mean_root(*(st[:, col + c + first:col + c + end] for c in (0, 3, 6, 9)), D)
                for t in range(first, end):
                    last = V.tensor_scalar(dg[:, t, :], ident[:], st[:, col + 9 + t:col + 10 + t], None, ALU.mult)
                last.then_inc(diag_ready, 1)

            def norm_rows(first, end, gain, dst, parts=range(4)):
                for t in range(first, end):
                    for j in parts:
                        n = P if t < 2 else 32
                        src = filled()[:, :].rearrange("p (k m) -> p k m", k=4)[:, :, 0:n]
                        V.tensor_tensor(dst[:, 4 * j:4 * j + 4, P * t:P * t + n], src,
                                        gT[:, gain, 4 * j:4 * j + 4].unsqueeze(2).to_broadcast([P, 4, n]), ALU.mult)\
                            .then_inc(v_freed, 1)

            def head_norm(rows, t, n, heads, width, squares, gain, done):
                nonlocal nsq
                nsq += 1
                dve.wait_ge(squared, nsq)
                sm, mean, root, inv = (st[0:n, c:c + heads] for c in (128, 32, 64, 128))
                link(V.tensor_reduce(sm, squares[0:n, 0:heads * width].rearrange("p (h e) -> p h e", h=heads), AX.X, ALU.add))
                mean_root(sm, mean, root, inv, width)
                r3 = rows[0:n, t, 0:heads * width].rearrange("p (h e) -> p h e", h=heads)
                link(V.tensor_tensor(r3, r3, inv.unsqueeze(2).to_broadcast([n, heads, width]), ALU.mult))
                gs = [gain[0:n, g, :].unsqueeze(1) for g in (range(2) if heads == 2 * H else done[1])]
                per = heads // len(gs)
                for i, g in enumerate(gs):
                    part = r3[:, i * per:(i + 1) * per, :]
                    last = V.tensor_tensor(part, part, g.to_broadcast([n, per, width]), ALU.mult)
                last.then_inc(done[0], 1)

            def sample_scores(buf, b, tiles, widths, heads_of, width):
                hf, i = b // 4, b % 4
                rows = buf[b % len(buf)]
                for (lo, n) in widths:
                    src = rows[:, :, lo:lo + n]
                    V.tensor_tensor(src, src, filled()[:, 0:n].unsqueeze(1).to_broadcast([P, tiles, n]), ALU.mult)\
                        .then_inc(v_freed, 1)
                dve.wait_ge(v_freed, nv)
                V.tensor_reduce(s_in[:, 0:tiles, hf, 32 * i:32 * i + heads_of],
                                rows.rearrange("p t (h e) -> p t h e", e=width), AX.X, ALU.add).then_inc(keys_used, 1)

            def sample_softmax(base, width, scale, rows):
                for hf in range(2):
                    bk = filled()
                    if rows is not None:
                        V.scalar_tensor_tensor(out=psm[:, hf, 0:width], in0=bk[:, 0:width], scalar=scale, in1=rows,
                                               op0=ALU.mult, op1=ALU.add).then_inc(v_freed, 1)
                    else:
                        V.tensor_scalar(psm[:, hf, 0:width], bk[:, 0:width], scale, None, ALU.mult).then_inc(v_freed, 1)
                    dve.wait_ge(v_freed, nv)
                    link(V.tensor_reduce(st[:, 120:121], psm[:, hf, 0:width], AX.X, ALU.max))
                    V.tensor_scalar(st[:, 112 + hf:113 + hf], st[:, 120:121], -1.0, None, ALU.mult).then_inc(s_biased, 1)

            def sample_probs(base, width):
                for hf in range(2):
                    dve.wait_ge(s_exped, 2 * base + hf + 1)
                    link(V.reciprocal(st[:, 122 + hf:123 + hf], st[:, 114 + hf:115 + hf]))
                    V.tensor_scalar(psm[:, hf, 0:width], psm[:, hf, 0:width], st[:, 122 + hf:123 + hf], None, ALU.mult)\
                        .then_inc(s_probs, 1)

            V.memset(rbs[0:32].rearrange("p i h -> p (i h)"), 0.0).then_inc(zeros_ready, 1)
            V.memset(x3[:, 2, :], 0.0).then_inc(zeros_ready, 1)
            V.memset(zero_i[:], 0)
            V.memset(z[:, 2, 0:AW], 0.0)
            V.memset(s_in[:].rearrange("p a b c -> p (a b c)"), 0.0)
            V.memset(rb[32:33], 1.0)
            link(V.memset(rbs[32:33].rearrange("p i h -> p (i h)"), 1.0))
            dve.nop().then_inc(zeros_ready, 1)
            dve.wait_ge(const_landed, 16 * N_CONST)
            V.tensor_copy(brow[0:H, :], filled()[0:H, 0:384]).then_inc(v_freed, 1)
            V.tensor_copy(biasS, filled()[:, 0:NDEC]).then_inc(v_freed, 1)
            V.tensor_copy(quarters[:].rearrange("p t c -> p (t c)"), moec[:, 2 * NE + 3 + OVB:])
            norm_scales(0, 2, 12)
            norm_rows(0, 2, 1, hmT)
            norm_scales(0, 3)
            V.tensor_copy(mk[:, 1, :], filled()[:, :]).then_inc(v_freed, 1)
            assert nv == V_MK
            dve.wait_ge(v_freed, nv)
            for t in range(2):
                head_norm(mk, t, P, XH, XD, msq, gxx, (mk_normed, (1,)))
            V.tensor_copy(mv[:, 1, :], filled()[:, :]).then_inc(v_freed, 1)
            dve.wait_ge(v_freed, nv)
            dve.wait_ge(a_freed, 2)
            dve.nop().then_inc(mk_normed, 1)
            norm_rows(0, 3, 0, hT)
            assert nv == V_PRE
            piece_used(dve, CV)
            V.memset(kbuf[0][96:P, 1:3], 0.0)
            V.memset(kbuf[1][96:P, 1:3], 0.0).then_inc(pads_ready, 1)
            for i in range(NCH):
                queries = iter(QUERIES.get(i, ()))

                def next_scores():
                    for b in queries:
                        key_ready(dve, b)
                        sample_scores(kbuf, b, 3, ((0, 512), (512, 256)), H, HD)
                        break

                next_scores()
                next_scores()
                V.tensor_copy(z[:, 1, 512 * i:512 * i + 512], filled()[:, :]).then_inc(v_freed, 1)
                next_scores()
                for n in range(FLIPS if i == 1 else 0):
                    V.tensor_copy(bias_flat[:, 512 * n:512 * n + 512], filled()[:, :]).then_inc(v_freed, 1)
                if i == 2:
                    dve.wait_ge(v_freed, nv)
                    dve.wait_ge(a_freed, A_MEM + 2 * 3)
                    for t in range(3):
                        head_norm(z, t, P if t < 2 else NB, 2 * H, HD, sq, gqk, (qk_normed, None))
            assert nv == V_IN
            dve.wait_ge(keys_used, NB)
            V.memset(mixT[:, :, TOK:TC], 0.0)
            sample_softmax(0, NDEC, HD ** -0.5, biasS)
            sample_probs(0, NDEC)

            heads_done = 0

            def attend(nh, parts, probs, enter, a_before):
                nonlocal heads_done
                for s in range(nh + 1):
                    if s < nh:
                        bk = filled()
                        if s >= 2:
                            dve.wait_ge(a_filled, a_before + turn_job(s - 2) + 1)
                        enter(s, bk)
                        dve.wait_ge(v_freed, nv)
                        q = 4 * (s % 2)
                        for j, (lo, hi) in enumerate(parts):
                            last = V.tensor_reduce(st[:, 116 + j:117 + j], probs[:, s % 2, lo:hi], AX.X, ALU.max)
                        link(last)
                        V.tensor_scalar(st[:, 96 + q:98 + q], st[:, 116:118], -1.0, None, ALU.mult).then_inc(biased, 1)
                    if s >= 1:
                        h = s - 1
                        heads_done += 1
                        dve.wait_ge(exped, heads_done)
                        q = 4 * (h % 2)
                        if heads_done > 1:
                            dve.wait_ge(probs_ready, heads_done - 1)
                        link(V.reciprocal(st[:, 118:120], st[:, 104 + q:106 + q]))
                        for j, (lo, hi) in enumerate(parts):
                            last = V.tensor_scalar(probs[:, h % 2, lo:hi], probs[:, h % 2, lo:hi], st[:, 118 + j:119 + j],
                                                   None, ALU.mult)
                        last.then_inc(probs_ready, 1)

            def enter_win(h, bk):
                V.scalar_tensor_tensor(out=prb[:, h % 2, 0:P], in0=bk[:, 0:P], scalar=HD ** -0.5, in1=bias[:, h, P:SEQ],
                                       op0=ALU.mult, op1=ALU.add)
                V.scalar_tensor_tensor(out=prb[:, h % 2, P:3 * P], in0=bk[:, P:3 * P], scalar=HD ** -0.5, in1=bias[:, h, :],
                                       op0=ALU.mult, op1=ALU.add).then_inc(v_freed, 1)

            dve.wait_ge(keys_stored, 2 * 16)
            dve.wait_ge(a_freed, A_QKT)
            attend(H, ((0, P), (P, 3 * P)), prb, enter_win, A_QKT)

            def sample_mask(hf, widths, out, m, a_before):
                if hf:
                    dve.wait_ge(a_freed, a_before + 1)
                for lo, n in widths:
                    V.tensor_tensor(out[:, lo:lo + n], filled()[:, 0:n], m[:, lo:lo + n], ALU.mult).then_inc(v_freed, 1)

            dve.wait_ge(mask_landed, 16)
            for hf in range(2):
                sample_mask(hf, ((0, 512), (512, 256)), masked, mask, A_SEL - 1)

            def add_prompt(n, t):
                c = slice(512 * n, 512 * n + 512)
                V.tensor_tensor(x3[:, t, c], filled()[:, :], x3[:, t, c], ALU.add).then_inc(v_freed, 1)

            def add_sample(n):
                bk = filled()
                for j in range(4):
                    d = x3[0:NB, 2, 512 * n + P * j:512 * n + P * j + P]
                    last = V.tensor_tensor(d, bk[32 * j:32 * j + NB, 0:P], d, ALU.add)
                last.then_inc(v_freed, 1)

            for n in range(4):
                add_prompt(n, 0)
                add_prompt(n, 1)
                add_sample(n)
            dve.wait_ge(v_freed, nv)
            assert nv == V_WOUT
            V.memset(oT[:, :, TOK:TC], 0.0)
            norm_scales(0, 3, chunks=4)
            norm_rows(0, 3, 2, hT)
            for t in (0, 2, 1):
                if t == 1:
                    V.tensor_copy(xq[:, 1, :], filled()[:, :]).then_inc(v_freed, 1)
                    assert nv == V_CQ
                    dve.wait_ge(v_freed, nv)
                head_norm(xq, t, P if t < 2 else NB, XH, XD, xsq, gxx, (xq_normed, (0,)))
            attend(XH, ((0, NM), (NM, 2 * NM)), xprb,
                   lambda h, bk: V.tensor_scalar(xprb[:, h % 2, :], bk[:, :], XD ** -0.5, None, ALU.mult).then_inc(v_freed, 1),
                   A_XQT)
            for n in range(4):
                for t in range(2):
                    add_prompt(n, t)
                    xkv_ready(dve, 2 * n + t)
                    sample_scores(xkv, 2 * n + t, 2, ((0, XW),), XH, XD)
            sample_softmax(1, NM, XD ** -0.5, None)
            norm_scales(0, 2, chunks=4)
            sample_probs(1, NM)
            norm_rows(0, 1, 3, hT)

            def expert_rows(t):
                V.tensor_scalar(xn[:, t, :].rearrange("p (k m) -> p k m", k=KT), x3[:, t, :].rearrange("p (m k) -> p k m", k=KT),
                                st[:, 9 + t:10 + t], None, ALU.mult).then_inc(xn_ready, 1)

            dve.wait_ge(mask_landed, 32)
            for hf in range(2):
                sample_mask(hf, ((0, XW),), xmasked, xmask, A_XQT + 2 * XH + 2)
                norm_rows(1, 2, 3, hT, (0, 1) if hf == 0 else (2, 3))
            assert nv == V_XR
            expert_rows(0)
            dve.wait_ge(vals_used, 2 * NB)
            expert_rows(1)
            for n in range(4):
                add_sample(n)
            dve.wait_ge(v_freed, nv)
            assert nv == V_CO
            norm_scales(2, 3, chunks=4)
            norm_rows(2, 3, 3, hT)
            V.memset(ones, 1.0)
            expert_rows(2)
            dve.wait_ge(router_landed, 4 * 16)
            V.tensor_scalar(LT, filled()[0:36, 0:TOK], b36, None, ALU.add).then_inc(v_freed, 1)
            R = lambda lo, n: rt[:, lo:lo + 3 * n].rearrange("p (t n) -> p t n", t=3)
            L36 = R(260, 36)
            pen, le, eq, c1, oh1, oh2 = R(370, 4), R(384, NE), R(480, NE), R(576, NE), R(672, NE), R(768, NE)
            lg2, ohg, m1, m2, cm = R(1300, 4), R(864, 4), R(880, 1), R(884, 1), R(888, 1)
            gmax, gsum, pgrp = R(892, 1), R(896, 1), R(900, 1)
            slotE, cnt, xo, xinc, tmp, cmp = R(904, NE), rt[:, 1000:1032], rt[:, 1032:1064], rt[:, 1064:1096], R(1100, NE), rt[:, 1200:1232]
            desc = moec[:, 0:NE].unsqueeze(1).to_broadcast([P, 3, NE])
            base = moec[:, NE:2 * NE].unsqueeze(1).to_broadcast([P, 3, NE])
            valid = moec[:, 2 * NE:2 * NE + 3].unsqueeze(2).to_broadcast([P, 3, NE])
            TT = V.tensor_tensor

            def b(x, n):
                return x.to_broadcast([P, 3, n])

            link(V.memset(L36, 0.0))
            bk = filled()
            V.tensor_copy(L36[:, 0:2, :], bk[:, 0:72].rearrange("p (t n) -> p t n", t=2))
            link(V.tensor_copy(L36[0:NB, 2, :], bk[0:NB, 72:108]))
            dve.nop().then_inc(v_freed, 1)
            lg = L36[:, :, 0:NG]
            link(V.tensor_reduce(gmax, lg, AX.X, ALU.max))
            TT(lg2, lg, b(gmax, NG), ALU.subtract).then_inc(exp_in, 1)
            link(TT(ohg, lg, b(gmax, NG), ALU.is_equal))
            link(TT(ohg, ohg, moec[:, NE - NG:NE].unsqueeze(1).to_broadcast([P, 3, NG]), ALU.mult))
            link(V.tensor_reduce(cm, ohg, AX.X, ALU.max))
            link(TT(ohg, ohg, b(cm, NG), ALU.is_equal))
            link(V.tensor_scalar(pen, ohg, -NEG, NEG, ALU.mult, ALU.add))
            for t in range(3):
                last = TT(le[:, t, :].rearrange("p (g e) -> p g e", g=NG), L36[:, t, NG:36].rearrange("p (g e) -> p g e", g=NG),
                          pen[:, t, :].unsqueeze(2).to_broadcast([P, NG, EG]), ALU.add)
            link(last)

            def top(oh, m):
                link(V.tensor_reduce(m, le, AX.X, ALU.max))
                link(TT(eq, le, b(m, NE), ALU.is_equal))
                link(TT(c1, eq, desc, ALU.mult))
                link(V.tensor_reduce(cm, c1, AX.X, ALU.max))
                link(TT(oh, c1, b(cm, NE), ALU.is_equal))

            top(oh1, m1)
            link(V.scalar_tensor_tensor(out=le, in0=oh1, scalar=3 * NEG, in1=le, op0=ALU.mult, op1=ALU.add))
            top(oh2, m2)
            dve.wait_ge(exp_out, 1)
            link(V.tensor_reduce(gsum, lg2, AX.X, ALU.add))
            e2 = R(1312, 1)
            TT(e2, m2, m1, ALU.subtract).then_inc(exp_in, 1)
            pairs = R(0, NE)
            link(TT(c1, oh1, oh2, ALU.add))
            link(TT(pairs, c1, valid, ALU.mult))
            before = rt[:, 96:224]
            V.memset(before[:, 0:NE], 0.0)
            link(V.tensor_copy(before[:, NE:2 * NE], pairs[:, 0, :]))
            link(TT(before[:, 2 * NE:3 * NE], before[:, NE:2 * NE], pairs[:, 1, :], ALU.add))
            TT(before[:, 3 * NE:4 * NE], before[:, 2 * NE:3 * NE], pairs[:, 2, :], ALU.add).then_inc(pairs_ready, 1)
            dve.wait_ge(exp_out, 2)
            link(V.reciprocal(pgrp, gsum))
            link(V.tensor_scalar(m1, e2, 1.0, None, ALU.add))
            link(V.reciprocal(m2, m1))
            link(TT(gates[:, 0, :].unsqueeze(2), m2, pgrp, ALU.mult))
            link(TT(gates[:, 1, :].unsqueeze(2), gates[:, 0, :].unsqueeze(2), e2, ALU.mult))
            pos = filled()
            link(V.tensor_copy(cnt, pos[:, 96:128]))
            link(V.tensor_scalar(xo, cnt, float(BLK), None, ALU.is_gt))
            for j in range(2, -(-TOK // BLK)):
                link(V.scalar_tensor_tensor(out=xo, in0=cnt, scalar=float(BLK * j), in1=xo, op0=ALU.is_gt, op1=ALU.add))
            link(TT(tmp[0:NE, 0, :], xo[0:NE, :], ident[0:NE, 0:NE], ALU.mult))
            link(V.tensor_reduce(cm[0:NE, 0, :], tmp[0:NE, 0, :], AX.X, ALU.add))
            V.tensor_scalar(rt[0:NE, 224:256], tri[0:NE, 0:NE], cm[0:NE, 0, :], None, ALU.mult).then_inc(over_cols_ready, 1)
            xb = filled()
            link(V.tensor_scalar(cmp, xb[:, 0:NE], float(BLK), float(NE * BLK - BLK), ALU.mult, ALU.add))
            link(TT(cmp, cmp, moec[:, NE:2 * NE], ALU.subtract))
            p3 = pos[:, 0:96].rearrange("p (t n) -> p t n", t=3)
            link(V.tensor_scalar(tmp, p3, float(BLK), None, ALU.is_ge))
            link(TT(tmp, tmp, cmp.unsqueeze(1).to_broadcast([P, 3, NE]), ALU.mult))
            link(TT(tmp, tmp, base, ALU.add))
            link(TT(slotE, p3, tmp, ALU.add))
            for s, oh in enumerate((oh1, oh2)):
                link(TT(c1, oh, slotE, ALU.mult))
                link(V.tensor_reduce(cm, c1, AX.X, ALU.add))
                link(V.tensor_copy(slot_i[:, s, :], cm[:, :, 0]))
            link(TT(xinc, xb[:, 0:NE], xo, ALU.add))
            o3 = rt[0:1, 300:300 + OVB * NE].rearrange("p (o e) -> p o e", o=OVB)
            link(TT(o3, moec[0:1, 2 * NE + 3:2 * NE + 3 + OVB].unsqueeze(2).to_broadcast([1, OVB, NE]),
                    xinc[0:1, :].unsqueeze(1).to_broadcast([1, OVB, NE]), ALU.is_ge))
            link(V.tensor_reduce(rt[0:1, 1400:1400 + OVB], o3, AX.X, ALU.add))
            link(V.tensor_scalar(rt[0:1, 1400:1400 + OVB], rt[0:1, 1400:1400 + OVB], float(NE - 1), None, ALU.min))
            V.tensor_copy(ov_i[0:1, 0:OVB], rt[0:1, 1400:1400 + OVB])
            link(V.tensor_copy(ov_i[0:1, OVB:OVB + 1], xinc[0:1, NE - 1:NE]))
            dve.nop().then_inc(v_freed, 2)
            dve.nop().then_inc(slots_ready, 1)

            def expert(i):
                first = isinstance(i, int)
                dve.wait_ge(xt_filled, i + 1)
                if not first:
                    dve.wait_ge(gu_used[1], i)
                V.tensor_tensor(XT.rearrange("p j (c s) -> p j c s", c=4), pb[0][:, :].rearrange("p (j c s) -> p j c s", j=4, c=4),
                                gT[:, 3, :].rearrange("p (c j) -> p j c", j=4).unsqueeze(3).to_broadcast([P, 4, 4, 32]),
                                ALU.mult).then_inc(xt_ready, 1)
                dve.wait_ge(gate_exp, i + 1)
                V.tensor_scalar(gd, ge, 1.0, None, ALU.add).then_inc(hid_seq, 1)
                dve.wait_ge(hid_seq, 3 * i + 1)
                V.reciprocal(gr, gd).then_inc(hid_seq, 1)
                dve.wait_ge(hid_seq, 3 * i + 2)
                V.tensor_tensor(gd, pb[1][:, 0:P], gr, ALU.mult).then_inc(hid_seq, 1)
                dve.wait_ge(hid_seq, 3 * i + 3)
                V.tensor_tensor(hid, pb[1][:, P:2 * P], gd, ALU.mult).then_inc(hid_ready, 1)

            expert(0)
            with dve.Fori(1, NE) as i:
                expert(i)
            n_over = dve.value_load(ov_i[0:1, OVB:OVB + 1], min_val=0, max_val=OVB)
            with dve.If(n_over > 0):
                with dve.Fori(NE, NBLK) as i:
                    expert(i)
            for t in range(3):
                n = P if t < 2 else NB
                for s in range(2):
                    j = 2 * t + s
                    dve.wait_ge(y_gathered[j], 16)
                    ins = V.scalar_tensor_tensor(out=x3[0:n, t, :], in0=ring[0:n, j // 4, (j % 4) * D:(j % 4 + 1) * D],
                                                 scalar=gates[0:n, s, t:t + 1], in1=x3[0:n, t, :], op0=ALU.mult, op1=ALU.add)
                    if s == 0:
                        link(ins)
                    else:
                        ins.then_inc(x_final, 1)


_INS = ['x_prompt', 'x_sample', 'cache_win_k', 'cache_win_v', 'state_pool', 'cache_mem_k', 'cache_mem_v', 'mem_prompt',
        'rel_bias', 'norm_mix_g', 'w_in', 'q_norm_g', 'k_norm_g', 'pool_w', 'pool_scale', 'w_out', 'norm_cross_g',
        'norm_mem_g', 'w_cq', 'w_ck', 'w_cv', 'cq_norm_g', 'ck_norm_g', 'w_co', 'norm_ffn_g', 'w_rg', 'b_rg', 'w_re',
        'b_re', 'w_e_gate', 'w_e_up', 'w_e_down']
_OUTS = [('y_prompt', (1, SEQ, D)), ('y_sample', (NB, 1, D)),
         ('win_k_prompt', (1, 1, SEQ, H, HD)), ('win_v_prompt', (1, 1, SEQ, H, HD)),
         ('win_k_sample', (1, NB, WB, H, HD)), ('win_v_sample', (1, NB, WB, H, HD)),
         ('pool_prompt', (1, 1, HIST, PW)), ('pool_sample', (1, NB, HIST, PW)),
         ('mem_k_prompt', (1, 1, NM, XH, XD)), ('mem_v_prompt', (1, 1, NM, XH, XD))]


def kernel(**inputs):
    import concourse.bacc as _bacc
    from concourse.bass_utils import run_bass_kernel_spmd as _run

    nc = _bacc.Bacc("TRN2", target_bir_lowering=False, num_devices=1)
    arrays, args = {}, {}
    for name in _INS + ["const"]:
        arr = constants() if name == "const" else np.ascontiguousarray(inputs[name])
        arrays[f"in_{name}_dram"] = arr
        args[name] = nc.dram_tensor(f"in_{name}_dram", arr.shape, mybir.dt.from_np(arr.dtype), kind="ExternalInput").ap()
    for name, shape in _OUTS:
        args[name] = nc.dram_tensor(f"out_{name}_dram", shape, F32, kind="ExternalOutput").ap()
    hybrid_decoder_layer(nc, args)
    r = _run(nc, [arrays], core_ids=[0])
    return tuple(r.results[0][f"out_{name}_dram"] for name, _ in _OUTS)
```
